# Optimizing a Trainium2 kernel written in Bass

```python
import jax, jax.numpy as jnp
from jax import lax
import numpy as np

D_MODEL = 1024
BATCH = 1
SEQ = 256
DEPTH = 2

N_A_LAYERS = DEPTH // 2
N_B_LAYERS = DEPTH - N_A_LAYERS
PLE_DIM = 256
NORM_EPS = 1e-6

GDN_HEADS = 8
GDN_HEAD_DIM = 128
GDN_KEY_DIM = GDN_HEADS * GDN_HEAD_DIM
GDN_VALUE_DIM = GDN_HEADS * GDN_HEAD_DIM
GDN_CONV = 4
GDN_CHUNK = 64
GDN_QKV_DIM = 2 * GDN_KEY_DIM + GDN_VALUE_DIM
GDN_IN_DIM = GDN_QKV_DIM + GDN_VALUE_DIM + 2 * GDN_HEADS

SB_Q_HEADS = 16
SB_KV_HEADS = 4
SB_GROUP = SB_Q_HEADS // SB_KV_HEADS
SB_HEAD_DIM = 64
SB_BLOCK = 128

MOE_GROUPS = 4
MOE_EXPERTS_PER_GROUP = 8
MOE_N_EXPERTS = MOE_GROUPS * MOE_EXPERTS_PER_GROUP
MOE_TOP_K = 2
MOE_D_EXPERT = 256

kernel_name = "yoco_gdn_stickbreak_hmoe"

def rms_norm(x, gain):
    xf = x.astype(jnp.float32)
    y = xf * lax.rsqrt(jnp.mean(xf * xf, axis=-1, keepdims=True) + NORM_EPS) * gain.astype(jnp.float32)
    return y.astype(x.dtype)

def l2_normalize(t):
    return t * lax.rsqrt(jnp.sum(t * t, axis=-1, keepdims=True) + NORM_EPS)

def causal_depthwise_conv(x, w):
    c = x.shape[-1]
    return lax.conv_general_dilated(
        x, w[:, None, :].astype(x.dtype), window_strides=(1,), padding=[(GDN_CONV - 1, 0)],
        dimension_numbers=("NWC", "WIO", "NWC"), feature_group_count=c)

def chunk_gated_delta_rule(q, k, v, g, beta):
    b_, s_, h_, dk = q.shape
    dv = v.shape[-1]
    c = GDN_CHUNK
    n = s_ // c

    def to_chunks(t):
        return t.reshape(b_, n, c, h_, t.shape[-1]).transpose(0, 3, 1, 2, 4)

    q, k, v = to_chunks(q), to_chunks(k), to_chunks(v)
    g = jnp.cumsum(g.reshape(b_, n, c, h_).transpose(0, 3, 1, 2), axis=-1)
    beta = beta.reshape(b_, n, c, h_).transpose(0, 3, 1, 2)
    k_beta = k * beta[..., None]
    v_beta = v * beta[..., None]

    incl = jnp.tril(jnp.ones((c, c), dtype=bool))
    strict = jnp.tril(jnp.ones((c, c), dtype=bool), -1)
    diff = g[..., :, None] - g[..., None, :]
    decay = jnp.where(incl, jnp.exp(jnp.where(incl, diff, 0.0)), 0.0)

    lmat = jnp.where(strict, jnp.einsum("bhncd,bhnsd->bhncs", k_beta, k) * decay, 0.0)
    eye = jnp.broadcast_to(jnp.eye(c, dtype=jnp.float32), lmat.shape)
    tmat = lax.linalg.triangular_solve(eye + lmat, eye, left_side=True, lower=True, unit_diagonal=True)
    u = jnp.einsum("bhncs,bhnse->bhnce", tmat, v_beta)
    w = jnp.einsum("bhncs,bhnsd->bhncd", tmat, k_beta * jnp.exp(g)[..., None])
    attn_qk = jnp.where(incl, jnp.einsum("bhncd,bhnsd->bhncs", q, k) * decay, 0.0)

    def step(state, xs):
        q_i, k_i, u_i, w_i, g_i, a_i = xs
        v_new = u_i - jnp.einsum("bhcd,bhde->bhce", w_i, state)
        o_i = (jnp.einsum("bhcd,bhde->bhce", q_i * jnp.exp(g_i)[..., None], state)
               + jnp.einsum("bhcs,bhse->bhce", a_i, v_new))
        g_last = g_i[..., -1]
        k_dec = k_i * jnp.exp(g_last[..., None] - g_i)[..., None]
        state = state * jnp.exp(g_last)[..., None, None] + jnp.einsum("bhcd,bhce->bhde", k_dec, v_new)
        return state, o_i

    xs = tuple(jnp.moveaxis(t, 2, 0) for t in (q, k, u, w, g, attn_qk))
    state0 = jnp.zeros((b_, h_, dk, dv), jnp.float32)
    _, o = lax.scan(step, state0, xs)
    return o.transpose(1, 0, 3, 2, 4).reshape(b_, s_, h_, dv)

def gated_deltanet(xn, w_in, conv_w, a_log, dt_bias, o_norm, w_out):
    b_, s_, _ = xn.shape
    proj = xn @ w_in
    qkv = jax.nn.silu(causal_depthwise_conv(proj[..., :GDN_QKV_DIM], conv_w)).astype(jnp.float32)
    z = proj[..., GDN_QKV_DIM:GDN_QKV_DIM + GDN_VALUE_DIM]
    a = proj[..., GDN_QKV_DIM + GDN_VALUE_DIM:GDN_QKV_DIM + GDN_VALUE_DIM + GDN_HEADS].astype(jnp.float32)
    bb = proj[..., GDN_QKV_DIM + GDN_VALUE_DIM + GDN_HEADS:].astype(jnp.float32)
    q = qkv[..., :GDN_KEY_DIM].reshape(b_, s_, GDN_HEADS, GDN_HEAD_DIM)
    k = qkv[..., GDN_KEY_DIM:2 * GDN_KEY_DIM].reshape(b_, s_, GDN_HEADS, GDN_HEAD_DIM)
    v = qkv[..., 2 * GDN_KEY_DIM:].reshape(b_, s_, GDN_HEADS, GDN_HEAD_DIM)
    q = l2_normalize(q) * (GDN_HEAD_DIM ** -0.5)
    k = l2_normalize(k)
    beta = jax.nn.sigmoid(bb)
    g = -jnp.exp(a_log.astype(jnp.float32)) * jax.nn.softplus(a + dt_bias.astype(jnp.float32))
    o = chunk_gated_delta_rule(q, k, v, g, beta)
    o = o * lax.rsqrt(jnp.mean(o * o, axis=-1, keepdims=True) + NORM_EPS) * o_norm.astype(jnp.float32)
    o = o * jax.nn.silu(z.astype(jnp.float32)).reshape(b_, s_, GDN_HEADS, GDN_HEAD_DIM)
    return o.reshape(b_, s_, GDN_VALUE_DIM).astype(xn.dtype) @ w_out

def stick_breaking_attention(q, k, v):
    s_ = q.shape[1]
    scale = SB_HEAD_DIM ** -0.5
    outs = []
    for i in range(s_ // SB_BLOCK):
        end = (i + 1) * SB_BLOCK
        q_blk = q[:, i * SB_BLOCK:end].astype(jnp.float32)
        k_pre = k[:, :end].astype(jnp.float32)
        v_pre = v[:, :end].astype(jnp.float32)
        z = jnp.einsum("bqhgd,bkhd->bhgqk", q_blk, k_pre) * scale
        t_pos = i * SB_BLOCK + jnp.arange(SB_BLOCK)
        s_pos = jnp.arange(end)
        mask = s_pos[None, :] < t_pos[:, None]
        log1m = jnp.where(mask, jax.nn.log_sigmoid(-z), 0.0)
        rev = lax.cumsum(log1m, axis=log1m.ndim - 1, reverse=True)
        rev_excl = jnp.concatenate([rev[..., 1:], jnp.zeros_like(rev[..., :1])], axis=-1)
        attn = jnp.where(mask, jnp.exp(jax.nn.log_sigmoid(z) + rev_excl), 0.0)
        outs.append(jnp.einsum("bhgqk,bkhd->bqhgd", attn, v_pre))
    return jnp.concatenate(outs, axis=1)

def stick_breaking_mixer(xn, k, v, w_q, w_out):
    b_, s_, _ = xn.shape
    q = (xn @ w_q).reshape(b_, s_, SB_KV_HEADS, SB_GROUP, SB_HEAD_DIM)
    o = stick_breaking_attention(q, k, v)
    return o.reshape(b_, s_, SB_Q_HEADS * SB_HEAD_DIM).astype(xn.dtype) @ w_out

def hierarchical_moe(xn, w_group, b_group, w_expert, b_expert, w_gate, w_up, w_down):
    b_, s_, d_ = xn.shape
    xf = xn.reshape(b_ * s_, d_)
    t_ = xf.shape[0]
    gprob = jax.nn.softmax((xf @ w_group + b_group).astype(jnp.float32), axis=-1)
    gp, gidx = lax.top_k(gprob, 1)
    elog = (xf @ w_expert + b_expert).astype(jnp.float32).reshape(t_, MOE_GROUPS, MOE_EXPERTS_PER_GROUP)
    elog_sel = jnp.take_along_axis(elog, gidx[:, :, None], axis=1)[:, 0]
    ev, eidx = lax.top_k(elog_sel, MOE_TOP_K)
    ew = jax.nn.softmax(ev, axis=-1) * gp
    flat = gidx * MOE_EXPERTS_PER_GROUP + eidx
    combine = jnp.sum(jax.nn.one_hot(flat, MOE_N_EXPERTS, dtype=jnp.float32) * ew[..., None], axis=1)
    combine = combine.astype(xf.dtype)
    y = jnp.zeros((t_, d_), xf.dtype)
    for gi in range(MOE_GROUPS):
        cw = combine[:, gi * MOE_EXPERTS_PER_GROUP:(gi + 1) * MOE_EXPERTS_PER_GROUP]
        hg = jnp.einsum("td,edf->tef", xf, w_gate[gi])
        hu = jnp.einsum("td,edf->tef", xf, w_up[gi])
        hh = jax.nn.silu(hg) * hu * cw[:, :, None]
        y = y + jnp.einsum("tef,efd->td", hh, w_down[gi])
    return y.reshape(b_, s_, d_)

def setup_inputs(seed: int = 0) -> dict:
    key = jax.random.key(seed)
    ks = iter(jax.random.split(key, 40))

    def nrm(shape, scale):
        return jax.random.normal(next(ks), shape, jnp.float32) * scale

    def gain(shape):
        return 1.0 + nrm(shape, 0.05)

    dt = jnp.exp(jax.random.uniform(next(ks), (N_A_LAYERS, GDN_HEADS), jnp.float32,
                                    float(np.log(1e-3)), float(np.log(1e-1))))
    return {
        "x": nrm((BATCH, SEQ, D_MODEL), 1.0),
        "p": nrm((DEPTH, BATCH, SEQ, PLE_DIM), 1.0),
        "attn_norm": gain((DEPTH, D_MODEL)),
        "moe_norm": gain((DEPTH, D_MODEL)),
        "ple_norm": gain((DEPTH, D_MODEL)),
        "gdn_w_in": nrm((N_A_LAYERS, D_MODEL, GDN_IN_DIM), D_MODEL ** -0.5),
        "gdn_conv": nrm((N_A_LAYERS, GDN_CONV, GDN_QKV_DIM), GDN_CONV ** -0.5),
        "gdn_a_log": jnp.log(jax.random.uniform(next(ks), (N_A_LAYERS, GDN_HEADS), jnp.float32, 1.0, 16.0)),
        "gdn_dt_bias": dt + jnp.log(-jnp.expm1(-dt)),
        "gdn_o_norm": gain((N_A_LAYERS, GDN_HEAD_DIM)),
        "gdn_w_out": nrm((N_A_LAYERS, GDN_VALUE_DIM, D_MODEL), GDN_VALUE_DIM ** -0.5),
        "kv_norm": gain((D_MODEL,)),
        "w_kv": nrm((D_MODEL, 2 * SB_KV_HEADS * SB_HEAD_DIM), D_MODEL ** -0.5),
        "sb_w_q": nrm((N_B_LAYERS, D_MODEL, SB_Q_HEADS * SB_HEAD_DIM), D_MODEL ** -0.5),
        "sb_w_out": nrm((N_B_LAYERS, SB_Q_HEADS * SB_HEAD_DIM, D_MODEL), (SB_Q_HEADS * SB_HEAD_DIM) ** -0.5),
        "moe_w_group": nrm((DEPTH, D_MODEL, MOE_GROUPS), D_MODEL ** -0.5),
        "moe_b_group": nrm((DEPTH, MOE_GROUPS), 0.01),
        "moe_w_expert": nrm((DEPTH, D_MODEL, MOE_N_EXPERTS), D_MODEL ** -0.5),
        "moe_b_expert": nrm((DEPTH, MOE_N_EXPERTS), 0.01),
        "moe_w_gate": nrm((DEPTH, MOE_GROUPS, MOE_EXPERTS_PER_GROUP, D_MODEL, MOE_D_EXPERT), D_MODEL ** -0.5),
        "moe_w_up": nrm((DEPTH, MOE_GROUPS, MOE_EXPERTS_PER_GROUP, D_MODEL, MOE_D_EXPERT), D_MODEL ** -0.5),
        "moe_w_down": nrm((DEPTH, MOE_GROUPS, MOE_EXPERTS_PER_GROUP, MOE_D_EXPERT, D_MODEL), MOE_D_EXPERT ** -0.5),
        "ple_w_gate": nrm((DEPTH, D_MODEL, D_MODEL), D_MODEL ** -0.5),
        "ple_w_proj": nrm((DEPTH, PLE_DIM, D_MODEL), PLE_DIM ** -0.5),
        "final_norm": gain((D_MODEL,)),
    }

def reference(x, p, attn_norm, moe_norm, ple_norm, gdn_w_in, gdn_conv, gdn_a_log, gdn_dt_bias,
              gdn_o_norm, gdn_w_out, kv_norm, w_kv, sb_w_q, sb_w_out, moe_w_group, moe_b_group,
              moe_w_expert, moe_b_expert, moe_w_gate, moe_w_up, moe_w_down, ple_w_gate, ple_w_proj,
              final_norm):
    h = x
    b_, s_, _ = x.shape
    kv_dim = SB_KV_HEADS * SB_HEAD_DIM
    k_shared = None
    v_shared = None
    for i in range(DEPTH):
        if i < N_A_LAYERS:
            a = i
            mix = gated_deltanet(rms_norm(h, attn_norm[i]), gdn_w_in[a], gdn_conv[a], gdn_a_log[a],
                                 gdn_dt_bias[a], gdn_o_norm[a], gdn_w_out[a])
        else:
            if i == N_A_LAYERS:
                kv = rms_norm(h, kv_norm) @ w_kv
                k_shared = kv[..., :kv_dim].reshape(b_, s_, SB_KV_HEADS, SB_HEAD_DIM)
                v_shared = kv[..., kv_dim:].reshape(b_, s_, SB_KV_HEADS, SB_HEAD_DIM)
            bi = i - N_A_LAYERS
            mix = stick_breaking_mixer(rms_norm(h, attn_norm[i]), k_shared, v_shared, sb_w_q[bi], sb_w_out[bi])
        h = h + mix.astype(h.dtype)
        h = h + hierarchical_moe(rms_norm(h, moe_norm[i]), moe_w_group[i], moe_b_group[i], moe_w_expert[i],
                                 moe_b_expert[i], moe_w_gate[i], moe_w_up[i], moe_w_down[i]).astype(h.dtype)
        gate = jax.nn.sigmoid((rms_norm(h, ple_norm[i]) @ ple_w_gate[i]).astype(jnp.float32))
        emb = (p[i] @ ple_w_proj[i]).astype(jnp.float32)
        h = h + (gate * emb).astype(h.dtype)
    return rms_norm(h, final_norm)


_drawn_inputs = setup_inputs


def setup_inputs(seed=0):
    import zlib

    import numpy as np

    out = dict(_drawn_inputs(seed))
    spreads = {}
    factors = {'ple_norm': 3.239, 'moe_b_group': 5.248, 'moe_b_expert': 3.104}
    for name, (base, spread) in spreads.items():
        noise = np.random.default_rng([zlib.crc32(name.encode()), seed]).standard_normal(out[name].shape)
        drawn = base * np.exp(spread * noise) if base else spread * noise
        out[name] = __import__('jax').numpy.asarray(drawn.astype(out[name].dtype))
    for name, factor in factors.items():
        out[name] = (out[name] * factor).astype(out[name].dtype)
    return out
```

```python
from contextlib import ExitStack

import concourse.bass as bass
from concourse import mybir
from concourse.alu_op_type import AluOpType as ALU

ACT = mybir.ActivationFunctionType
F32 = mybir.dt.float32
I32 = mybir.dt.int32
AX_X = mybir.AxisListType.X

P = 128
T = 256
TT = T // P
D = 1024
KT = D // P
HALF = 512
NH, DH = 8, 128
CONV = 4
QH, KVH, SD = 16, 4, 64
NG, NE, FE = 4, 32, 256
EPG = NE // NG
CAP = 64
SLOTS = 2 * T
SPAD = SLOTS + CAP
RING = 4
PLE = 256
EPS = 1e-6
BIG = 1e30
LEVELS = [1 << n for n in range(7)]

CHUNKS = ["qk0", "v0", "qk1", "qk2", "v1", "qk3", "z0", "z1", "go0", "go1",
          "pg0.0", "pg0.1", "pp0", "kv", "sq0", "sq1", "so0", "so1", "pg1.0", "pg1.1", "pp1"]
WSLOTS = 3

NORMS = ["attn0", "moe0", "ple0", "attn1", "moe1", "ple1"]


def gdn_plan():
    steps = [("norm", 0), ("gram", 0), ("flip", 0)]
    for n in range(1, len(LEVELS)):
        steps += [("half", n), ("full", n)]
    steps += [("new0", 0), ("state", 0), ("read", 0), ("new1", 0), ("out", 0)]
    plan = [("mm", j, k) for j in range(6) for k in range(KT)]
    for pair in range(NH // 2):
        fill = [("mm", 6 * (pair + 1) + j, k) for j in range(6) for k in range(KT)] if pair < 3 \
            else [("zmm", j, k) for j in range(4) for k in range(KT)]
        done = 0
        for n, (name, level) in enumerate(steps):
            plan.append(("step", pair, name, level))
            want = len(fill) * (n + 1) // len(steps)
            plan += fill[done:want]
            done = want
    return plan


def tile_of(j):
    pair, i = divmod(j, 6)
    kind, head = divmod(i, 2)
    if kind < 2:
        return f"qk{pair}", 256 * kind + 128 * head, 8 * kind + 2 * pair + head
    return f"v{pair // 2}", 256 * (pair % 2) + 128 * head, 16 + 2 * pair + head


def yoco_kernel(nc, x, p, attn_norm, moe_norm, ple_norm, gdn_w_in, gdn_conv, gdn_a_log, gdn_dt_bias,
                gdn_o_norm, gdn_w_out, kv_norm, w_kv, sb_w_q, sb_w_out, moe_w_group, moe_b_group,
                moe_w_expert, moe_b_expert, moe_w_gate, moe_w_up, moe_w_down, ple_w_gate, ple_w_proj,
                final_norm, out):
    ctx = ExitStack()
    with ctx:
        def sb(name, shape, dt=F32):
            return ctx.enter_context(nc.sbuf_tensor(name, shape, dt))

        sems = {}

        def sem(name):
            if name not in sems:
                sems[name] = ctx.enter_context(nc.semaphore(name))
            return sems[name]

        bank = [ctx.enter_context(nc.psum_tensor(f"bank{i}", [P, HALF], F32)) for i in range(8)]

        moe_w = sb("moe_w", [P, RING, 3, KT * FE])
        wring = sb("wring", [P, WSLOTS, KT * HALF])
        h = sb("h", [P, TT, D])
        xh = sb("xh", [P, TT, KT, P])
        xT = sb("xT", [P, KT, T])
        region = sb("region", [P, KT * SPAD])
        scr = sb("scr", [P, 3072])
        ident = sb("ident", [P, P])
        upper = sb("upper", [P, P])
        below = sb("below", [P, P])
        lower = sb("lower", [P, P])
        ones = sb("ones", [P, P])
        iota = sb("iota", [P, SLOTS])
        rev_idx = sb("rev_idx", [P, NE])
        gains = sb("gains", [P, 7, KT])
        w_ab = sb("w_ab", [P, KT, 2 * NH])
        w_rt = sb("w_rt", [P, KT, NG + NE])
        b_rt = sb("b_rt", [P, 2, NG + NE])
        ab_row = sb("ab_row", [P, 2, NH])
        o_gain = sb("o_gain", [P, DH])
        half_neg = sb("half_neg", [P, 2 * NH])
        stat = sb("stat", [P, 2])
        rstd = sb("rstd", [P, 2])
        decay = sb("decay", [P, 10, 2 * NH])
        rank = sb("rank", [P, TT, NE])
        cw = sb("cw", [P, TT, NE])
        cw_over = sb("cw_over", [P, TT, NE])
        off_i = sb("off_i", [P, NE], I32)
        over_i = sb("over_i", [P, 1], I32)
        eps_t = sb("eps_t", [P, 2])

        slot2 = moe_w[:, 2, :, :].rearrange("p a n -> p (a n)")
        slot3 = moe_w[:, 3, :, :].rearrange("p a n -> p (a n)")
        qkvT = slot3.rearrange("p (n t) -> p n t", t=T)
        zs = slot2[:, 0:2048].rearrange("p (c n) -> p c n", c=TT)
        o_tok = slot2[:, 2048:4096].rearrange("p (c h n) -> p c h n", c=TT, h=NH)
        sq = slot2[:, 4096:5120]
        blk = slot2[:, 5120:5120 + 7 * P].rearrange("p (n q) -> p n q", q=P)
        mats = region[:, 0:9 * 512].rearrange("p (m n q) -> p m n q", m=9, n=4)
        Lm, Am, LTm, ATm, Tm, Zm, Xm, Dm, LMm = (mats[:, i] for i in range(9))
        v_tok = scr[:, 0:512].rearrange("p (u n) -> p u n", u=4)
        k_tok = scr[:, 512:768].rearrange("p (u n) -> p u n", u=2)
        S_st = scr[:, 768:1024].rearrange("p (u n) -> p u n", u=2)
        B_in = scr[:, 1024:1280].rearrange("p (u n) -> p u n", u=2)
        v_new = scr[:, 1280:1792].rearrange("p (u n) -> p u n", u=4)
        q_st = scr[:, 1792:2048].rearrange("p (u n) -> p u n", u=2)
        cv = scr[:, 2048:2560].rearrange("p (u n) -> p u n", u=2)
        conv_rows = scr[0:CONV * 24, 2560:2688]
        conv_w = scr[:, 2688:2784].rearrange("p (t n) -> p t n", t=CONV)
        o_sum = scr[:, 2784:2800]
        xs = region[:, :].rearrange("p (k s) -> p k s", k=KT)
        xe = scr[:, 0:1024].rearrange("p (b k s) -> p b k s", b=2, k=KT)
        ye = scr[:, 1024:1536]
        rw = scr[:, 1536:1792].rearrange("p (c s) -> p c s", c=TT)
        sg = scr[:, 1792:2048]
        hh = scr[:, 2048:2304]
        hr = scr[:, 2304:3072].rearrange("p (b n) -> p b n", b=2)
        one_hot = scr[:, 0:1024].rearrange("p (c s) -> p c s", c=TT)
        rt = scr[:, 1024:3072].rearrange("p (n c e) -> p n c e", c=TT, e=NE)
        xkvT = region[:, 0:2048].rearrange("p (k t) -> p k t", k=KT)
        qT = region[:, 2048:4096].rearrange("p (k t) -> p k t", k=KT)
        kT = scr[:, 0:1024].rearrange("p (g t) -> p g t", g=KVH)
        v_sb = scr[:, 1024:1536].rearrange("p (c n) -> p c n", c=TT)
        soft = xkvT.rearrange("p k t -> p (k t)")[:, 0:768].rearrange("p (b n) -> p b n", b=2)
        soft_u = xkvT.rearrange("p k t -> p (k t)")[:, 768:1536].rearrange("p (b n) -> p b n", b=2)
        attn = scr[:, 1536:2304].rearrange("p (b n) -> p b n", b=2)
        p_tok = scr[:, 0:512].rearrange("p (c n) -> p c n", c=TT)
        pT = scr[:, 512:1024].rearrange("p (j t) -> p j t", j=2)
        gate = scr[:, 1024:3072].rearrange("p (n q) -> p n q", n=4)
        fin_gain = region[:, 0:D]
        fin_out = region[:, D:3 * D].rearrange("p (c n) -> p c n", c=TT)

        def dchunk(name):
            at = CHUNKS.index(name) % WSLOTS
            slot = wring[:, at, :]
            wide = slot.rearrange("p (k n) -> p k n", k=KT)

            def by_row(w):
                return w.rearrange("(p k) n -> p k n", k=KT)

            def by_tile(w):
                return w.rearrange("(k p) n -> p k n", p=P)
            if name[:2] == "qk":
                n = int(name[2])
                w = by_row(gdn_w_in[0])
                return [(wide[:, :, 256 * a:256 * a + 256], w[:, :, D * a + 256 * n:D * a + 256 * n + 256])
                        for a in range(2)]
            half = int(name[-1])
            cols = slice(HALF * half, HALF * half + HALF)
            if name[0] == "v":
                return [(wide, by_row(gdn_w_in[0])[:, :, 2 * D + HALF * half:2 * D + HALF * half + HALF])]
            if name[0] == "z":
                return [(wide, by_row(gdn_w_in[0])[:, :, 3 * D + HALF * half:3 * D + HALF * half + HALF])]
            if name[:2] == "go":
                return [(wide, by_tile(gdn_w_out[0])[:, :, cols])]
            if name[:2] == "pg":
                return [(wide, by_row(ple_w_gate[int(name[2])])[:, :, cols])]
            if name[:2] == "pp":
                return [(slot[:, 0:2 * D].rearrange("p (j n) -> p j n", j=2),
                         ple_w_proj[half].rearrange("(j p) n -> p j n", p=P))]
            if name[:2] == "sq":
                return [(wide, by_row(sb_w_q[0])[:, :, cols])]
            if name[:2] == "so":
                return [(wide, by_tile(sb_w_out[0])[:, :, cols])]
            raise ValueError(name)

        def chunk_parts(name):
            if name == "kv":
                slot = wring[:, CHUNKS.index(name) % WSLOTS, :]
                return [(slot.rearrange("p (k n) -> p k n", k=KT), w_kv.rearrange("(p k) n -> p k n", k=KT))]
            return dchunk(name)

        def chunk(name):
            return wring[:, CHUNKS.index(name) % WSLOTS, :].rearrange("p (k n) -> p k n", k=KT)

        landed, slot_count = {}, [0] * WSLOTS
        for n, name in enumerate(CHUNKS):
            slot_count[n % WSLOTS] += 16 * len(chunk_parts(name))
            landed[name] = slot_count[n % WSLOTS]

        def wait_chunk(eng, name):
            eng.wait_ge(sem(f"chunk_landed{CHUNKS.index(name) % WSLOTS}"), landed[name])

        def chunk_used(name):
            if name[:2] == "qk":
                return sem("proj_done"), 6 * int(name[2]) + 4
            if name[0] == "v":
                return sem("proj_done"), 12 * int(name[1]) + 12
            if name[0] == "z":
                return sem("z_done"), 2 * int(name[1]) + 2
            if name[:2] == "go":
                return sem("gdn_out_done"), 2 * int(name[2]) + 2
            if name[:2] == "pg":
                return sem("ple_gate_done"), 4 * int(name[2]) + 2 * int(name[4]) + 2
            if name[:2] == "pp":
                return sem("ple_emb_done"), 4 * int(name[2]) + 4
            if name == "kv":
                return sem("kv_done"), 4
            if name[:2] == "sq":
                return sem("sbq_done"), 4 * int(name[2]) + 4
            return sem("sb_out_done"), 2 * int(name[2]) + 2

        def chain_of(eng, name):
            count = [0]

            def link(ins):
                count[0] += 1
                ins.then_inc(sem(name), 1)
                eng.wait_ge(sem(name), count[0])
            return link

        def over_w(n):
            return (region[:, 0:2048], region[:, 2048:4096], xh[:, :, :, :].rearrange("p c k q -> p (c k q)"))[n]

        over_g = scr[:, 0:512].rearrange("p (f t) -> p f t", f=2)
        over_col = scr[:, 512:514]

        plan = gdn_plan()
        block = ctx.enter_context(nc.Block())

        @block.sync
        def _(sp):
            def load_chunk(n):
                name = CHUNKS[n]
                if n >= WSLOTS:
                    sp.wait_ge(*chunk_used(CHUNKS[n - WSLOTS]))
                for dst, src in chunk_parts(name):
                    sp.dma_start(dst, src).then_inc(sem(f"chunk_landed{n % WSLOTS}"), 16)

            def load_expert(layer, e, slot):
                g, i = (e // EPG, e % EPG) if isinstance(e, int) else (None, None)
                for n, w in enumerate((moe_w_gate, moe_w_up, moe_w_down)):
                    flat = w[layer].rearrange("g e a b -> (g e) (a b)").rearrange("e (p n) -> e p n", p=P)
                    src = flat[e, :, :] if isinstance(e, int) else flat[bass.ds(e, 1), :, :].rearrange(
                        "e p n -> (e p) n")
                    name = "expert_gu" if n < 2 else "expert_d"
                    sp.dma_start(moe_w[:, slot, n, :], src).then_inc(sem(f"{name}{slot}"), 16)

            def load_experts(layer):
                with sp.Fori(1, NE // RING) as i:
                    for s in range(RING):
                        sp.wait_ge(sem("down_done"), i * RING + (NE * layer + s - RING + 1))
                        load_expert(layer, i * RING + s, s)

            sp.dma_start(h[:, :, :], x[0].rearrange("(c p) d -> p c d", p=P)).then_inc(sem("x_landed"), 16)
            small = sem("small_landed")
            for i, g in enumerate((attn_norm[0], moe_norm[0], ple_norm[0], attn_norm[1], moe_norm[1],
                                   ple_norm[1], kv_norm)):
                sp.dma_start(gains[:, i, :], g.rearrange("(p k) -> p k", k=KT)).then_inc(small, 16)
            sp.dma_start(conv_rows, gdn_conv[0].rearrange("t (n c) -> (t n) c", c=P)).then_inc(small, 16)
            sp.dma_start(w_ab[:, :, :], gdn_w_in[0].rearrange("(p k) n -> p k n", k=KT)[:, :, 4 * D:4 * D + 16]
                         ).then_inc(small, 16)
            load_chunk(0)
            load_chunk(1)
            load_chunk(2)
            for i, row in enumerate((gdn_a_log, gdn_dt_bias)):
                sp.dma_start(ab_row[:, i, :], row.broadcast_to([P, NH])).then_inc(small, 16)
            sp.dma_start(o_gain[:, :], gdn_o_norm.broadcast_to([P, DH])).then_inc(small, 16)
            for i in range(2):
                sp.dma_start(b_rt[:, i, 0:NG], moe_b_group[i:i + 1, :].broadcast_to([P, NG])).then_inc(small, 16)
                sp.dma_start(b_rt[:, i, NG:], moe_b_expert[i:i + 1, :].broadcast_to([P, NE])).then_inc(small, 16)

            def load_router(layer):
                rtr = sem("router_landed")
                sp.dma_start(w_rt[:, :, 0:NG], moe_w_group[layer].rearrange("(p k) n -> p k n", k=KT)
                             ).then_inc(rtr, 16)
                sp.dma_start(w_rt[:, :, NG:], moe_w_expert[layer].rearrange("(p k) n -> p k n", k=KT)
                             ).then_inc(rtr, 16)

            load_router(0)
            load_expert(0, 0, 0)
            load_expert(0, 1, 1)
            for n in range(WSLOTS, CHUNKS.index("go1") + 1):
                load_chunk(n)
            sp.wait_ge(sem("oT_flip_done"), 4)
            load_expert(0, 2, 2)
            load_expert(0, 3, 3)
            for n in range(CHUNKS.index("pg0.0"), CHUNKS.index("pp0") + 1):
                load_chunk(n)
            load_experts(0)
            for layer in range(2):
                if layer == 1:
                    load_experts(1)
                sp.wait_ge(sem("routed"), layer + 1)
                flag = sp.value_load(over_i[0:1, 0:1], min_val=0, max_val=1)
                with sp.If(flag > 0):
                    with sp.Fori(0, NE) as e:
                        sp.wait_ge(sem(f"over_free{layer}"), e + 1)
                        for n, w in enumerate((moe_w_gate, moe_w_up, moe_w_down)):
                            flat = w[layer].rearrange("g e a b -> (g e) (a b)").rearrange("e (p n) -> e p n", p=P)
                            sp.dma_start(over_w(n), flat[bass.ds(e, 1), :, :].rearrange("e p n -> (e p) n")
                                         ).then_inc(sem(f"over_landed{layer}"), 16)
                sp.wait_ge(sem("xh_dve"), 3 * layer + 3)
                sp.dma_start(p_tok, p[layer, 0].rearrange("(c p) d -> p c d", p=P)).then_inc(sem("p_landed"), 16)
                if layer == 0:
                    load_router(1)
                    for s in range(RING):
                        sp.wait_ge(sem("down_done"), NE - RING + s + 1)
                        load_expert(1, s, s)
                    for n in range(CHUNKS.index("kv"), len(CHUNKS)):
                        load_chunk(n)
            sp.wait_ge(sem("ple_h"), 8)
            sp.dma_start(fin_gain, final_norm.rearrange("(a n) -> a n", a=1).broadcast_to([P, D])
                         ).then_inc(sem("fin_gain_landed"), 16)
            for c in range(TT):
                sp.wait_ge(sem("fin_ready"), c + 1)
                sp.dma_start(out[0].rearrange("(c p) d -> p c d", p=P)[:, c, :], fin_out[:, c, :]
                             ).then_inc(sem("out_stored"), 16)
            sp.wait_ge(sem("out_stored"), 32)

        @block.gpsimd
        def _(pool):
            link = chain_of(pool, "pool_chain")
            for t in (ident, upper, below, lower):
                pool.memset(t[:, :], 0.0 if t is ident else 1.0).then_inc(sem("mask_set"), 1)
            pool.memset(half_neg[:, :], -0.5).then_inc(sem("const_set"), 1)
            pool.memset(ones[:, :], 1.0).then_inc(sem("const_set"), 1)
            pool.wait_ge(sem("mask_set"), 4)
            pool.affine_select(out=ident[:, :], in_=ident[:, :], compare_op=ALU.not_equal, fill=1.0, base=0,
                               pattern=[[-1, P]], channel_multiplier=1).then_inc(sem("const_set"), 1)
            pool.affine_select(out=upper[:, :], in_=upper[:, :], compare_op=ALU.is_ge, fill=0.0, base=0,
                               pattern=[[1, P]], channel_multiplier=-1).then_inc(sem("const_set"), 1)
            pool.affine_select(out=below[:, :], in_=below[:, :], compare_op=ALU.is_gt, fill=0.0, base=0,
                               pattern=[[1, P]], channel_multiplier=-1).then_inc(sem("const_set"), 1)
            pool.affine_select(out=lower[:, :], in_=lower[:, :], compare_op=ALU.is_ge, fill=0.0, base=0,
                               pattern=[[-1, P]], channel_multiplier=1).then_inc(sem("const_set"), 1)

            def rsqrt(dst, src, scale, n, ready):
                link(pool.tensor_scalar(dst, src, scale, EPS, ALU.mult, ALU.add))
                pool.tensor_tensor(dst, dst, half_neg[:, 0:n], ALU.pow).then_inc(ready, 1)

            def norm_scale(n):
                pool.wait_ge(sem("norm_sums"), n + 1)
                rsqrt(rstd[:, :], stat[:, :], 1.0 / D, 2, sem("norm_rstd"))

            norm_scale(0)
            for n in range(len(LEVELS)):
                b = LEVELS[n]
                view = blk[:, n, :].rearrange("p (m b) -> p m b", b=b)
                link(pool.memset(blk[:, n, :], 1.0))
                link(pool.affine_select(out=view, in_=view, compare_op=ALU.is_ge, fill=0.0, base=0,
                                        pattern=[[-b, P // b], [0, b]], channel_multiplier=1))
                ins = pool.affine_select(out=view, in_=view, compare_op=ALU.is_ge, fill=0.0, base=b - 1,
                                         pattern=[[b, P // b], [0, b]], channel_multiplier=-1)
                if n < len(LEVELS) - 1:
                    link(ins)
                else:
                    ins.then_inc(sem("blocks_set"), 1)
            iota_i = region[:, 0:SLOTS].bitcast(I32)
            link(pool.iota(iota_i, [[1, SLOTS]], base=0, channel_multiplier=0))
            link(pool.tensor_copy(iota[:, :], iota_i))
            pool.tensor_scalar(rev_idx[:, :], iota[:, 0:NE], -1.0, float(NE), ALU.mult, ALU.add
                               ).then_inc(sem("iota_set"), 1)
            pool.wait_ge(sem("o_sums"), NH // 2)
            pool.wait_ge(sem("const_set"), 6)
            rsqrt(o_sum, o_sum, 1.0 / DH, 2 * NH, sem("o_rstd"))

            for layer in range(2):
                if layer == 1:
                    norm_scale(3)
                    for hd in range(QH):
                        pool.wait_ge(sem("attn_exp"), hd + 1)
                        view = attn[:, hd % 2, :].rearrange("p (b n) -> p b n", n=P)[:, 0:3:2, :]
                        pool.tensor_tensor(view, view, below[:, :].unsqueeze(1).broadcast_to([P, 2, P]), ALU.mult
                                           ).then_inc(sem("attn_ready"), 1)
                norm_scale(1 + 3 * layer)
                pool.wait_ge(sem("norm_rstd"), 2 + 3 * layer)
                pool.memset(xs[:, :, SLOTS:], 0.0).then_inc(sem("pad_set"), 1)
                pool.wait_ge(sem("pad_set"), layer + 1)
                pool.wait_ge(sem("xs_act"), 4 * layer + 4)
                pool.wait_ge(sem("xs_dve"), 4 * layer + 4)
                pool.wait_ge(sem("routed"), layer + 1)

                def window(e, buf, base):
                    at = pool.value_load(off_i[0:1, bass.ds(e, 1)], min_val=0, max_val=SLOTS)
                    if base is not None:
                        pool.wait_ge(sem("gu_done"), base)
                    pool.tensor_copy(xe[:, buf, :, :], xs[:, :, bass.ds(at, CAP)]).then_inc(sem("xe_ready"), 1)

                for e in range(RING):
                    window(e, e % 2, NE * layer + e - 1 if e >= 2 else None)
                with pool.Fori(1, NE // RING) as i:
                    for s in range(RING):
                        window(i * RING + s, s % 2, i * RING + (NE * layer + s - 1))
                norm_scale(2 + 3 * layer)
            pool.wait_ge(sem("norm_sums"), 7)
            rsqrt(rstd[:, :], stat[:, :], 1.0 / D, 2, sem("norm_rstd"))

        @block.scalar
        def _(act):
            link = chain_of(act, "act_chain")

            def norm_apply(n):
                act.wait_ge(sem("norm_rstd"), n + 1)
                act.activation(xh[:, 1], h[:, 1, :].rearrange("p (q k) -> p k q", k=KT), ACT.Copy,
                               scale=rstd[:, 1:2]).then_inc(sem("xh_act"), 1)

            def norm_gain(n, gain, dst, first):
                for b in range(4):
                    act.wait_ge(sem("norm_flip"), 4 * n + b + 1)
                    ins = act.activation(dst[:, 2 * b, :], bank[b][:, 0:T], ACT.Copy,
                                         scale=gains[:, gain, 2 * b:2 * b + 1])
                    ins = act.activation(dst[:, 2 * b + 1, :], bank[b][:, T:2 * T], ACT.Copy,
                                         scale=gains[:, gain, 2 * b + 1:2 * b + 2])
                    ins.then_inc(sem(f"{first}"), 1)

            act.wait_ge(sem("small_landed"), 16 * 16)
            norm_apply(0)
            norm_gain(0, 0, xT, "xT_ready")
            act.wait_ge(sem("conv_flip"), 1)
            act.activation(conv_w.rearrange("p t n -> p (t n)"), bank[4][:, 0:96], ACT.Copy
                           ).then_inc(sem("conv_ready"), 1)
            d = [decay[:, i, :] for i in range(10)]
            act.wait_ge(sem("ab_abs"), 1)
            link(act.activation(d[1], d[1], ACT.Exp, scale=-1.0))
            link(act.activation(d[1], d[1], ACT.Ln, bias=1.0))
            link(act.activation(d[4][:, 0:NH], ab_row[:, 0, :], ACT.Exp))
            act.activation(d[2], d[2], ACT.Exp, scale=-1.0).then_inc(sem("ab_exp"), 1)
            act.wait_ge(sem("cum_ready"), 1)
            link(act.activation(d[6], d[5], ACT.Exp))
            act.activation(d[7], d[7], ACT.Exp).then_inc(sem("decay_exp"), 1)

            for item in plan:
                if item[0] == "mm":
                    _, j, k = item
                    if k == KT - 1:
                        act.wait_ge(sem("conv_done"), j + 1)
                        act.activation(qkvT[:, tile_of(j)[2], :], cv[:, j % 2, :], ACT.Silu
                                       ).then_inc(sem("silu_done"), 1)
                elif item[0] == "zmm":
                    _, j, k = item
                    if k == KT - 1:
                        chunk_n, c = divmod(j, 2)
                        act.wait_ge(sem("z_done"), j + 1)
                        act.activation(zs[:, c, HALF * chunk_n:HALF * chunk_n + HALF], bank[j % 2][:, :], ACT.Silu
                                       ).then_inc(sem("z_ready"), 1)
                else:
                    _, pair, name, level = item
                    n = pair * 6 + level - 1
                    if name == "norm":
                        act.wait_ge(sem("silu_done"), 6 * pair + 4)
                        act.activation(sq[:, 0:512], qkvT[:, 2 * pair:2 * pair + 2, :].rearrange(
                            "p a t -> p (a t)"), ACT.Square).then_inc(sem("squares"), 1)
                        act.activation(sq[:, 512:1024], qkvT[:, 8 + 2 * pair:10 + 2 * pair, :].rearrange(
                            "p a t -> p (a t)"), ACT.Square).then_inc(sem("squares"), 1)
                        act.wait_ge(sem("sumsq_done"), pair + 1)
                        link(act.activation(sq[:, 0:512], bank[2][:, :], ACT.Sqrt, scale=float(DH),
                                            bias=eps_t[:, 0:1]))
                        act.activation(sq[:, 512:1024], bank[3][:, :], ACT.Sqrt, bias=eps_t[:, 1:2]
                                       ).then_inc(sem("norms_sqrt"), 1)
                        act.wait_ge(sem("decay_diff"), pair + 1)
                        act.activation(Dm, Dm, ACT.Exp, scale=-1.0).then_inc(sem("decay_mat"), 1)
                    elif name == "flip":
                        act.wait_ge(sem("flip_done"), pair + 1)
                        act.activation(ATm.rearrange("p u n -> p (u n)"), bank[3][:, :], ACT.Copy
                                       ).then_inc(sem("AT_ready"), 1)
                    elif name == "half":
                        act.wait_ge(sem("half_done"), n + 1)
                        act.activation(Xm.rearrange("p u n -> p (u n)"), bank[4][:, :], ACT.Copy
                                       ).then_inc(sem("X_ready"), 1)
                    elif name == "new0":
                        act.wait_ge(sem("new0_done"), pair + 1)
                        act.activation(v_new[:, 0:4:2, :], bank[7][:, 0:256].rearrange("p (u n) -> p u n", u=2),
                                       ACT.Copy).then_inc(sem("new0_ready"), 1)
                    elif name == "state":
                        act.wait_ge(sem("state_done"), pair + 1)
                        act.activation(S_st, bank[4][:, 0:256].rearrange("p (u n) -> p u n", u=2), ACT.Copy
                                       ).then_inc(sem("state_ready"), 1)
                    elif name == "new1":
                        act.wait_ge(sem("new1_done"), pair + 1)
                        act.activation(v_new[:, 1:4:2, :], bank[7][:, 0:256].rearrange("p (u n) -> p u n", u=2),
                                       ACT.Copy).then_inc(sem("new1_ready"), 1)
            for b in range(4):
                act.wait_ge(sem("oT_flip_done"), b + 1)
                act.activation(xT[:, 2 * b:2 * b + 2, :].rearrange("p k t -> p (k t)"), bank[b][:, :], ACT.Copy
                               ).then_inc(sem("oT_ready"), 1)

            for layer in range(2):
                if layer == 1:
                    norm_apply(3)
                    norm_gain(3, 3, xT, "xT_ready")
                    norm_gain(3, 6, xkvT, "xkv_ready")
                    for c in range(TT):
                        act.wait_ge(sem("kv_done"), c + 1)
                        act.activation(v_sb[:, c, :], bank[4 + c][:, 0:256], ACT.Copy).then_inc(sem("v_ready"), 1)
                    for g in range(2):
                        act.wait_ge(sem("kv_done"), 3 + g)
                        for a in range(2):
                            for b in range(2):
                                ins = act.activation(kT[64 * b:64 * b + 64, 2 * g + a, :],
                                                     bank[6 + g][64 * a:64 * a + 64, 0:T], ACT.Copy)
                        ins.then_inc(sem("kT_ready"), 1)
                    for i in range(KT):
                        act.wait_ge(sem("sbq_done"), i + 1)
                        act.activation(qT[:, i, :], bank[i % 2][:, 0:T], ACT.Copy, scale=-(SD ** -0.5)
                                       ).then_inc(sem("qT_ready"), 1)

                    def softplus(hd):
                        act.wait_ge(sem("z_score"), hd + 1)
                        u = soft_u[:, hd % 2, :]
                        if hd >= 2:
                            act.wait_ge(sem("soft_ready"), hd - 1)
                        link(act.activation(u, bank[hd % 3][:, 0:384], ACT.Abs))
                        link(act.activation(u, u, ACT.Exp, scale=-1.0))
                        act.activation(u, u, ACT.Ln, bias=1.0).then_inc(sem("soft_log"), 1)

                    def attn_exp(hd):
                        act.wait_ge(sem("rev_done"), hd + 1)
                        if hd >= 2:
                            act.wait_ge(sem("pv_done"), hd - 1)
                        act.activation(attn[:, hd % 2, :], bank[hd % 3][:, 0:384], ACT.Exp, scale=-1.0
                                       ).then_inc(sem("attn_exp"), 1)

                    for hd in range(QH + 1):
                        if hd < QH:
                            softplus(hd)
                        if hd >= 1:
                            attn_exp(hd - 1)

                norm_apply(1 + 3 * layer)
                norm_gain(1 + 3 * layer, 1 + 3 * layer, xT, "xT_ready")
                act.wait_ge(sem("group_shift"), layer + 1)
                act.activation(rt[:, 2, :, 0:NG], rt[:, 1, :, 0:NG], ACT.Exp).then_inc(sem("group_exp"), 1)
                act.wait_ge(sem("pair_diff"), layer + 1)
                act.activation(rt[:, 14, :, 2:3], rt[:, 14, :, 1:2], ACT.Exp).then_inc(sem("pair_exp"), 1)
                act.wait_ge(sem("counts_done"), layer + 1)
                act.activation(rt[0:NE, 15, :, :].rearrange("p c e -> p (c e)")[:, 0:64], bank[6][0:NE, 0:64],
                               ACT.Copy).then_inc(sem("counts_ready"), 1)
                for k in range(0, KT, 2):
                    act.wait_ge(sem("gather_done"), KT * layer + k + 1)
                    act.activation(xs[:, k, 0:SLOTS], bank[k % 4][:, :], ACT.Copy,
                                   scale=gains[:, 1 + 3 * layer, k:k + 1]).then_inc(sem("xs_act"), 1)

                base = NE * layer

                def bank_gu_of(s):
                    return bank[4 + s % 2]

                for e in range(RING):
                    act.wait_ge(sem("gu_done"), base + e + 1)
                    if base + e >= 1:
                        act.wait_ge(sem("hh_ready"), base + e)
                    act.activation(sg[64:128, :], bank_gu_of(e)[0:64, 0:FE], ACT.Silu).then_inc(sem("sg_ready"), 1)
                    if e >= 1:
                        act.wait_ge(sem("tr_done"), base + e)
                        if base + e - 2 >= 1:
                            act.wait_ge(sem("scat_done"), base + e - 2)
                        act.activation(hr[:, (e - 1) % 2, :], bank[6][:, 0:384], ACT.Copy
                                       ).then_inc(sem("hr_ready"), 1)
                with act.Fori(1, NE // RING) as i:
                    for s in range(RING):
                        e = i * RING + (base + s)
                        act.wait_ge(sem("gu_done"), e + 1)
                        act.wait_ge(sem("hh_ready"), e)
                        act.activation(sg[64:128, :], bank_gu_of(s)[0:64, 0:FE], ACT.Silu
                                       ).then_inc(sem("sg_ready"), 1)
                        act.wait_ge(sem("tr_done"), e)
                        act.wait_ge(sem("scat_done"), e - 2)
                        act.activation(hr[:, (s - 1) % 2, :], bank[6][:, 0:384], ACT.Copy
                                       ).then_inc(sem("hr_ready"), 1)
                act.wait_ge(sem("tr_done"), base + NE)
                act.wait_ge(sem("scat_done"), base + NE - 2)
                act.activation(hr[:, (NE - 1) % 2, :], bank[6][:, 0:384], ACT.Copy).then_inc(sem("hr_ready"), 1)

                flag = act.value_load(over_i[0:1, 0:1], min_val=0, max_val=1)
                with act.If(flag > 0):
                    with act.Fori(0, NE) as e:
                        for f in range(2):
                            act.wait_ge(sem(f"over_gu{layer}"), e * 2 + (f + 1))
                            act.activation(over_g[:, f, :], bank[4][:, 0:T], ACT.Silu
                                           ).then_inc(sem(f"over_silu{layer}"), 1)

                n = 2 + 3 * layer
                norm_apply(n)
                norm_gain(n, n, xT, "xT_ready")
                act.wait_ge(sem("p_flip"), layer + 1)
                act.activation(pT.rearrange("p j t -> p (j t)"), bank[4][:, :], ACT.Copy).then_inc(sem("pT_ready"), 1)
                for j in range(4):
                    act.wait_ge(sem("ple_gate_done"), 4 * layer + j + 1)
                    act.activation(gate[:, j, :], bank[j][:, :], ACT.Sigmoid).then_inc(sem("gate_ready"), 1)

        @block.tensor
        def _(pe):
            def norm_flip(n):
                pe.wait_ge(sem("xh_act"), n + 1)
                pe.wait_ge(sem("xh_dve"), n + 1)
                for b in range(4):
                    for k in range(2 * b, 2 * b + 2):
                        for c in range(TT):
                            col = T * (k % 2) + P * c
                            ins = pe.transpose(bank[b][:, col:col + P], xh[:, c, k, :], ident[:, :])
                    ins.then_inc(sem("norm_flip"), 1)

            def by_token(dst, src, w, c, ready, kts=KT):
                for k in range(kts):
                    ins = pe.matmul(dst, src[:, k, P * c:P * c + P], w[:, k, :], start=(k == 0),
                                    stop=(k == kts - 1))
                ins.then_inc(ready, 1)

            pe.wait_ge(sem("const_set"), 6)
            norm_flip(0)
            pe.wait_ge(sem("small_landed"), 16 * 16)
            pe.transpose(bank[4][:, 0:96], conv_rows, ident[0:96, 0:96]).then_inc(sem("conv_flip"), 1)
            pe.wait_ge(sem("xT_ready"), 4)
            for c in range(TT):
                for k in range(KT):
                    ins = pe.matmul(bank[5][:, 16 * c:16 * c + 16], xT[:, k, P * c:P * c + P], w_ab[:, k, :],
                                    start=(k == 0), stop=(k == KT - 1))
            ins.then_inc(sem("ab_done"), 1)
            pe.wait_ge(sem("g_ready"), 1)
            g_all = decay[:, 3, :]
            pe.matmul(bank[6][:, 0:16], upper[:, :], g_all, start=True, stop=True)
            pe.matmul(bank[6][:, 16:32], ones[:, :], g_all, start=True, stop=True).then_inc(sem("cum_done"), 1)

            for item in plan:
                if item[0] == "mm":
                    _, j, k = item
                    name, col, _ = tile_of(j)
                    if k == 0:
                        wait_chunk(pe, name)
                        if j >= 2:
                            pe.wait_ge(sem("conv_done"), j - 1)
                    ins = pe.matmul(bank[j % 2][:, 0:T], chunk(name)[:, k, col:col + P], xT[:, k, :],
                                    start=(k == 0), stop=(k == KT - 1))
                    if k == KT - 1:
                        ins.then_inc(sem("proj_done"), 1)
                elif item[0] == "zmm":
                    _, j, k = item
                    cn, c = divmod(j, 2)
                    if k == 0:
                        wait_chunk(pe, f"z{cn}")
                        if j < 2:
                            pe.wait_ge(sem("conv_done"), 23 + j)
                        else:
                            pe.wait_ge(sem("z_ready"), j - 1)
                    ins = pe.matmul(bank[j % 2][:, :], xT[:, k, P * c:P * c + P], chunk(f"z{cn}")[:, k, :],
                                    start=(k == 0), stop=(k == KT - 1))
                    if k == KT - 1:
                        ins.then_inc(sem("z_done"), 1)
                else:
                    _, pair, name, level = item
                    n = pair * 6 + level - 1
                    heads = (2 * pair, 2 * pair + 1)

                    def qT_of(i, c):
                        return qkvT[:, heads[i], P * c:P * c + P]

                    def kT_of(i, c):
                        return qkvT[:, 8 + heads[i], P * c:P * c + P]

                    if name == "norm":
                        if pair:
                            pe.wait_ge(sem("o_sums"), pair)
                        for a in range(2):
                            pe.wait_ge(sem("squares"), 2 * pair + a + 1)
                            ins = pe.matmul(bank[2 + a][:, :], ones[:, :], sq[:, 512 * a:512 * a + 512],
                                            start=True, stop=True)
                        ins.then_inc(sem("sumsq_done"), 1)
                        for i in range(2):
                            for c in range(TT):
                                u, col = 2 * i + c, NH * c + heads[i]
                                ins = pe.matmul(bank[4][:, P * u:P * u + P],
                                                g_all[:, col:col + 1].broadcast_to([P, P]), upper[:, :],
                                                start=True, stop=True)
                        ins.then_inc(sem("row_cum_done"), 1)
                    elif name == "gram":
                        pe.wait_ge(sem("qk_normed"), pair + 1)
                        for i in range(2):
                            for c in range(TT):
                                u = 2 * i + c
                                pe.matmul(bank[5][:, P * u:P * u + P], kT_of(i, c), kT_of(i, c), start=True, stop=True)
                        for i in range(2):
                            for c in range(TT):
                                u = 2 * i + c
                                ins = pe.matmul(bank[6][:, P * u:P * u + P], qT_of(i, c), kT_of(i, c),
                                                start=True, stop=True)
                        ins.then_inc(sem("gram_done"), 1)
                        pe.wait_ge(sem("silu_done"), 6 * pair + 6)
                        pe.wait_ge(sem("decay_diff"), pair + 1)
                        for i in range(2):
                            for c in range(TT):
                                u = 2 * i + c
                                pe.transpose(bank[7][:, P * u:P * u + P],
                                             qkvT[:, 16 + heads[i], P * c:P * c + P], ident[:, :])
                            ins = pe.transpose(bank[4][:, P * i:P * i + P], kT_of(i, 0), ident[:, :])
                        ins.then_inc(sem("kv_flip_done"), 1)
                    elif name == "flip":
                        pe.wait_ge(sem("gram_ready"), pair + 1)
                        for u in range(4):
                            pe.transpose(bank[2][:, P * u:P * u + P], Lm[:, u, :], ident[:, :])
                        for u in range(4):
                            ins = pe.transpose(bank[3][:, P * u:P * u + P], Am[:, u, :], ident[:, :])
                        ins.then_inc(sem("flip_done"), 1)
                    elif name == "half":
                        pe.wait_ge(sem("level_ready"), n + 1)
                        for u in range(4):
                            ins = pe.matmul(bank[4][:, P * u:P * u + P], LMm[:, u, :], Tm[:, u, :],
                                            start=True, stop=True)
                        ins.then_inc(sem("half_done"), 1)
                    elif name == "full":
                        pe.wait_ge(sem("X_ready"), n + 1)
                        for u in range(4):
                            ins = pe.matmul(bank[6][:, P * u:P * u + P], Xm[:, u, :], Zm[:, u, :],
                                            start=True, stop=True)
                        if level < 6:
                            for u in range(4):
                                ins = pe.matmul(bank[5][:, P * u:P * u + P], Zm[:, u, :], Xm[:, u, :],
                                                start=True, stop=True)
                        ins.then_inc(sem("full_done"), 1)
                    elif name == "new0":
                        pe.wait_ge(sem("inverse_ready"), pair + 1)
                        for i in range(2):
                            ins = pe.matmul(bank[7][:, P * i:P * i + P], Zm[:, 2 * i, :], B_in[:, i, :],
                                            start=True, stop=True)
                        ins.then_inc(sem("new0_done"), 1)
                    elif name == "state":
                        pe.wait_ge(sem("new0_ready"), pair + 1)
                        for i in range(2):
                            ins = pe.matmul(bank[4][:, P * i:P * i + P], k_tok[:, i, :], v_new[:, 2 * i, :],
                                            start=True, stop=True)
                        ins.then_inc(sem("state_done"), 1)
                    elif name == "read":
                        pe.wait_ge(sem("state_ready"), pair + 1)
                        for i in range(2):
                            ins = pe.matmul(bank[5][:, P * i:P * i + P], kT_of(i, 1), S_st[:, i, :],
                                            start=True, stop=True)
                        ins.then_inc(sem("read_done"), 1)
                    elif name == "new1":
                        pe.wait_ge(sem("B1_ready"), pair + 1)
                        for i in range(2):
                            pe.matmul(bank[6][:, P * i:P * i + P], qT_of(i, 1), S_st[:, i, :],
                                      start=True, stop=True)
                        for i in range(2):
                            ins = pe.matmul(bank[7][:, P * i:P * i + P], Zm[:, 2 * i + 1, :], B_in[:, i, :],
                                            start=True, stop=True)
                        ins.then_inc(sem("new1_done"), 1)
                    elif name == "out":
                        pe.wait_ge(sem("new1_ready"), pair + 1)
                        for u in range(4):
                            ins = pe.matmul(bank[2][:, P * u:P * u + P], ATm[:, u, :], v_new[:, u, :],
                                            start=True, stop=True)
                        ins.then_inc(sem("o_done"), 1)

            pe.wait_ge(sem("o_gated"), 1)
            for b in range(4):
                for hd in range(2 * b, 2 * b + 2):
                    for c in range(TT):
                        col = T * (hd % 2) + P * c
                        ins = pe.transpose(bank[b][:, col:col + P], o_tok[:, c, hd, :], ident[:, :])
                ins.then_inc(sem("oT_flip_done"), 1)
            pe.wait_ge(sem("oT_ready"), 4)
            for half in range(2):
                wait_chunk(pe, f"go{half}")
                for c in range(TT):
                    by_token(bank[4 + 2 * half + c][:, :], xT, chunk(f"go{half}"), c, sem("gdn_out_done"))

            for layer in range(2):
                if layer == 1:
                    norm_flip(3)
                    pe.wait_ge(sem("xkv_ready"), 4)
                    wait_chunk(pe, "kv")
                    pe.wait_ge(sem("ple_h"), 4)
                    for c in range(TT):
                        by_token(bank[4 + c][:, 0:256], xkvT, chunk("kv")[:, :, 256:512], c, sem("kv_done"))
                    for g in range(2):
                        for k in range(KT):
                            ins = pe.matmul(bank[6 + g][:, 0:T], chunk("kv")[:, k, P * g:P * g + P], xkvT[:, k, :],
                                            start=(k == 0), stop=(k == KT - 1))
                        ins.then_inc(sem("kv_done"), 1)
                    pe.wait_ge(sem("xT_ready"), 16)
                    for i in range(KT):
                        cn = i // 4
                        if i % 4 == 0:
                            wait_chunk(pe, f"sq{cn}")
                        if i >= 2:
                            pe.wait_ge(sem("qT_ready"), i - 1)
                        for k in range(KT):
                            ins = pe.matmul(bank[i % 2][:, 0:T], chunk(f"sq{cn}")[:, k, P * (i % 4):P * (i % 4) + P],
                                            xT[:, k, :], start=(k == 0), stop=(k == KT - 1))
                        ins.then_inc(sem("sbq_done"), 1)
                    pe.wait_ge(sem("kT_ready"), 2)
                    pe.wait_ge(sem("v_ready"), 2)
                    pe.wait_ge(sem("qT_ready"), KT)

                    def score(hd):
                        lo = 64 * (hd % 2)
                        if hd >= 3:
                            pe.wait_ge(sem("attn_exp"), hd - 2)
                        k_, q_ = kT[lo:lo + 64, hd // 4, :], qT[lo:lo + 64, hd // 2, :]
                        b = bank[hd % 3]
                        pe.matmul(b[:, 0:256], k_[:, 0:P], q_, start=True, stop=True)
                        pe.matmul(b[:, 256:384], k_[:, P:T], q_[:, P:T], start=False, stop=True,
                                  skip_group_check=True).then_inc(sem("z_score"), 1)

                    def reverse(hd):
                        pe.wait_ge(sem("soft_ready"), hd + 1)
                        b, s_ = bank[hd % 3], soft[:, hd % 2, :]
                        pe.matmul(b[:, 0:256], lower[:, :], s_[:, 0:256], start=False, stop=False,
                                  skip_group_check=True)
                        pe.matmul(b[:, 128:256], ones[:, :], s_[:, 256:384], start=False, stop=False,
                                  skip_group_check=True)
                        pe.matmul(b[:, 256:384], lower[:, :], s_[:, 256:384], start=False, stop=True,
                                  skip_group_check=True).then_inc(sem("rev_done"), 1)

                    def values(hd):
                        lo, g = 64 * (hd % 2), hd // 4
                        pe.wait_ge(sem("attn_ready"), hd + 1)
                        if hd % 2 == 0 and hd >= 4:
                            pe.wait_ge(sem("sbo_ready"), hd // 2 - 1)
                        a = attn[:, hd % 2, :]
                        o = bank[3 + (hd // 2) % 2][lo:lo + 64, 0:T]
                        pe.matmul(o, v_sb[:, 0, SD * g:SD * g + SD], a[:, 0:256], start=True, stop=False,
                                  skip_group_check=True)
                        pe.matmul(o[:, 128:256], v_sb[:, 1, SD * g:SD * g + SD], a[:, 256:384], start=False,
                                  stop=True, skip_group_check=True).then_inc(sem("pv_done"), 1)

                    for hd in range(QH + 2):
                        if hd < QH:
                            score(hd)
                        if 1 <= hd <= QH:
                            reverse(hd - 1)
                        if hd >= 2:
                            values(hd - 2)
                    pe.wait_ge(sem("sbo_ready"), KT)
                    for half in range(2):
                        wait_chunk(pe, f"so{half}")
                        for c in range(TT):
                            by_token(bank[5 + c if half == 0 else 7 * (c == 0)][:, :], xT, chunk(f"so{half}"), c,
                                     sem("sb_out_done"))

                n = 1 + 3 * layer
                norm_flip(n)
                pe.wait_ge(sem("xT_ready"), 4 * (n + 1))
                pe.wait_ge(sem("router_landed"), 32 * (layer + 1))
                for c in range(TT):
                    for k in range(KT):
                        ins = pe.matmul(bank[4][:, 36 * c:36 * c + 36], xT[:, k, P * c:P * c + P], w_rt[:, k, :],
                                        start=(k == 0), stop=(k == KT - 1))
                ins.then_inc(sem("logits_done"), 1)
                pe.wait_ge(sem("chosen"), layer + 1)
                ch = rt[:, 9, :, :]
                pe.matmul(bank[5][:, 0:32], below[:, :], ch[:, 0, :], start=True, stop=True)
                pe.matmul(bank[5][:, 32:64], ones[:, :], ch[:, 0, :], start=True, stop=False)
                pe.matmul(bank[5][:, 32:64], below[:, :], ch[:, 1, :], start=False, stop=True)
                for c in range(TT):
                    pe.matmul(bank[5][:, 64:96], ones[:, :], ch[:, c, :], start=(c == 0), stop=(c == 1))
                for c in range(TT):
                    ins = pe.matmul(bank[6][0:NE, 0:64], ch[:, c, :], ones[:, 0:64], start=(c == 0), stop=(c == 1))
                ins.then_inc(sem("counts_done"), 1)
                pe.wait_ge(sem("counts_ready"), layer + 1)
                cnt = rt[0:NE, 15, :, :].rearrange("p c e -> p (c e)")
                for a in range(2):
                    ins = pe.matmul(bank[7][64 * a:64 * a + 64, 0:NE], cnt[:, 0:64], below[0:NE, 0:NE],
                                    start=True, stop=True)
                ins.then_inc(sem("offsets_done"), 1)
                pe.wait_ge(sem("one_hot_ready"), layer + 1)
                for k in range(KT):
                    if k >= 4:
                        pe.wait_ge(sem("xs_act" if k % 2 == 0 else "xs_dve"), 4 * layer + (k - 4) // 2 + 1)
                    for c in range(TT):
                        ins = pe.matmul(bank[k % 4][:, :], xh[:, c, k, :], one_hot[:, c, :], start=(c == 0),
                                        stop=(c == 1))
                    ins.then_inc(sem("gather_done"), 1)
                pe.wait_ge(sem("xs_act"), 4 * layer + 4)
                pe.wait_ge(sem("xs_dve"), 4 * layer + 4)

                base = NE * layer

                def gate_up(e, s, turn):
                    pe.wait_ge(sem(f"expert_gu{s}"), turn * 32 + 32)
                    pe.wait_ge(sem("xe_ready"), e + 1)
                    b = bank[4 + s % 2]
                    w = moe_w[:, s, :, :].rearrange("p a (k f) -> p a k f", k=KT)
                    for k in range(KT):
                        for a in range(2):
                            ins = pe.matmul(b[64 * a:64 * a + 64, 0:FE], xe[:, s % 2, k, :], w[:, a, k, :],
                                            start=(k == 0), stop=(k == KT - 1), skip_group_check=True)
                    ins.then_inc(sem("gu_done"), 1)

                def turns(e, s):
                    pe.wait_ge(sem("hh_ready"), e + 1)
                    pe.wait_ge(sem("rw_ready"), e + 1)
                    for c in range(TT):
                        pe.transpose(bank[6][:, P + P * c:2 * P + P * c], rw[:, c, :], ident[:, :])
                    for j in range(2):
                        ins = pe.transpose(bank[6][:, 64 * j:64 * j + 64], hh[64:128, j:FE:2], ident[64:128, 64:128])
                    ins.then_inc(sem("tr_done"), 1)

                def down(e, s, turn):
                    pe.wait_ge(sem(f"expert_d{s}"), turn * 16 + 16)
                    pe.wait_ge(sem("hr_ready"), e + 1)
                    w = moe_w[:, s, 2, :].rearrange("p (j d) -> p j d", j=2)
                    for j in range(2):
                        for a in range(2):
                            ins = pe.matmul(bank[7][64 * a:64 * a + 64, :], hr[:, s % 2, 64 * j:64 * j + 64],
                                            w[:, j, HALF * a:HALF * a + HALF], start=(j == 0), stop=(j == 1),
                                            skip_group_check=True)
                    ins.then_inc(sem("down_done"), 1)

                def scatter(e, s, first, last):
                    pe.wait_ge(sem("ye_ready"), e + 1)
                    for c in range(TT):
                        for a in range(2):
                            ins = pe.matmul(bank[2 * c + a][:, :], hr[64 * a:64 * a + 64, s % 2, P + P * c:2 * P + P * c],
                                            ye[64 * a:64 * a + 64, :], start=first, stop=last,
                                            skip_group_check=True)
                    ins.then_inc(sem("scat_done"), 1)

                def expert(e, s, turn, behind=2, first=False):
                    gate_up(e, s, turn)
                    if behind >= 1:
                        turns(e - 1, s - 1)
                    if behind >= 2:
                        scatter(e - 2, (s - 2) % RING, first, False)
                    if behind >= 1:
                        down(e - 1, (s - 1) % RING, turn if s else turn - 1)

                t0 = (NE // RING) * layer
                for s in range(RING):
                    expert(base + s, s, t0, behind=s, first=(s == 2))
                with pe.Fori(1, NE // RING) as i:
                    for s in range(RING):
                        expert(i * RING + (base + s), s, i + t0)
                last = base + NE - 1
                turns(last, RING - 1)
                scatter(last - 1, RING - 2, False, False)
                down(last, RING - 1, t0 + NE // RING - 1)
                scatter(last, RING - 1, False, True)

                pe.wait_ge(sem("moe_acc"), layer + 1)
                flag = pe.value_load(over_i[0:1, 0:1], min_val=0, max_val=1)
                with pe.If(flag > 0):
                    with pe.Fori(0, NE) as e:
                        pe.wait_ge(sem(f"over_landed{layer}"), e * 48 + 48)
                        for f in range(2):
                            pe.wait_ge(sem(f"over_hid{layer}"), e * 2 + (f + 1))
                            for a in range(2):
                                w = over_w(a).rearrange("p (k f) -> p k f", k=KT)
                                for k in range(KT):
                                    ins = pe.matmul(bank[4 + a][:, 0:T], w[:, k, f:FE:2], xT[:, k, :],
                                                    start=(k == 0), stop=(k == KT - 1))
                            ins.then_inc(sem(f"over_gu{layer}"), 1)
                        pe.wait_ge(sem(f"over_hid{layer}"), e * 2 + 3)
                        w = over_w(2).rearrange("p (j d) -> p j d", j=2)
                        for c in range(TT):
                            for a in range(2):
                                for f in range(2):
                                    ins = pe.matmul(bank[2 * c + a][:, :], over_g[:, f, P * c:P * c + P],
                                                    w[:, f, HALF * a:HALF * a + HALF], start=(f == 0), stop=(f == 1))
                        ins.then_inc(sem(f"over_down{layer}"), 1)

                n = 2 + 3 * layer
                norm_flip(n)
                pe.wait_ge(sem("p_landed"), 16 * (layer + 1))
                for j in range(2):
                    for c in range(TT):
                        ins = pe.transpose(bank[4][:, T * j + P * c:T * j + P * c + P], p_tok[:, c, P * j:P * j + P],
                                           ident[:, :])
                ins.then_inc(sem("p_flip"), 1)
                pe.wait_ge(sem("xT_ready"), 4 * (n + 1))
                for half in range(2):
                    wait_chunk(pe, f"pg{layer}.{half}")
                    for c in range(TT):
                        by_token(bank[2 * half + c][:, :], xT, chunk(f"pg{layer}.{half}"), c, sem("ple_gate_done"))
                wait_chunk(pe, f"pp{layer}")
                pe.wait_ge(sem("pT_ready"), layer + 1)
                w = wring[:, CHUNKS.index(f"pp{layer}") % WSLOTS, 0:2 * D].rearrange("p (j n) -> p j n", j=2)
                for half in range(2):
                    for c in range(TT):
                        by_token(bank[4 + 2 * half + c][:, :], pT, w[:, :, HALF * half:HALF * half + HALF], c,
                                 sem("ple_emb_done"), kts=2)

        @block.vector
        def _(dve):
            link = chain_of(dve, "dve_chain")

            def norm_sums(n):
                junk = xh[:, :, :, :].rearrange("p c k q -> p c (k q)")
                for c in range(TT):
                    ins = dve.tensor_tensor_reduce(junk[:, c, :], h[:, c, :], h[:, c, :], 1.0, 0.0, ALU.mult, ALU.add,
                                                   stat[:, c:c + 1])
                ins.then_inc(sem("norm_sums"), 1)

            def norm_apply(n):
                dve.wait_ge(sem("norm_rstd"), n + 1)
                dve.tensor_scalar(xh[:, 0], h[:, 0, :].rearrange("p (q k) -> p k q", k=KT), rstd[:, 0:1], None,
                                  ALU.mult).then_inc(sem("xh_dve"), 1)

            dve.memset(eps_t[:, 0:1], EPS * DH)
            dve.memset(eps_t[:, 1:2], EPS).then_inc(sem("eps_set"), 1)
            dve.wait_ge(sem("x_landed"), 16)
            norm_sums(0)
            norm_apply(0)
            dve.wait_ge(sem("blocks_set"), 1)
            dve.wait_ge(sem("iota_set"), 1)
            for n in range(len(LEVELS)):
                nxt = blk[:, n + 1, :] if n + 1 < len(LEVELS) else ones[:, :]
                link(dve.tensor_tensor(blk[:, n, :], blk[:, n, :], nxt, ALU.subtract))
            d = [decay[:, i, :] for i in range(10)]

            def pairs(t):
                return t.rearrange("p (c h) -> p c h", c=TT)
            dve.wait_ge(sem("ab_done"), 1)
            dve.wait_ge(sem("small_landed"), 16 * 16)
            ab = bank[5][:, 0:32].rearrange("p (c n) -> p c n", c=TT)
            link(dve.tensor_tensor(pairs(d[0]), ab[:, :, 0:NH], ab_row[:, 1:2, :].broadcast_to([P, TT, NH]), ALU.add))
            link(dve.tensor_copy(pairs(d[2]), ab[:, :, NH:]))
            link(dve.tensor_scalar(d[1], d[0], -1.0, None, ALU.mult))
            dve.tensor_tensor(d[1], d[1], d[0], ALU.max).then_inc(sem("ab_abs"), 1)
            dve.wait_ge(sem("ab_exp"), 1)
            link(dve.scalar_tensor_tensor(out=d[3], in0=d[0], scalar=0.0, in1=d[1], op0=ALU.max, op1=ALU.add))
            link(dve.tensor_tensor(pairs(d[3]), pairs(d[3]), d[4][:, 0:NH].unsqueeze(1).broadcast_to([P, TT, NH]),
                                   ALU.mult))
            dve.tensor_scalar(d[3], d[3], -1.0, None, ALU.mult).then_inc(sem("g_ready"), 1)
            link(dve.tensor_scalar(d[2], d[2], 1.0, None, ALU.add))
            link(dve.reciprocal(d[8], d[2]))
            dve.wait_ge(sem("cum_done"), 1)
            link(dve.tensor_copy(d[5], bank[6][:, 0:16]))
            dve.tensor_tensor(d[7], bank[6][:, 16:32], d[5], ALU.subtract).then_inc(sem("cum_ready"), 1)
            dve.wait_ge(sem("decay_exp"), 1)
            link(dve.tensor_scalar(d[9], d[6], -1.0, None, ALU.mult))
            G, eG, kdec, beta, neg_eG = d[5], d[6], d[7], d[8], d[9]
            dve.wait_ge(sem("conv_ready"), 1)

            for item in plan:
                if item[0] == "mm":
                    _, j, k = item
                    if k < KT - 1:
                        continue
                    ct = tile_of(j)[2]
                    dve.wait_ge(sem("proj_done"), j + 1)
                    if j >= 2:
                        dve.wait_ge(sem("silu_done"), j - 1)
                    src, dst = bank[j % 2][:, 0:T], cv[:, j % 2, :]
                    link(dve.tensor_scalar(dst, src, conv_w[:, 3, ct:ct + 1], None, ALU.mult))
                    for tap in (2, 1, 0):
                        lag = 3 - tap
                        ins = dve.scalar_tensor_tensor(out=dst[:, lag:], in0=src[:, 0:T - lag],
                                                       scalar=conv_w[:, tap, ct:ct + 1], in1=dst[:, lag:],
                                                       op0=ALU.mult, op1=ALU.add)
                        if tap:
                            link(ins)
                        else:
                            ins.then_inc(sem("conv_done"), 1)
                elif item[0] == "step":
                    _, pair, name, level = item
                    n = pair * 6 + level - 1
                    heads = (2 * pair, 2 * pair + 1)
                    cols = [NH * c + heads[i] for i in range(2) for c in range(TT)]
                    if name == "norm":
                        dve.wait_ge(sem("row_cum_done"), pair + 1)
                        for u in range(4):
                            ins = dve.tensor_scalar(Dm[:, u, :], bank[4][:, P * u:P * u + P], G[:, cols[u]:cols[u] + 1],
                                                    0.0, ALU.subtract, ALU.max)
                        ins.then_inc(sem("decay_diff"), 1)
                        dve.wait_ge(sem("norms_sqrt"), pair + 1)
                        link(dve.reciprocal(sq, sq))
                        for a in range(2):
                            view = qkvT[:, 8 * a + heads[0]:8 * a + heads[0] + 2, :]
                            ins = dve.tensor_tensor(view, view, sq[:, 512 * a:512 * a + 512].rearrange(
                                "p (u t) -> p u t", u=2), ALU.mult)
                        ins.then_inc(sem("qk_normed"), 1)
                        dve.wait_ge(sem("decay_mat"), pair + 1)
                        link(dve.tensor_tensor(Dm, Dm, lower[:, :].unsqueeze(1).broadcast_to([P, 4, P]), ALU.mult))
                    elif name == "gram":
                        dve.wait_ge(sem("gram_done"), pair + 1)
                        for u in range(4):
                            dve.scalar_tensor_tensor(out=Lm[:, u, :], in0=bank[5][:, P * u:P * u + P],
                                                     scalar=beta[:, cols[u]:cols[u] + 1], in1=Dm[:, u, :],
                                                     op0=ALU.mult, op1=ALU.mult)
                        dve.tensor_tensor(Am.rearrange("p u n -> p (u n)"), bank[6][:, :],
                                          Dm.rearrange("p u n -> p (u n)"), ALU.mult).then_inc(sem("gram_ready"), 1)
                        dve.wait_ge(sem("kv_flip_done"), pair + 1)
                        link(dve.tensor_copy(v_tok.rearrange("p u n -> p (u n)"), bank[7][:, :]))
                        for i in range(2):
                            link(dve.tensor_scalar(k_tok[:, i, :], bank[4][:, P * i:P * i + P],
                                                   kdec[:, cols[2 * i]:cols[2 * i] + 1], None, ALU.mult))
                    elif name == "flip":
                        dve.wait_ge(sem("flip_done"), pair + 1)
                        link(dve.tensor_copy(LTm.rearrange("p u n -> p (u n)"), bank[2][:, :]))
                        m1 = blk[:, 0:1, :].broadcast_to([P, 4, P])
                        idb = ident[:, :].unsqueeze(1).broadcast_to([P, 4, P])
                        link(dve.tensor_tensor(Tm, Lm, m1, ALU.mult))
                        link(dve.tensor_tensor(Zm, LTm, m1, ALU.mult))
                        link(dve.tensor_tensor(Tm, Tm, idb, ALU.add))
                        link(dve.tensor_tensor(Zm, Zm, idb, ALU.add))
                        dve.tensor_tensor(LMm, LTm, blk[:, 1:2, :].broadcast_to([P, 4, P]), ALU.mult
                                          ).then_inc(sem("level_ready"), 1)
                    elif name == "full":
                        dve.wait_ge(sem("full_done"), n + 1)
                        flat = "p u n -> p (u n)"
                        ins = dve.tensor_tensor(Zm.rearrange(flat), bank[6][:, :], Zm.rearrange(flat), ALU.add)
                        link(ins)
                        if level < 6:
                            link(dve.tensor_tensor(Tm.rearrange(flat), bank[5][:, :], Tm.rearrange(flat), ALU.add))
                            dve.tensor_tensor(LMm, LTm, blk[:, level + 1:level + 2, :].broadcast_to([P, 4, P]), ALU.mult
                                              ).then_inc(sem("level_ready"), 1)
                        else:
                            for i in range(2):
                                ins = dve.tensor_scalar(B_in[:, i, :], v_tok[:, 2 * i, :],
                                                        beta[:, cols[2 * i]:cols[2 * i] + 1], None, ALU.mult)
                            ins.then_inc(sem("inverse_ready"), 1)
                    elif name == "read":
                        dve.wait_ge(sem("read_done"), pair + 1)
                        for i in range(2):
                            u = 2 * i + 1
                            link(dve.scalar_tensor_tensor(out=B_in[:, i, :], in0=bank[5][:, P * i:P * i + P],
                                                          scalar=neg_eG[:, cols[u]:cols[u] + 1], in1=v_tok[:, u, :],
                                                          op0=ALU.mult, op1=ALU.add))
                        for i in range(2):
                            u = 2 * i + 1
                            ins = dve.tensor_scalar(B_in[:, i, :], B_in[:, i, :], beta[:, cols[u]:cols[u] + 1], None,
                                                    ALU.mult)
                        ins.then_inc(sem("B1_ready"), 1)
                    elif name == "new1":
                        dve.wait_ge(sem("new1_done"), pair + 1)
                        for i in range(2):
                            u = 2 * i + 1
                            link(dve.tensor_scalar(q_st[:, i, :], bank[6][:, P * i:P * i + P],
                                                   eG[:, cols[u]:cols[u] + 1], None, ALU.mult))
                    elif name == "out":
                        dve.wait_ge(sem("o_done"), pair + 1)
                        ob = bank[2][:, :].rearrange("p (i c n) -> p i c n", i=2, c=TT)
                        link(dve.tensor_copy(o_tok[:, 0, heads[0]:heads[0] + 2, :], ob[:, :, 0, :]))
                        link(dve.tensor_tensor(o_tok[:, 1, heads[0]:heads[0] + 2, :], ob[:, :, 1, :], q_st, ALU.add))
                        for i in range(2):
                            for c in range(TT):
                                ins = dve.tensor_tensor_reduce(Xm[:, 2 * i + c, :], o_tok[:, c, heads[i], :],
                                                               o_tok[:, c, heads[i], :], 1.0, 0.0, ALU.mult, ALU.add,
                                                               o_sum[:, NH * c + heads[i]:NH * c + heads[i] + 1])
                                if (i, c) != (1, 1):
                                    link(ins)
                        ins.then_inc(sem("o_sums"), 1)
            o_all = o_tok.rearrange("p c h n -> p (c h) n")
            dve.wait_ge(sem("o_rstd"), 1)
            link(dve.tensor_tensor(o_all, o_all, o_sum.unsqueeze(2).broadcast_to([P, 2 * NH, DH]), ALU.mult))
            link(dve.tensor_tensor(o_all, o_all, o_gain[:, :].unsqueeze(1).broadcast_to([P, 2 * NH, DH]), ALU.mult))
            dve.wait_ge(sem("z_ready"), 4)
            dve.tensor_tensor(o_tok.rearrange("p c h n -> p (c h n)"), o_tok.rearrange("p c h n -> p (c h n)"),
                              zs.rearrange("p c n -> p (c n)"), ALU.mult).then_inc(sem("o_gated"), 1)
            for j in range(4):
                half, c = divmod(j, 2)
                dve.wait_ge(sem("gdn_out_done"), j + 1)
                view = h[:, c, HALF * half:HALF * half + HALF]
                link(dve.tensor_tensor(view, bank[4 + j][:, :], view, ALU.add))

            for layer in range(2):
                if layer == 1:
                    norm_sums(3)
                    norm_apply(3)

                    def soft_sum(hd):
                        dve.wait_ge(sem("soft_log"), hd + 1)
                        if hd >= 2:
                            dve.wait_ge(sem("rev_done"), hd - 1)
                        s_ = soft[:, hd % 2, :]
                        link(dve.scalar_tensor_tensor(out=s_, in0=bank[hd % 3][:, 0:384], scalar=0.0,
                                                      in1=soft_u[:, hd % 2, :], op0=ALU.min, op1=ALU.subtract,
                                                      reverse1=True))
                        view = s_.rearrange("p (b n) -> p b n", n=P)[:, 0:3:2, :]
                        dve.tensor_tensor(view, view, below[:, :].unsqueeze(1).broadcast_to([P, 2, P]), ALU.mult
                                          ).then_inc(sem("soft_ready"), 1)

                    def out_pair(i):
                        dve.wait_ge(sem("pv_done"), 2 * i + 2)
                        dve.tensor_copy(xT[:, i, :], bank[3 + i % 2][:, 0:T]).then_inc(sem("sbo_ready"), 1)

                    for hd in range(QH + 3):
                        if hd < QH:
                            soft_sum(hd)
                        if hd >= 4 and hd % 2 == 0:
                            out_pair(hd // 2 - 2)
                    for j in range(4):
                        half, c = divmod(j, 2)
                        dve.wait_ge(sem("sb_out_done"), j + 1)
                        view = h[:, c, HALF * half:HALF * half + HALF]
                        b = bank[(5, 6, 7, 0)[j]]
                        link(dve.tensor_tensor(view, b[:, :], view, ALU.add))

                n = 1 + 3 * layer
                norm_sums(n)
                norm_apply(n)
                dve.wait_ge(sem("logits_done"), layer + 1)
                lg = bank[4][:, 0:72].rearrange("p (c e) -> p c e", c=TT)
                bias = b_rt[:, layer:layer + 1, :].broadcast_to([P, TT, NG + NE])
                grp, shift, gexp, eq4, hot4 = (rt[:, i, :, 0:NG] for i in (0, 1, 2, 3, 4))
                elog, masked, hot1, masked2, hot2, chosen, cand = (rt[:, i] for i in (5, 6, 7, 8, 10, 9, 11))
                sm = [rt[:, i, :, j:j + 1] for i in (12, 13) for j in range(4)]
                m1, m2, diff, ediff = (rt[:, 14, :, j:j + 1] for j in (0, 3, 1, 2))
                gmax, gsum, gp, c1, w1, w2, pos1, pos2 = sm
                link(dve.tensor_tensor(grp, lg[:, :, 0:NG], bias[:, :, 0:NG], ALU.add))
                link(dve.tensor_tensor(elog, lg[:, :, NG:], bias[:, :, NG:], ALU.add))
                link(dve.tensor_reduce(gmax, grp, AX_X, ALU.max))
                dve.tensor_tensor(shift, grp, gmax.broadcast_to([P, TT, NG]), ALU.subtract
                                  ).then_inc(sem("group_shift"), 1)

                def first_max(hot, vals, m, width):
                    cd = cand[:, :, 0:width]
                    link(dve.tensor_tensor(cd, vals, m.broadcast_to([P, TT, width]), ALU.is_equal))
                    link(dve.tensor_tensor(cd, cd, rev_idx[:, 0:width].unsqueeze(1).broadcast_to([P, TT, width]),
                                           ALU.mult))
                    link(dve.tensor_reduce(c1, cd, AX_X, ALU.max))
                    link(dve.tensor_tensor(hot, cd, c1.broadcast_to([P, TT, width]), ALU.is_equal))

                first_max(hot4, grp, gmax, NG)
                link(dve.tensor_scalar(eq4, hot4, -1.0, BIG, ALU.add, ALU.mult))
                link(dve.tensor_copy(masked.rearrange("p c (g e) -> p c g e", g=NG),
                                     hot4.unsqueeze(3).broadcast_to([P, TT, NG, EPG])))
                link(dve.tensor_tensor(masked, masked, elog, ALU.mult))
                link(dve.tensor_copy(cand.rearrange("p c (g e) -> p c g e", g=NG),
                                     eq4.unsqueeze(3).broadcast_to([P, TT, NG, EPG])))
                link(dve.tensor_tensor(masked, masked, cand, ALU.add))
                link(dve.tensor_reduce(m1, masked, AX_X, ALU.max))
                first_max(hot1, masked, m1, NE)
                link(dve.scalar_tensor_tensor(out=masked2, in0=hot1, scalar=-3 * BIG, in1=masked, op0=ALU.mult,
                                              op1=ALU.add))
                link(dve.tensor_reduce(m2, masked2, AX_X, ALU.max))
                first_max(hot2, masked2, m2, NE)
                dve.tensor_tensor(chosen, hot1, hot2, ALU.add).then_inc(sem("chosen"), 1)
                dve.tensor_tensor(diff, m2, m1, ALU.subtract).then_inc(sem("pair_diff"), 1)
                dve.wait_ge(sem("group_exp"), layer + 1)
                link(dve.tensor_reduce(gsum, gexp, AX_X, ALU.add))
                link(dve.reciprocal(gp, gsum))
                dve.wait_ge(sem("pair_exp"), layer + 1)
                link(dve.tensor_scalar(w2, ediff, 1.0, None, ALU.add))
                link(dve.reciprocal(w1, w2))
                link(dve.tensor_tensor(w1, w1, gp, ALU.mult))
                link(dve.tensor_tensor(w2, w1, ediff, ALU.mult))
                link(dve.tensor_tensor(cw[:, :, :], hot1, w1.broadcast_to([P, TT, NE]), ALU.mult))
                link(dve.tensor_tensor(cand, hot2, w2.broadcast_to([P, TT, NE]), ALU.mult))
                link(dve.tensor_tensor(cw_over[:, :, :], cw[:, :, :], cand, ALU.add))
                dve.wait_ge(sem("counts_done"), layer + 1)
                link(dve.tensor_copy(rank[:, :, :].rearrange("p c e -> p (c e)"), bank[5][:, 0:64]))
                link(dve.tensor_reduce(m1[:, 0, :], bank[5][:, 64:96], AX_X, ALU.max))
                link(dve.tensor_scalar(over_i[:, :], m1[:, 0, :], float(CAP), None, ALU.is_gt))
                link(dve.tensor_scalar(cand, rank[:, :, :], float(CAP), None, ALU.is_lt))
                link(dve.tensor_tensor(cw[:, :, :], cw_over[:, :, :], cand, ALU.mult))
                link(dve.tensor_tensor(cw_over[:, :, :], cw_over[:, :, :], cw[:, :, :], ALU.subtract))
                dve.wait_ge(sem("offsets_done"), layer + 1)
                off = masked[:, 0, :]
                link(dve.tensor_copy(off, bank[7][:, 0:NE]))
                link(dve.tensor_copy(off_i[:, :], off))
                link(dve.tensor_tensor(cand, rank[:, :, :], off.unsqueeze(1).broadcast_to([P, TT, NE]), ALU.add))
                link(dve.tensor_tensor(hot1, hot1, cand, ALU.mult))
                link(dve.tensor_tensor(hot2, hot2, cand, ALU.mult))
                link(dve.tensor_reduce(pos1, hot1, AX_X, ALU.add))
                dve.tensor_reduce(pos2, hot2, AX_X, ALU.add).then_inc(sem("routed"), 1)
                dve.wait_ge(sem("routed"), layer + 1)
                for c in range(TT):
                    link(dve.tensor_scalar(one_hot[:, c, :], iota[:, :], pos1[:, c, :], None, ALU.is_equal))
                    ins = dve.scalar_tensor_tensor(out=one_hot[:, c, :], in0=iota[:, :], scalar=pos2[:, c, :],
                                                   in1=one_hot[:, c, :], op0=ALU.is_equal, op1=ALU.add)
                    if c == 0:
                        link(ins)
                ins.then_inc(sem("one_hot_ready"), 1)
                for k in range(1, KT, 2):
                    dve.wait_ge(sem("gather_done"), KT * layer + k + 1)
                    dve.tensor_scalar(xs[:, k, 0:SLOTS], bank[k % 4][:, :], gains[:, n, k:k + 1], None, ALU.mult
                                      ).then_inc(sem("xs_dve"), 1)
                base = NE * layer

                def scatter_mat(e, i, wait):
                    if wait is not None:
                        dve.wait_ge(sem("tr_done"), wait)
                    for c in range(TT):
                        ins = dve.tensor_scalar(rw[:, c, :].rearrange("p (a s) -> p a s", a=2),
                                                iota[:, 0:CAP].unsqueeze(1).broadcast_to([P, 2, CAP]),
                                                rank[:, c, bass.ds(i, 1)], cw[:, c, bass.ds(i, 1)],
                                                ALU.is_equal, ALU.mult)
                    ins.then_inc(sem("rw_ready"), 1)

                def hidden(e, s, wait):
                    dve.wait_ge(sem("sg_ready"), e + 1)
                    if wait:
                        dve.wait_ge(sem("tr_done"), e)
                    dve.tensor_tensor(hh[64:128, :], bank[4 + s % 2][64:128, 0:FE], sg[64:128, :], ALU.mult
                                      ).then_inc(sem("hh_ready"), 1)

                def rows_out(e, s, wait):
                    dve.wait_ge(sem("down_done"), e + 1)
                    if wait:
                        dve.wait_ge(sem("scat_done"), e)
                    dve.tensor_copy(ye, bank[7][:, :]).then_inc(sem("ye_ready"), 1)

                for s in range(RING):
                    e = base + s
                    scatter_mat(e, s, e if e >= 1 else None)
                    hidden(e, s, e >= 1)
                    if s >= 1:
                        rows_out(e - 1, s - 1, e - 1 >= 1)
                with dve.Fori(1, NE // RING) as i:
                    for s in range(RING):
                        e = i * RING + (base + s)
                        scatter_mat(e, i * RING + s, e)
                        hidden(e, s, True)
                        rows_out(e - 1, s - 1, True)
                rows_out(base + NE - 1, RING - 1, True)
                dve.wait_ge(sem("scat_done"), base + NE)
                for j in range(4):
                    c, a = divmod(j, 2)
                    view = h[:, c, HALF * a:HALF * a + HALF]
                    ins = dve.tensor_tensor(view, bank[j][:, :], view, ALU.add)
                    if j < 3:
                        link(ins)
                ins.then_inc(sem("moe_acc"), 1)
                dve.wait_ge(sem("moe_acc"), layer + 1)

                flag = dve.value_load(over_i[0:1, 0:1], min_val=0, max_val=1)
                with dve.If(flag > 0):
                    done = sem(f"over_step{layer}")
                    dve.tensor_copy(over_col[:, 0:1], cw_over[:, 0, 0:1]).then_inc(sem(f"over_free{layer}"), 1)
                    dve.tensor_copy(over_col[:, 1:2], cw_over[:, 1, 0:1]).then_inc(sem(f"over_hid{layer}"), 1)
                    with dve.Fori(0, NE) as e:
                        dve.wait_ge(sem(f"over_free{layer}"), e + 1)
                        for f in range(2):
                            dve.wait_ge(sem(f"over_silu{layer}"), e * 2 + (f + 1))
                            dve.tensor_tensor(over_g[:, f, :], bank[5][:, 0:T], over_g[:, f, :], ALU.mult
                                              ).then_inc(sem(f"over_hid{layer}"), 1)
                        for c in range(TT):
                            dve.tensor_copy(over_col[:, c:c + 1], cw_over[:, c, bass.ds(e, 1)]).then_inc(done, 1)
                        dve.wait_ge(sem(f"over_down{layer}"), e + 1)
                        for j in range(4):
                            c, a = divmod(j, 2)
                            view = h[:, c, HALF * a:HALF * a + HALF]
                            dve.wait_ge(done, e * 5 + (j + 2))
                            ins = dve.scalar_tensor_tensor(out=view, in0=bank[j][:, :], scalar=over_col[:, c:c + 1],
                                                           in1=view, op0=ALU.mult, op1=ALU.add)
                            if j < 3:
                                ins.then_inc(done, 1)
                        ins.then_inc(sem(f"over_free{layer}"), 1)
                    dve.wait_ge(sem(f"over_free{layer}"), NE + 1)

                n = 2 + 3 * layer
                norm_sums(n)
                norm_apply(n)
                for j in range(4):
                    half, c = divmod(j, 2)
                    dve.wait_ge(sem("gate_ready"), 4 * layer + j + 1)
                    dve.wait_ge(sem("ple_emb_done"), 4 * layer + j + 1)
                    link(dve.tensor_tensor(gate[:, j, :], bank[4 + j][:, :], gate[:, j, :], ALU.mult))
                    view = h[:, c, HALF * half:HALF * half + HALF]
                    dve.tensor_tensor(view, view, gate[:, j, :], ALU.add).then_inc(sem("ple_h"), 1)
                dve.wait_ge(sem("ple_h"), 4 * layer + 4)
            norm_sums(6)
            dve.wait_ge(sem("norm_rstd"), 7)
            dve.wait_ge(sem("fin_gain_landed"), 16)
            for c in range(TT):
                dve.scalar_tensor_tensor(out=fin_out[:, c, :], in0=h[:, c, :], scalar=rstd[:, c:c + 1], in1=fin_gain,
                                         op0=ALU.mult, op1=ALU.mult).then_inc(sem("fin_ready"), 1)


_INS = ["x", "p", "attn_norm", "moe_norm", "ple_norm", "gdn_w_in", "gdn_conv", "gdn_a_log", "gdn_dt_bias",
        "gdn_o_norm", "gdn_w_out", "kv_norm", "w_kv", "sb_w_q", "sb_w_out", "moe_w_group", "moe_b_group",
        "moe_w_expert", "moe_b_expert", "moe_w_gate", "moe_w_up", "moe_w_down", "ple_w_gate", "ple_w_proj",
        "final_norm"]
_OUTS = [((1, T, D), "float32")]


def kernel(**inputs):
    import numpy as _np
    import concourse.bacc as _bacc
    from concourse import mybir as _mybir
    from concourse.bass_utils import run_bass_kernel_spmd as _run

    nc = _bacc.Bacc("TRN2", target_bir_lowering=False, num_devices=1)
    arrays, args = {}, []
    for name in _INS:
        a = _np.ascontiguousarray(inputs[name])
        arrays[f"in_{name}_dram"] = a
        args.append(nc.dram_tensor(f"in_{name}_dram", a.shape, _mybir.dt.from_np(a.dtype), kind="ExternalInput").ap())
    for i, (shape, dtype) in enumerate(_OUTS):
        dt = _mybir.dt.from_np(_np.dtype(dtype))
        args.append(nc.dram_tensor(f"out_{i}_dram", shape, dt, kind="ExternalOutput").ap())
    yoco_kernel(nc, *args)
    r = _run(nc, [arrays], core_ids=[0])
    got = tuple(r.results[0][f"out_{i}_dram"] for i in range(len(_OUTS)))
    return got[0]
```

```python
from contextlib import ExitStack

import concourse.bass as bass
from concourse import mybir
from concourse.alu_op_type import AluOpType as ALU

ACT = mybir.ActivationFunctionType
F32 = mybir.dt.float32
I32 = mybir.dt.int32
AX_X = mybir.AxisListType.X

P = 128
T = 256
TT = T // P
D = 1024
KT = D // P
HALF = 512
NH, DH = 8, 128
CONV = 4
QH, KVH, SD = 16, 4, 64
NG, NE, FE = 4, 32, 256
EPG = NE // NG
CAP = 64
SLOTS = 2 * T
SPAD = SLOTS + CAP
RING = 4
PLE = 256
EPS = 1e-6
BIG = 1e30
LEVELS = [1 << n for n in range(7)]

CHUNKS = ["qk0", "v0", "qk1", "qk2", "v1", "qk3", "z0", "z1", "go0", "go1",
          "pg0.0", "pg0.1", "pp0", "kv", "sq0", "sq1", "so0", "so1", "pg1.0", "pg1.1", "pp1"]
WSLOTS = 3

NORMS = ["attn0", "moe0", "ple0", "attn1", "moe1", "ple1"]


def gdn_plan():
    tiles = 3 * NH + 4
    stream = [("mm", j, k) for j in range(tiles) for k in range(KT)]
    plan, sent = [], 0

    def fill(n):
        nonlocal sent
        plan.extend(stream[sent:sent + n])
        sent = min(sent + n, len(stream))

    def fill_to(j):
        fill(max(0, j * KT - sent))

    pairs = NH // 2
    fill(12)
    plan.append(("cum", 0, 0))
    fill_to(6)
    plan.append(("silu", 0, 0))
    fill(8)
    plan.append(("norm", 0, 0))
    fill(12)
    plan.append(("gram", 0, 0))
    fill(4)
    plan.append(("flip", 0, 0))
    fill(4)
    for pair in range(pairs):
        for level in range(1, len(LEVELS)):
            plan.append(("half", pair, level))
            fill(2)
            plan.append(("full", pair, level))
            fill(2)
            if level == 5 and pair + 1 < pairs:
                fill_to(6 * (pair + 2))
                plan.append(("silu", pair + 1, 0))
                fill(4)
            if level == 5 and pair + 1 == pairs:
                fill_to(tiles)
                plan.append(("silu_z", 0, 0))
        plan.append(("new0", pair, 0))
        if pair + 1 < pairs:
            plan.append(("norm", pair + 1, 0))
        for name in ("state", "read", "new1", "out"):
            fill(2)
            plan.append((name, pair, 0))
            if pair + 1 == pairs and name != "out":
                plan.append(("turn", ("state", "read", "new1").index(name), 0))
        if pair + 1 < pairs:
            fill(3)
            plan.append(("gram", pair + 1, 0))
            fill(4)
            plan.append(("flip", pair + 1, 0))
            fill(4)
    plan.append(("turn", pairs - 1, 0))
    return plan


def tile_of(j):
    pair, i = divmod(j, 6)
    kind, head = divmod(i, 2)
    if kind < 2:
        return f"qk{pair}", 256 * kind + 128 * head, 8 * kind + 2 * pair + head
    return f"v{pair // 2}", 256 * (pair % 2) + 128 * head, 16 + 2 * pair + head


def yoco_kernel(nc, x, p, attn_norm, moe_norm, ple_norm, gdn_w_in, gdn_conv, gdn_a_log, gdn_dt_bias,
                gdn_o_norm, gdn_w_out, kv_norm, w_kv, sb_w_q, sb_w_out, moe_w_group, moe_b_group,
                moe_w_expert, moe_b_expert, moe_w_gate, moe_w_up, moe_w_down, ple_w_gate, ple_w_proj,
                final_norm, out):
    ctx = ExitStack()
    with ctx:
        def sb(name, shape, dt=F32):
            return ctx.enter_context(nc.sbuf_tensor(name, shape, dt))

        sems = {}

        def sem(name):
            if name not in sems:
                sems[name] = ctx.enter_context(nc.semaphore(name))
            return sems[name]

        bank = [ctx.enter_context(nc.psum_tensor(f"bank{i}", [P, HALF], F32)) for i in range(8)]

        moe_w = sb("moe_w", [P, RING, 3, KT * FE])
        wring = sb("wring", [P, WSLOTS, KT * HALF])
        h = sb("h", [P, TT, D])
        xh = sb("xh", [P, TT, KT, P])
        xT = sb("xT", [P, KT, T])
        region = sb("region", [P, KT * SPAD])
        scr = sb("scr", [P, 3072])
        ident = sb("ident", [P, P])
        upper = sb("upper", [P, P])
        below = sb("below", [P, P])
        lower = sb("lower", [P, P])
        ones = sb("ones", [P, P])
        iota = sb("iota", [P, SLOTS])
        rev_idx = sb("rev_idx", [P, NE])
        gains = sb("gains", [P, 7, KT])
        w_ab = sb("w_ab", [P, KT, 2 * NH])
        w_rt = sb("w_rt", [P, KT, NG + NE])
        b_rt = sb("b_rt", [P, 2, NG + NE])
        ab_row = sb("ab_row", [P, 2, NH])
        o_gain = sb("o_gain", [P, DH])
        half_neg = sb("half_neg", [P, 2 * NH])
        stat = sb("stat", [P, 2])
        rstd = sb("rstd", [P, 2])
        decay = sb("decay", [P, 10, 2 * NH])
        rank = sb("rank", [P, TT, NE])
        cw = sb("cw", [P, TT, NE])
        cw_over = sb("cw_over", [P, TT, NE])
        off_i = sb("off_i", [P, NE], I32)
        over_i = sb("over_i", [P, 1], I32)
        over_col = sb("over_col", [P, TT])
        eps_t = sb("eps_t", [P, 2])

        slot2 = moe_w[:, 2, :, :].rearrange("p a n -> p (a n)")
        slot3 = moe_w[:, 3, :, :].rearrange("p a n -> p (a n)")
        qkvT = slot3.rearrange("p (n t) -> p n t", t=T)
        zs = slot2[:, 0:2048].rearrange("p (c n) -> p c n", c=TT)
        o_tok = slot2[:, 2048:4096].rearrange("p (c h n) -> p c h n", c=TT, h=NH)
        sq = slot2[:, 4096:5120]
        blk = slot2[:, 5120:5120 + 7 * P].rearrange("p (n q) -> p n q", q=P)
        mats = region[:, 0:9 * 512].rearrange("p (m n q) -> p m n q", m=9, n=4)
        Lm, Am, LTm, ATm, Tm, Zm, Xm, Dm, LMm = (mats[:, i] for i in range(9))
        v_tok = scr[:, 0:512].rearrange("p (u n) -> p u n", u=4)
        k_tok = scr[:, 512:768].rearrange("p (u n) -> p u n", u=2)
        S_st = scr[:, 768:1024].rearrange("p (u n) -> p u n", u=2)
        B_in = scr[:, 1024:1280].rearrange("p (u n) -> p u n", u=2)
        v_new = scr[:, 1280:1792].rearrange("p (u n) -> p u n", u=4)
        q_st = scr[:, 1792:2048].rearrange("p (u n) -> p u n", u=2)
        conv_rows = scr[0:CONV * 24, 2560:2688]
        conv_w = scr[:, 2688:2784].rearrange("p (t n) -> p t n", t=CONV)
        o_sum = scr[:, 2784:2800].rearrange("p (n c i) -> p n c i", c=TT, i=2)
        xs = region[:, :].rearrange("p (k s) -> p k s", k=KT)
        xe = scr[:, 0:1024].rearrange("p (b k s) -> p b k s", b=2, k=KT)
        rw = scr[:, 1024:1280].rearrange("p (c s) -> p c s", c=TT)
        sg = scr[:, 1280:1792].rearrange("p (b f) -> p b f", b=2)
        hh = scr[:, 1792:2304].rearrange("p (b f) -> p b f", b=2)
        xh_flat = xh[:, :, :, :].rearrange("p c k q -> p (c k q)")
        ye = xh_flat[:, 0:1024].rearrange("p (a n) -> p a n", a=2)
        hr = xh_flat[:, 1024:2048].rearrange("p (b n) -> p b n", b=2)
        one_hot = scr[:, 0:1024].rearrange("p (c s) -> p c s", c=TT)
        rt = scr[:, 1024:3072].rearrange("p (n c e) -> p n c e", c=TT, e=NE)
        xkvT = region[:, 0:2048].rearrange("p (k t) -> p k t", k=KT)
        qT = region[:, 2048:4096].rearrange("p (k t) -> p k t", k=KT)
        kT = scr[:, 0:1024].rearrange("p (g t) -> p g t", g=KVH)
        v_sb = scr[:, 1024:1536].rearrange("p (c n) -> p c n", c=TT)
        soft = xkvT.rearrange("p k t -> p (k t)")[:, 0:768].rearrange("p (b n) -> p b n", b=2)
        soft_u = xkvT.rearrange("p k t -> p (k t)")[:, 768:1536].rearrange("p (b n) -> p b n", b=2)
        attn = scr[:, 1536:2304].rearrange("p (b n) -> p b n", b=2)
        p_tok = scr[:, 2304:2816].rearrange("p (c n) -> p c n", c=TT)
        pT = scr[:, 0:512].rearrange("p (j t) -> p j t", j=2)
        gate = scr[:, 1024:3072].rearrange("p (n q) -> p n q", n=4)
        fin_gain = region[:, 0:D]
        fin_out = region[:, D:3 * D].rearrange("p (c n) -> p c n", c=TT)

        def dchunk(name):
            at = CHUNKS.index(name) % WSLOTS
            slot = wring[:, at, :]
            wide = slot.rearrange("p (k n) -> p k n", k=KT)

            def by_row(w):
                return w.rearrange("(p k) n -> p k n", k=KT)

            def by_tile(w):
                return w.rearrange("(k p) n -> p k n", p=P)
            if name[:2] == "qk":
                n = int(name[2])
                w = by_row(gdn_w_in[0])
                return [(wide[:, :, 256 * a:256 * a + 256], w[:, :, D * a + 256 * n:D * a + 256 * n + 256])
                        for a in range(2)]
            half = int(name[-1])
            cols = slice(HALF * half, HALF * half + HALF)
            if name[0] == "v":
                return [(wide, by_row(gdn_w_in[0])[:, :, 2 * D + HALF * half:2 * D + HALF * half + HALF])]
            if name[0] == "z":
                return [(wide, by_row(gdn_w_in[0])[:, :, 3 * D + HALF * half:3 * D + HALF * half + HALF])]
            if name[:2] == "go":
                return [(wide, by_tile(gdn_w_out[0])[:, :, cols])]
            if name[:2] == "pg":
                return [(wide, by_row(ple_w_gate[int(name[2])])[:, :, cols])]
            if name[:2] == "pp":
                return [(slot[:, 0:2 * D].rearrange("p (j n) -> p j n", j=2),
                         ple_w_proj[half].rearrange("(j p) n -> p j n", p=P))]
            if name[:2] == "sq":
                return [(wide, by_row(sb_w_q[0])[:, :, cols])]
            if name[:2] == "so":
                return [(wide, by_tile(sb_w_out[0])[:, :, cols])]
            raise ValueError(name)

        def chunk_parts(name):
            if name == "kv":
                slot = wring[:, CHUNKS.index(name) % WSLOTS, :]
                return [(slot.rearrange("p (k n) -> p k n", k=KT), w_kv.rearrange("(p k) n -> p k n", k=KT))]
            return dchunk(name)

        def chunk(name):
            return wring[:, CHUNKS.index(name) % WSLOTS, :].rearrange("p (k n) -> p k n", k=KT)

        landed, slot_count = {}, [0] * WSLOTS
        for n, name in enumerate(CHUNKS):
            slot_count[n % WSLOTS] += 16 * len(chunk_parts(name))
            landed[name] = slot_count[n % WSLOTS]

        def wait_chunk(eng, name):
            eng.wait_ge(sem(f"chunk_landed{CHUNKS.index(name) % WSLOTS}"), landed[name])

        def chunk_used(name):
            if name[:2] == "qk":
                return sem("proj_done"), 6 * int(name[2]) + 4
            if name[0] == "v":
                return sem("proj_done"), 12 * int(name[1]) + 12
            if name[0] == "z":
                return sem("proj_done"), 3 * NH + 2 * int(name[1]) + 2
            if name[:2] == "go":
                return sem("gdn_out_done"), 4
            if name[:2] == "pg":
                return sem("ple_gate_done"), 4 * int(name[2]) + 2 * int(name[4]) + 2
            if name[:2] == "pp":
                return sem("ple_emb_done"), 4 * int(name[2]) + 4
            if name == "kv":
                return sem("kv_done"), 4
            if name[:2] == "sq":
                return sem("sbq_done"), 4 * int(name[2]) + 4
            return sem("sb_out_done"), 2 * int(name[2]) + 2

        def chain_of(eng, name):
            count = [0]

            def link(ins):
                count[0] += 1
                ins.then_inc(sem(name), 1)
                eng.wait_ge(sem(name), count[0])
            return link

        def over_w(n):
            return (region[:, 0:2048], region[:, 2048:4096], xh_flat)[n]

        over_g = scr[:, 512:1024].rearrange("p (f t) -> p f t", f=2)

        plan = gdn_plan()
        block = ctx.enter_context(nc.Block())

        @block.sync
        def _(sp):
            def load_chunk(n):
                name = CHUNKS[n]
                if n >= WSLOTS:
                    sp.wait_ge(*chunk_used(CHUNKS[n - WSLOTS]))
                for dst, src in chunk_parts(name):
                    sp.dma_start(dst, src).then_inc(sem(f"chunk_landed{n % WSLOTS}"), 16)

            def load_expert(layer, e, slot, which=range(3)):
                for n in which:
                    w = (moe_w_gate, moe_w_up, moe_w_down)[n]
                    flat = w[layer].rearrange("g e a b -> (g e) (a b)").rearrange("e (p n) -> e p n", p=P)
                    src = flat[e, :, :] if isinstance(e, int) else flat[bass.ds(e, 1), :, :].rearrange(
                        "e p n -> (e p) n")
                    name = "expert_gu" if n < 2 else "expert_d"
                    sp.dma_start(moe_w[:, slot, n, :], src).then_inc(sem(f"{name}{slot}"), 16)

            def load_gu(layer, e, slot, used):
                sp.wait_ge(sem("gu_done"), used)
                load_expert(layer, e, slot, (0, 1))

            def load_d(layer, e, b, used):
                sp.wait_ge(sem("down_done"), used)
                for x in range(2):
                    load_expert(layer, e + x, 2 * b + x, (2,))

            def load_experts(layer):
                with sp.Fori(1, NE // RING) as i:
                    for b in range(2):
                        for x in range(2):
                            s = 2 * b + x
                            load_gu(layer, i * RING + s, s, i * RING + (NE * layer - RING + s + 1))
                        load_d(layer, i * RING + (2 * b - 2), 1 - b, i * RING + (NE * layer - RING + 2 * b))
                load_d(layer, NE - 2, 1, NE * layer + NE - 4)

            sp.dma_start(h[:, :, :], x[0].rearrange("(c p) d -> p c d", p=P)).then_inc(sem("x_landed"), 16)
            first, small = sem("first_landed"), sem("small_landed")

            def load_gain(i, g):
                sp.dma_start(gains[:, i, :], g.rearrange("(p k) -> p k", k=KT)).then_inc(small if i else first, 16)

            load_gain(0, attn_norm[0])
            sp.dma_start(conv_rows, gdn_conv[0].rearrange("t (n c) -> (t n) c", c=P)).then_inc(first, 16)
            sp.dma_start(w_ab[:, :, :], gdn_w_in[0].rearrange("(p k) n -> p k n", k=KT)[:, :, 4 * D:4 * D + 16]
                         ).then_inc(first, 16)
            for i, row in enumerate((gdn_a_log, gdn_dt_bias)):
                sp.dma_start(ab_row[:, i, :], row.broadcast_to([P, NH])).then_inc(first, 16)
            load_chunk(0)
            load_chunk(1)
            load_chunk(2)
            for i, g in enumerate((moe_norm[0], ple_norm[0], attn_norm[1], moe_norm[1], ple_norm[1], kv_norm)):
                load_gain(i + 1, g)
            sp.dma_start(o_gain[:, :], gdn_o_norm.broadcast_to([P, DH])).then_inc(small, 16)
            for i in range(2):
                sp.dma_start(b_rt[:, i, 0:NG], moe_b_group[i:i + 1, :].broadcast_to([P, NG])).then_inc(small, 16)
                sp.dma_start(b_rt[:, i, NG:], moe_b_expert[i:i + 1, :].broadcast_to([P, NE])).then_inc(small, 16)

            def load_router(layer):
                rtr = sem("router_landed")
                sp.dma_start(w_rt[:, :, 0:NG], moe_w_group[layer].rearrange("(p k) n -> p k n", k=KT)
                             ).then_inc(rtr, 16)
                sp.dma_start(w_rt[:, :, NG:], moe_w_expert[layer].rearrange("(p k) n -> p k n", k=KT)
                             ).then_inc(rtr, 16)

            def load_p(layer):
                sp.dma_start(p_tok, p[layer, 0].rearrange("(c p) d -> p c d", p=P)).then_inc(sem("p_landed"), 16)

            load_router(0)
            load_expert(0, 0, 0)
            load_expert(0, 1, 1)
            for n in range(WSLOTS, CHUNKS.index("go1") + 1):
                load_chunk(n)
            sp.wait_ge(sem("oT_flip_done"), 4)
            load_p(0)
            load_expert(0, 2, 2, (0, 1))
            load_expert(0, 3, 3, (0, 1))
            for n in range(CHUNKS.index("pg0.0"), CHUNKS.index("pp0") + 1):
                load_chunk(n)
            load_experts(0)
            for layer in range(2):
                if layer == 1:
                    load_p(1)
                    load_experts(1)
                sp.wait_ge(sem("routed"), layer + 1)
                flag = sp.value_load(over_i[0:1, 0:1], min_val=0, max_val=1)
                with sp.If(flag > 0):
                    with sp.Fori(0, NE) as e:
                        sp.wait_ge(sem(f"over_free{layer}"), e + 1)
                        for n, w in enumerate((moe_w_gate, moe_w_up, moe_w_down)):
                            flat = w[layer].rearrange("g e a b -> (g e) (a b)").rearrange("e (p n) -> e p n", p=P)
                            sp.dma_start(over_w(n), flat[bass.ds(e, 1), :, :].rearrange("e p n -> (e p) n")
                                         ).then_inc(sem(f"over_landed{layer}"), 16)
                if layer == 0:
                    load_router(1)
                    for s in range(RING):
                        load_gu(1, s, s, NE - RING + s + 1)
                    load_d(1, 0, 0, NE - 2)
                    for n in range(CHUNKS.index("kv"), len(CHUNKS)):
                        load_chunk(n)
            sp.wait_ge(sem("ple_h"), 8)
            sp.dma_start(fin_gain, final_norm.rearrange("(a n) -> a n", a=1).broadcast_to([P, D])
                         ).then_inc(sem("fin_gain_landed"), 16)
            for c in range(TT):
                sp.wait_ge(sem("fin_ready"), c + 1)
                sp.dma_start(out[0].rearrange("(c p) d -> p c d", p=P)[:, c, :], fin_out[:, c, :]
                             ).then_inc(sem("out_stored"), 16)
            sp.wait_ge(sem("out_stored"), 32)

        @block.gpsimd
        def _(pool):
            link = chain_of(pool, "pool_chain")
            for t in (ident, upper, below, lower):
                pool.memset(t[:, :], 0.0 if t is ident else 1.0).then_inc(sem("mask_set"), 1)
            pool.memset(half_neg[:, :], -0.5).then_inc(sem("const_set"), 1)
            pool.memset(ones[:, :], 1.0).then_inc(sem("const_set"), 1)
            pool.wait_ge(sem("mask_set"), 4)
            pool.affine_select(out=ident[:, :], in_=ident[:, :], compare_op=ALU.not_equal, fill=1.0, base=0,
                               pattern=[[-1, P]], channel_multiplier=1).then_inc(sem("const_set"), 1)
            pool.affine_select(out=upper[:, :], in_=upper[:, :], compare_op=ALU.is_ge, fill=0.0, base=0,
                               pattern=[[1, P]], channel_multiplier=-1).then_inc(sem("const_set"), 1)
            pool.affine_select(out=below[:, :], in_=below[:, :], compare_op=ALU.is_gt, fill=0.0, base=0,
                               pattern=[[1, P]], channel_multiplier=-1).then_inc(sem("const_set"), 1)
            pool.affine_select(out=lower[:, :], in_=lower[:, :], compare_op=ALU.is_ge, fill=0.0, base=0,
                               pattern=[[-1, P]], channel_multiplier=1).then_inc(sem("const_set"), 1)

            def rsqrt(dst, src, scale, n, ready):
                link(pool.tensor_scalar(dst, src, scale, EPS, ALU.mult, ALU.add))
                pool.tensor_tensor(dst, dst, half_neg[:, 0:n], ALU.pow).then_inc(ready, 1)

            def norm_scale(n):
                pool.wait_ge(sem("sums0"), n + 1)
                pool.wait_ge(sem("sums1"), n + 1)
                rsqrt(rstd[:, :], stat[:, :], 1.0 / D, 2, sem("norm_rstd"))

            pool.wait_ge(sem("const_set"), 6)
            norm_scale(0)
            for n in range(len(LEVELS)):
                b = LEVELS[n]
                view = blk[:, n, :].rearrange("p (m b) -> p m b", b=b)
                link(pool.memset(blk[:, n, :], 1.0))
                link(pool.affine_select(out=view, in_=view, compare_op=ALU.is_ge, fill=0.0, base=0,
                                        pattern=[[-b, P // b], [0, b]], channel_multiplier=1))
                ins = pool.affine_select(out=view, in_=view, compare_op=ALU.is_ge, fill=0.0, base=b - 1,
                                         pattern=[[b, P // b], [0, b]], channel_multiplier=-1)
                if n < len(LEVELS) - 1:
                    link(ins)
                else:
                    ins.then_inc(sem("blocks_set"), 1)
            iota_i = region[:, 0:SLOTS].bitcast(I32)
            link(pool.iota(iota_i, [[1, SLOTS]], base=0, channel_multiplier=0))
            link(pool.tensor_copy(iota[:, :], iota_i))
            pool.tensor_scalar(rev_idx[:, :], iota[:, 0:NE], -1.0, float(NE), ALU.mult, ALU.add
                               ).then_inc(sem("iota_set"), 1)
            for pair in range(NH // 2):
                pool.wait_ge(sem("o_sums"), pair + 1)
                cols = o_sum[:, pair, :, :].rearrange("p c i -> p (c i)")
                rsqrt(cols, cols, 1.0 / DH, 4, sem("o_rstd"))

            for layer in range(2):
                if layer == 1:
                    norm_scale(3)
                    for hd in range(QH):
                        pool.wait_ge(sem("attn_exp"), hd + 1)
                        view = attn[:, hd % 2, :].rearrange("p (b n) -> p b n", n=P)[:, 0:3:2, :]
                        pool.tensor_tensor(view, view, below[:, :].unsqueeze(1).broadcast_to([P, 2, P]), ALU.mult
                                           ).then_inc(sem("attn_ready"), 1)
                norm_scale(1 + 3 * layer)
                pool.wait_ge(sem("norm_rstd"), 2 + 3 * layer)
                pool.memset(xs[:, :, SLOTS:], 0.0).then_inc(sem("pad_set"), 1)
                pool.wait_ge(sem("pad_set"), layer + 1)
                pool.wait_ge(sem("xs_act"), 4 * layer + 4)
                pool.wait_ge(sem("xs_dve"), 4 * layer + 4)
                pool.wait_ge(sem("routed"), layer + 1)

                def window(e, buf, base):
                    at = pool.value_load(off_i[0:1, bass.ds(e, 1)], min_val=0, max_val=SLOTS)
                    if base is not None:
                        pool.wait_ge(sem("gu_done"), base)
                    pool.tensor_copy(xe[:, buf, :, :], xs[:, :, bass.ds(at, CAP)]).then_inc(sem("xe_ready"), 1)

                for e in range(RING):
                    window(e, e % 2, NE * layer + e - 1 if e >= 2 else None)
                with pool.Fori(1, NE // RING) as i:
                    for s in range(RING):
                        window(i * RING + s, s % 2, i * RING + (NE * layer + s - 1))
                norm_scale(2 + 3 * layer)
            norm_scale(6)

        @block.scalar
        def _(act):
            link = chain_of(act, "act_chain")

            exp_ln = "natural_log_exp_and_others"

            def norm_sum(n):
                if n == 3:
                    act.wait_ge(sem("ple_h"), 4)
                elif n:
                    act.wait_ge(sem("h_ready"), 1 if n == 1 else 2)
                else:
                    act.wait_ge(sem("x_landed"), 16)
                act.activation(xh[:, 1].rearrange("p k q -> p (k q)"), h[:, 1, :], ACT.Square,
                               accum_out=stat[:, 1:2]).then_inc(sem("sums1"), 1)

            def norm_apply(n):
                act.wait_ge(sem("norm_rstd"), n + 1)
                act.activation(xh[:, 1], h[:, 1, :].rearrange("p (q k) -> p k q", k=KT), ACT.Copy,
                               scale=rstd[:, 1:2]).then_inc(sem("xh_act"), 1)

            def norm_gain(n, gain, dst, ready, banks=(0, 2)):
                for b in banks:
                    act.wait_ge(sem("norm_flip"), 4 * n + b + 1)
                    act.activation(dst[:, 2 * b, :], bank[b][:, 0:T], ACT.Copy, scale=gains[:, gain, 2 * b:2 * b + 1])
                    act.activation(dst[:, 2 * b + 1, :], bank[b][:, T:2 * T], ACT.Copy,
                                   scale=gains[:, gain, 2 * b + 1:2 * b + 2]).then_inc(sem(ready), 1)

            act.preload_act_table_set(exp_ln)
            norm_sum(0)
            norm_apply(0)
            act.wait_ge(sem("first_landed"), 5 * 16)
            norm_gain(0, 0, xT, "xT_act")
            act.wait_ge(sem("conv_flip"), 1)
            act.activation(conv_w.rearrange("p t n -> p (t n)"), bank[4][:, 0:96], ACT.Copy
                           ).then_inc(sem("conv_ready"), 1)
            d = [decay[:, i, :] for i in range(10)]
            act.wait_ge(sem("ab_abs"), 1)
            link(act.activation(d[1], d[1], ACT.Exp, scale=-1.0))
            link(act.activation(d[1], d[1], ACT.Ln, bias=1.0))
            link(act.activation(d[4][:, 0:NH], ab_row[:, 0, :], ACT.Exp))
            act.activation(d[2], d[2], ACT.Exp, scale=-1.0).then_inc(sem("ab_exp"), 1)
            for name, pair, level in plan:
                n = pair * 6 + level - 1
                if name == "mm":
                    j, k = pair, level
                    if k == KT - 1 and j >= 3 * NH:
                        cn, c = divmod(j - 3 * NH, 2)
                        act.wait_ge(sem("proj_done"), j + 1)
                        act.activation(zs[:, c, HALF * cn:HALF * cn + HALF], bank[j % 2][:, :], ACT.Copy
                                       ).then_inc(sem("z_out"), 1)
                elif name == "cum":
                    act.wait_ge(sem("cum_ready"), 1)
                    link(act.activation(d[6], d[5], ACT.Exp))
                    act.activation(d[7], d[7], ACT.Exp).then_inc(sem("decay_exp"), 1)
                elif name == "silu":
                    act.wait_ge(sem("conv_done"), 6 * pair + 6)
                    for first in (0, 8, 16):
                        view = qkvT[:, first + 2 * pair:first + 2 * pair + 2, :]
                        act.activation(view, view, ACT.Silu).then_inc(sem("silu_done"), 1)
                    act.preload_act_table_set(exp_ln)
                    act.wait_ge(sem("silu_done"), 3 * pair + 3)
                    if pair:
                        act.wait_ge(sem("qk_normed"), pair)
                    for a in range(2):
                        act.activation(sq[:, 512 * a:512 * a + 512].rearrange("p (u t) -> p u t", u=2),
                                       qkvT[:, 8 * a + 2 * pair:8 * a + 2 * pair + 2, :], ACT.Square
                                       ).then_inc(sem("squares"), 1)
                elif name == "silu_z":
                    act.wait_ge(sem("z_out"), 4)
                    act.activation(zs, zs, ACT.Silu).then_inc(sem("z_ready"), 1)
                    act.preload_act_table_set(exp_ln)
                elif name == "norm":
                    act.wait_ge(sem("sumsq_done"), pair + 1)
                    act.activation(sq[:, 0:512], bank[2][:, :], ACT.Ln, scale=float(DH), bias=eps_t[:, 0:1]
                                   ).then_inc(sem("norm_ln"), 1)
                    act.activation(sq[:, 512:1024], bank[3][:, :], ACT.Ln, bias=eps_t[:, 1:2]
                                   ).then_inc(sem("norm_ln"), 1)
                    act.wait_ge(sem("norm_ln"), 2 * pair + 2)
                    act.activation(sq, sq, ACT.Exp, scale=-0.5).then_inc(sem("norm_exp"), 1)
                    act.wait_ge(sem("decay_diff"), pair + 1)
                    act.activation(Dm, Dm, ACT.Exp, scale=-1.0).then_inc(sem("decay_mat"), 1)
                elif name == "flip":
                    act.wait_ge(sem("flip_done"), 2 * pair + 2)
                    act.activation(ATm.rearrange("p u n -> p (u n)"), bank[3][:, :], ACT.Copy
                                   ).then_inc(sem("AT_ready"), 1)
                elif name == "half":
                    act.wait_ge(sem("half_done"), n + 1)
                    act.activation(Xm.rearrange("p u n -> p (u n)"), bank[4][:, :], ACT.Copy
                                   ).then_inc(sem("X_ready"), 1)
                elif name in ("new0", "new1"):
                    first = int(name[3])
                    act.wait_ge(sem(f"{name}_done"), pair + 1)
                    act.activation(v_new[:, first:4:2, :], bank[7][:, 0:256].rearrange("p (u n) -> p u n", u=2),
                                   ACT.Copy).then_inc(sem(f"{name}_ready"), 1)
                elif name == "state":
                    act.wait_ge(sem("state_done"), pair + 1)
                    act.activation(S_st, bank[5][:, 0:256].rearrange("p (u n) -> p u n", u=2), ACT.Copy
                                   ).then_inc(sem("state_ready"), 1)
                elif name == "turn":
                    act.wait_ge(sem("oT_flip_done"), pair + 1)
                    act.activation(xT[:, 2 * pair:2 * pair + 2, :].rearrange("p k t -> p (k t)"),
                                   bank[3][:, :], ACT.Copy).then_inc(sem("oT_ready"), 1)

            act.wait_ge(sem("small_landed"), 11 * 16)
            for layer in range(2):
                if layer == 1:
                    norm_sum(3)
                    norm_apply(3)
                    norm_gain(3, 6, xkvT, "xkv_ready", banks=range(4))
                    norm_gain(3, 3, xT, "xT_act")
                    for c in range(TT):
                        act.wait_ge(sem("kv_done"), c + 1)
                        act.activation(v_sb[:, c, :], bank[4 + c][:, 0:256], ACT.Copy).then_inc(sem("v_ready"), 1)
                    for g in range(2):
                        act.wait_ge(sem("kv_done"), 3 + g)
                        for a in range(2):
                            for b in range(2):
                                ins = act.activation(kT[64 * b:64 * b + 64, 2 * g + a, :],
                                                     bank[6 + g][64 * a:64 * a + 64, 0:T], ACT.Copy)
                        ins.then_inc(sem("kT_ready"), 1)
                    for i in range(KT):
                        act.wait_ge(sem("sbq_done"), i + 1)
                        act.activation(qT[:, i, :], bank[i % 2][:, 0:T], ACT.Copy, scale=-(SD ** -0.5)
                                       ).then_inc(sem("qT_ready"), 1)

                    act.preload_act_table_set(exp_ln)

                    def softplus(hd):
                        act.wait_ge(sem("z_score"), hd + 1)
                        u = soft_u[:, hd % 2, :]
                        if hd >= 2:
                            act.wait_ge(sem("soft_ready"), hd - 1)
                        link(act.activation(u, bank[hd % 3][:, 0:384], ACT.Abs))
                        link(act.activation(u, u, ACT.Exp, scale=-1.0))
                        act.activation(u, u, ACT.Ln, bias=1.0).then_inc(sem("soft_log"), 1)

                    def attn_exp(hd):
                        act.wait_ge(sem("rev_done"), hd + 1)
                        if hd >= 2:
                            act.wait_ge(sem("pv_done"), hd - 1)
                        act.activation(attn[:, hd % 2, :], bank[hd % 3][:, 0:384], ACT.Exp, scale=-1.0
                                       ).then_inc(sem("attn_exp"), 1)

                    for hd in range(QH + 1):
                        if hd < QH:
                            softplus(hd)
                        if hd >= 1:
                            attn_exp(hd - 1)

                norm_sum(1 + 3 * layer)
                norm_apply(1 + 3 * layer)
                norm_gain(1 + 3 * layer, 1 + 3 * layer, xT, "xT_act")
                act.wait_ge(sem("group_shift"), layer + 1)
                act.activation(rt[:, 2, :, 0:NG], rt[:, 1, :, 0:NG], ACT.Exp).then_inc(sem("group_exp"), 1)
                act.wait_ge(sem("pair_diff"), layer + 1)
                act.activation(rt[:, 14, :, 2:3], rt[:, 14, :, 1:2], ACT.Exp).then_inc(sem("pair_exp"), 1)
                act.wait_ge(sem("counts_done"), layer + 1)
                act.activation(rt[0:NE, 15, :, :].rearrange("p c e -> p (c e)")[:, 0:64], bank[6][0:NE, 0:64],
                               ACT.Copy).then_inc(sem("counts_ready"), 1)
                for k in range(0, KT, 2):
                    act.wait_ge(sem("gather_done"), KT * layer + k + 1)
                    act.activation(xs[:, k, 0:SLOTS], bank[k % 4][:, :], ACT.Copy,
                                   scale=gains[:, 1 + 3 * layer, k:k + 1]).then_inc(sem("xs_act"), 1)

                def gate_silu(x, done, used):
                    act.wait_ge(sem("gu_done"), done)
                    if used is not None:
                        act.wait_ge(sem("hh_ready"), used)
                    act.activation(sg[64:128, x, :], bank[4 + x][0:64, 0:FE], ACT.Silu).then_inc(sem("sg_ready"), 1)

                def turned_out(x, done, used):
                    act.wait_ge(sem("tr_done"), done)
                    if used is not None:
                        act.wait_ge(sem("scat_done"), used)
                    act.activation(hr[:, x, :], bank[6][:, :], ACT.Copy).then_inc(sem("hr_ready"), 1)

                q0 = NE // 2 * layer
                for x in range(2):
                    q = q0 + x
                    gate_silu(0, 2 * q + 1, 2 * q - 1 if q else None)
                    if x:
                        turned_out(0, q, 2 * q - 4 if q > 2 else None)
                    gate_silu(1, 2 * q + 2, 2 * q if q else None)
                with act.Fori(1, NE // RING) as i:
                    for x in range(2):
                        gate_silu(0, i * 4 + (2 * (q0 + x) + 1), i * 4 + (2 * (q0 + x) - 1))
                        turned_out(1 - x, i * 2 + (q0 + x), i * 4 + (2 * (q0 + x) - 4) if x or q0 else
                                   i * 4 + (2 * q0 - 3))
                        gate_silu(1, i * 4 + (2 * (q0 + x) + 2), i * 4 + 2 * (q0 + x))
                turned_out(1, q0 + NE // 2, 2 * (q0 + NE // 2) - 4)

                act.wait_ge(sem("p_flip"), layer + 1)
                act.activation(pT.rearrange("p j t -> p (j t)"), bank[5][:, :], ACT.Copy).then_inc(sem("pT_ready"), 1)

                flag = act.value_load(over_i[0:1, 0:1], min_val=0, max_val=1)
                with act.If(flag > 0):
                    with act.Fori(0, NE) as e:
                        for f in range(2):
                            act.wait_ge(sem(f"over_gu{layer}"), e * 2 + (f + 1))
                            act.activation(over_g[:, f, :], bank[4][:, 0:T], ACT.Silu
                                           ).then_inc(sem(f"over_silu{layer}"), 1)

                n = 2 + 3 * layer
                norm_apply(n)
                norm_gain(n, n, xT, "xT_act")
                for j in range(4):
                    act.wait_ge(sem("ple_gate_done"), 4 * layer + j + 1)
                    act.activation(gate[:, j, :], bank[j][:, :], ACT.Sigmoid).then_inc(sem("gate_ready"), 1)

        @block.tensor
        def _(pe):
            def norm_flip(n):
                pe.wait_ge(sem("xh_act"), n + 1)
                pe.wait_ge(sem("xh_dve"), n + 1)
                for b in range(4):
                    for k in range(2 * b, 2 * b + 2):
                        for c in range(TT):
                            col = T * (k % 2) + P * c
                            ins = pe.transpose(bank[b][:, col:col + P], xh[:, c, k, :], ident[:, :])
                    ins.then_inc(sem("norm_flip"), 1)

            def by_token(dst, src, w, c, ready, kts=KT):
                for k in range(kts):
                    ins = pe.matmul(dst, src[:, k, P * c:P * c + P], w[:, k, :], start=(k == 0),
                                    stop=(k == kts - 1))
                ins.then_inc(ready, 1)

            pe.wait_ge(sem("const_set"), 6)
            norm_flip(0)
            pe.wait_ge(sem("first_landed"), 5 * 16)
            pe.transpose(bank[4][:, 0:96], conv_rows, ident[0:96, 0:96]).then_inc(sem("conv_flip"), 1)
            pe.wait_ge(sem("xT_act"), 2)
            pe.wait_ge(sem("xT_dve"), 2)
            for c in range(TT):
                for k in range(KT):
                    ins = pe.matmul(bank[5][:, 16 * c:16 * c + 16], xT[:, k, P * c:P * c + P], w_ab[:, k, :],
                                    start=(k == 0), stop=(k == KT - 1))
            ins.then_inc(sem("ab_done"), 1)
            g_all = decay[:, 3, :]

            def head(pair, kind, i, c):
                return qkvT[:, 8 * kind + 2 * pair + i, P * c:P * c + P]

            for name, pair, level in plan:
                n = pair * 6 + level
                if name == "mm" and pair < 3 * NH:
                    j, k = pair, level
                    source, col, _ = tile_of(j)
                    if k == 0:
                        wait_chunk(pe, source)
                        if j >= 2:
                            pe.wait_ge(sem("conv_done"), j - 1)
                    ins = pe.matmul(bank[j % 2][:, 0:T], chunk(source)[:, k, col:col + P], xT[:, k, :],
                                    start=(k == 0), stop=(k == KT - 1))
                    if k == KT - 1:
                        ins.then_inc(sem("proj_done"), 1)
                elif name == "mm":
                    j, k = pair, level
                    cn, c = divmod(j - 3 * NH, 2)
                    if k == 0:
                        wait_chunk(pe, f"z{cn}")
                        if j < 3 * NH + 2:
                            pe.wait_ge(sem("conv_done"), j - 1)
                        else:
                            pe.wait_ge(sem("z_out"), j - 3 * NH - 1)
                    ins = pe.matmul(bank[j % 2][:, :], xT[:, k, P * c:P * c + P], chunk(f"z{cn}")[:, k, :],
                                    start=(k == 0), stop=(k == KT - 1))
                    if k == KT - 1:
                        ins.then_inc(sem("proj_done"), 1)
                elif name == "cum":
                    pe.wait_ge(sem("g_ready"), 1)
                    pe.matmul(bank[6][:, 0:16], upper[:, :], g_all, start=True, stop=True)
                    pe.matmul(bank[6][:, 16:32], ones[:, :], g_all, start=True, stop=True
                              ).then_inc(sem("cum_done"), 1)
                elif name == "norm":
                    for a in range(2):
                        pe.wait_ge(sem("squares"), 2 * pair + a + 1)
                        if pair and not a:
                            pe.wait_ge(sem("lt_ready"), pair)
                            pe.wait_ge(sem("AT_ready"), pair)
                        ins = pe.matmul(bank[2 + a][:, :], ones[:, :], sq[:, 512 * a:512 * a + 512],
                                        start=True, stop=True)
                    ins.then_inc(sem("sumsq_done"), 1)
                    for u in range(4):
                        i, c = divmod(u, 2)
                        col = NH * c + 2 * pair + i
                        ins = pe.matmul(bank[4][:, P * u:P * u + P], g_all[:, col:col + 1].broadcast_to([P, P]),
                                        upper[:, :], start=True, stop=True)
                    ins.then_inc(sem("row_cum_done"), 1)
                elif name == "gram":
                    pe.wait_ge(sem("qk_normed"), pair + 1)
                    if pair:
                        pe.wait_ge(sem("q_state_ready"), pair)
                    for kind in (1, 0):
                        for u in range(4):
                            i, c = divmod(u, 2)
                            ins = pe.matmul(bank[6 - kind][:, P * u:P * u + P], head(pair, kind, i, c),
                                            head(pair, 1, i, c), start=True, stop=True)
                    ins.then_inc(sem("gram_done"), 1)
                    pe.wait_ge(sem("decay_diff"), pair + 1)
                    for i in range(2):
                        for c in range(TT):
                            u = 2 * i + c
                            pe.transpose(bank[7][:, P * u:P * u + P], qkvT[:, 16 + 2 * pair + i, P * c:P * c + P],
                                         ident[:, :])
                        ins = pe.transpose(bank[4][:, P * i:P * i + P], head(pair, 1, i, 0), ident[:, :])
                    ins.then_inc(sem("kv_flip_done"), 1)
                elif name == "flip":
                    pe.wait_ge(sem("L_ready"), pair + 1)
                    pe.wait_ge(sem("norm_ln"), 2 * pair + 2)
                    if pair:
                        pe.wait_ge(sem("o_out"), pair)
                    for m, b in ((Lm, 2), (Am, 3)):
                        if m is Am:
                            pe.wait_ge(sem("A_ready"), pair + 1)
                        for u in range(4):
                            ins = pe.transpose(bank[b][:, P * u:P * u + P], m[:, u, :], ident[:, :])
                        ins.then_inc(sem("flip_done"), 1)
                elif name == "half":
                    pe.wait_ge(sem("LM_ready"), n)
                    pe.wait_ge(sem("T_ready"), n)
                    if level == 1:
                        pe.wait_ge(sem("kv_tok"), pair + 1)
                    for u in range(4):
                        ins = pe.matmul(bank[4][:, P * u:P * u + P], LMm[:, u, :], Tm[:, u, :], start=True, stop=True)
                    ins.then_inc(sem("half_done"), 1)
                elif name == "full":
                    pe.wait_ge(sem("X_ready"), n)
                    pe.wait_ge(sem("Z_ready"), pair * 7 + level)
                    if level < 6:
                        for u in range(4):
                            ins = pe.matmul(bank[5][:, P * u:P * u + P], Zm[:, u, :], Xm[:, u, :],
                                            start=True, stop=True)
                        ins.then_inc(sem("fullT_done"), 1)
                    for u in range(4):
                        ins = pe.matmul(bank[6][:, P * u:P * u + P], Xm[:, u, :], Zm[:, u, :], start=True, stop=True)
                    ins.then_inc(sem("fullZ_done"), 1)
                elif name == "new0":
                    pe.wait_ge(sem("Z_ready"), pair * 7 + 7)
                    pe.wait_ge(sem("B0_ready"), pair + 1)
                    for i in range(2):
                        ins = pe.matmul(bank[7][:, P * i:P * i + P], Zm[:, 2 * i, :], B_in[:, i, :],
                                        start=True, stop=True)
                    ins.then_inc(sem("new0_done"), 1)
                elif name == "state":
                    pe.wait_ge(sem("new0_ready"), pair + 1)
                    for i in range(2):
                        ins = pe.matmul(bank[5][:, P * i:P * i + P], k_tok[:, i, :], v_new[:, 2 * i, :],
                                        start=True, stop=True)
                    ins.then_inc(sem("state_done"), 1)
                elif name == "read":
                    pe.wait_ge(sem("state_ready"), pair + 1)
                    for i in range(2):
                        ins = pe.matmul(bank[5][:, 256 + P * i:256 + P * i + P], head(pair, 1, i, 1), S_st[:, i, :],
                                        start=True, stop=True)
                    ins.then_inc(sem("read_done"), 1)
                    for i in range(2):
                        ins = pe.matmul(bank[6][:, P * i:P * i + P], head(pair, 0, i, 1), S_st[:, i, :],
                                        start=True, stop=True)
                    ins.then_inc(sem("q_state_done"), 1)
                elif name == "new1":
                    pe.wait_ge(sem("B1_ready"), pair + 1)
                    for i in range(2):
                        ins = pe.matmul(bank[7][:, P * i:P * i + P], Zm[:, 2 * i + 1, :], B_in[:, i, :],
                                        start=True, stop=True)
                    ins.then_inc(sem("new1_done"), 1)
                elif name == "out":
                    pe.wait_ge(sem("new1_ready"), pair + 1)
                    if pair + 2 <= NH // 2:
                        pe.wait_ge(sem("norm_ln"), 2 * pair + 4)
                    for u in range(4):
                        ins = pe.matmul(bank[2][:, P * u:P * u + P], ATm[:, u, :], v_new[:, u, :],
                                        start=True, stop=True)
                    ins.then_inc(sem("o_done"), 1)
                    if pair == NH // 2 - 1:
                        pe.wait_ge(sem("oT_ready"), 3)
                        pe.wait_ge(sem("q_state_ready"), pair + 1)
                        for half in range(2):
                            wait_chunk(pe, f"go{half}")
                            for c in range(TT):
                                for k in range(6):
                                    pe.matmul(bank[4 + 2 * half + c][:, :], xT[:, k, P * c:P * c + P],
                                              chunk(f"go{half}")[:, k, :], start=(k == 0), stop=False)
                elif name == "turn":
                    pe.wait_ge(sem("o_gated"), pair + 1)
                    if pair:
                        pe.wait_ge(sem("oT_ready"), pair)
                    for i in range(2):
                        for c in range(TT):
                            ins = pe.transpose(bank[3][:, T * i + P * c:T * i + P * c + P],
                                               o_tok[:, c, 2 * pair + i, :], ident[:, :])
                    ins.then_inc(sem("oT_flip_done"), 1)
            pe.wait_ge(sem("oT_ready"), 4)
            for half in range(2):
                for c in range(TT):
                    for k in range(6, KT):
                        ins = pe.matmul(bank[4 + 2 * half + c][:, :], xT[:, k, P * c:P * c + P],
                                        chunk(f"go{half}")[:, k, :], start=False, stop=(k == KT - 1))
                    ins.then_inc(sem("gdn_out_done"), 1)

            for layer in range(2):
                if layer == 1:
                    norm_flip(3)
                    pe.wait_ge(sem("xkv_ready"), 4)
                    wait_chunk(pe, "kv")
                    pe.wait_ge(sem("ple_h"), 4)
                    for c in range(TT):
                        by_token(bank[4 + c][:, 0:256], xkvT, chunk("kv")[:, :, 256:512], c, sem("kv_done"))
                    for g in range(2):
                        for k in range(KT):
                            ins = pe.matmul(bank[6 + g][:, 0:T], chunk("kv")[:, k, P * g:P * g + P], xkvT[:, k, :],
                                            start=(k == 0), stop=(k == KT - 1))
                        ins.then_inc(sem("kv_done"), 1)
                    pe.wait_ge(sem("xT_act"), 8)
                    pe.wait_ge(sem("xT_dve"), 8)
                    for i in range(KT):
                        cn = i // 4
                        if i % 4 == 0:
                            wait_chunk(pe, f"sq{cn}")
                        if i >= 2:
                            pe.wait_ge(sem("qT_ready"), i - 1)
                        for k in range(KT):
                            ins = pe.matmul(bank[i % 2][:, 0:T], chunk(f"sq{cn}")[:, k, P * (i % 4):P * (i % 4) + P],
                                            xT[:, k, :], start=(k == 0), stop=(k == KT - 1))
                        ins.then_inc(sem("sbq_done"), 1)
                    pe.wait_ge(sem("kT_ready"), 2)
                    pe.wait_ge(sem("v_ready"), 2)
                    pe.wait_ge(sem("qT_ready"), KT)

                    def score(hd):
                        lo = 64 * (hd % 2)
                        if hd >= 3:
                            pe.wait_ge(sem("attn_exp"), hd - 2)
                        k_, q_ = kT[lo:lo + 64, hd // 4, :], qT[lo:lo + 64, hd // 2, :]
                        b = bank[hd % 3]
                        pe.matmul(b[:, 0:256], k_[:, 0:P], q_, start=True, stop=True)
                        pe.matmul(b[:, 256:384], k_[:, P:T], q_[:, P:T], start=False, stop=True,
                                  skip_group_check=True).then_inc(sem("z_score"), 1)

                    def reverse(hd):
                        pe.wait_ge(sem("soft_ready"), hd + 1)
                        b, s_ = bank[hd % 3], soft[:, hd % 2, :]
                        pe.matmul(b[:, 0:256], lower[:, :], s_[:, 0:256], start=False, stop=False,
                                  skip_group_check=True)
                        pe.matmul(b[:, 128:256], ones[:, :], s_[:, 256:384], start=False, stop=False,
                                  skip_group_check=True)
                        pe.matmul(b[:, 256:384], lower[:, :], s_[:, 256:384], start=False, stop=True,
                                  skip_group_check=True).then_inc(sem("rev_done"), 1)

                    def values(hd):
                        lo, g = 64 * (hd % 2), hd // 4
                        pe.wait_ge(sem("attn_ready"), hd + 1)
                        if hd % 2 == 0 and hd >= 4:
                            pe.wait_ge(sem("sbo_ready"), hd // 2 - 1)
                        a = attn[:, hd % 2, :]
                        o = bank[3 + (hd // 2) % 2][lo:lo + 64, 0:T]
                        pe.matmul(o, v_sb[:, 0, SD * g:SD * g + SD], a[:, 0:256], start=True, stop=False,
                                  skip_group_check=True)
                        pe.matmul(o[:, 128:256], v_sb[:, 1, SD * g:SD * g + SD], a[:, 256:384], start=False,
                                  stop=True, skip_group_check=True).then_inc(sem("pv_done"), 1)

                    for hd in range(QH + 2):
                        if hd < QH:
                            score(hd)
                        if 1 <= hd <= QH:
                            reverse(hd - 1)
                        if hd >= 2:
                            values(hd - 2)
                    pe.wait_ge(sem("sbo_ready"), KT)
                    for half in range(2):
                        wait_chunk(pe, f"so{half}")
                        for c in range(TT):
                            by_token(bank[5 + c if half == 0 else 7 * (c == 0)][:, :], xT, chunk(f"so{half}"), c,
                                     sem("sb_out_done"))

                n = 1 + 3 * layer
                norm_flip(n)
                pe.wait_ge(sem("xT_act"), 2 * (n + 1))
                pe.wait_ge(sem("xT_dve"), 2 * (n + 1))
                pe.wait_ge(sem("router_landed"), 32 * (layer + 1))
                for c in range(TT):
                    for k in range(KT):
                        ins = pe.matmul(bank[4][:, 36 * c:36 * c + 36], xT[:, k, P * c:P * c + P], w_rt[:, k, :],
                                        start=(k == 0), stop=(k == KT - 1))
                ins.then_inc(sem("logits_done"), 1)
                pe.wait_ge(sem("chosen"), layer + 1)
                ch = rt[:, 9, :, :]
                pe.matmul(bank[5][:, 0:32], below[:, :], ch[:, 0, :], start=True, stop=True)
                pe.matmul(bank[5][:, 32:64], ones[:, :], ch[:, 0, :], start=True, stop=False)
                pe.matmul(bank[5][:, 32:64], below[:, :], ch[:, 1, :], start=False, stop=True)
                for c in range(TT):
                    pe.matmul(bank[5][:, 64:96], ones[:, :], ch[:, c, :], start=(c == 0), stop=(c == 1))
                for c in range(TT):
                    ins = pe.matmul(bank[6][0:NE, 0:64], ch[:, c, :], ones[:, 0:64], start=(c == 0), stop=(c == 1))
                ins.then_inc(sem("counts_done"), 1)
                pe.wait_ge(sem("counts_ready"), layer + 1)
                cnt = rt[0:NE, 15, :, :].rearrange("p c e -> p (c e)")
                for a in range(2):
                    ins = pe.matmul(bank[7][64 * a:64 * a + 64, 0:NE], cnt[:, 0:64], below[0:NE, 0:NE],
                                    start=True, stop=True)
                ins.then_inc(sem("offsets_done"), 1)
                pe.wait_ge(sem("one_hot_ready"), layer + 1)
                for k in range(KT):
                    if k >= 4:
                        pe.wait_ge(sem("xs_act" if k % 2 == 0 else "xs_dve"), 4 * layer + (k - 4) // 2 + 1)
                    for c in range(TT):
                        ins = pe.matmul(bank[k % 4][:, :], xh[:, c, k, :], one_hot[:, c, :], start=(c == 0),
                                        stop=(c == 1))
                    ins.then_inc(sem("gather_done"), 1)
                pe.wait_ge(sem("xs_act"), 4 * layer + 4)
                pe.wait_ge(sem("xs_dve"), 4 * layer + 4)

                def gate_up(x, s, e1, turn, used):
                    pe.wait_ge(sem(f"expert_gu{s}"), turn * 32 + 32)
                    pe.wait_ge(sem("xe_ready"), e1)
                    if used is not None:
                        pe.wait_ge(sem("hh_ready"), used)
                    w = moe_w[:, s, :, :].rearrange("p a (k f) -> p a k f", k=KT)
                    for k in range(KT):
                        for a in range(2):
                            ins = pe.matmul(bank[4 + x][64 * a:64 * a + 64, 0:FE], xe[:, x, k, :], w[:, a, k, :],
                                            start=(k == 0), stop=(k == KT - 1), skip_group_check=True)
                    ins.then_inc(sem("gu_done"), 1)

                def turn_pair(q1):
                    pe.wait_ge(sem("hh_ready"), q1 * 2)
                    pe.wait_ge(sem("rw_ready"), q1)
                    for c in range(TT):
                        pe.transpose(bank[6][:, 256 + P * c:256 + P * c + P], rw[:, c, :], ident[:, :])
                    for x in range(2):
                        for j in range(2):
                            ins = pe.transpose(bank[6][:, P * x + 64 * j:P * x + 64 * j + 64],
                                               hh[64:128, x, j:FE:2], ident[64:128, 64:128])
                    ins.then_inc(sem("tr_done"), 1)

                def down_half(a, b, q1, turn, ready):
                    if a == 0:
                        for x in range(2):
                            pe.wait_ge(sem(f"expert_d{2 * b + x}"), turn * 16 + 16)
                        pe.wait_ge(sem("hr_ready"), q1)
                    if ready is not None:
                        pe.wait_ge(sem("ye_ready"), ready)
                    for j in range(2):
                        for x in range(2):
                            w = moe_w[:, 2 * b + x, 2, :].rearrange("p (j d) -> p j d", j=2)
                            ins = pe.matmul(bank[7][64 * x:64 * x + 64, :], hr[:, b, P * x + 64 * j:P * x + 64 * j + 64],
                                            w[:, j, HALF * a:HALF * a + HALF], start=(j == 0), stop=(j == 1),
                                            skip_group_check=True)
                    ins.then_inc(sem("down_done"), 1)

                def scatter_half(a, b, ready, first=False, last=False):
                    pe.wait_ge(sem("ye_ready"), ready)
                    for c in range(TT):
                        ins = pe.matmul(bank[2 * c + a][:, :], hr[:, b, 256 + P * c:256 + P * c + P], ye[:, a, :],
                                        start=first, stop=last, skip_group_check=True)
                    ins.then_inc(sem("scat_done"), 1)

                pe.wait_ge(sem("pad_set"), layer + 1)
                for j in (1, 3):
                    pe.matmul(bank[j][:, :], ones[:, :], xs[:, :, SLOTS:], start=True, stop=False,
                              skip_group_check=True)

                q0, t0 = NE // 2 * layer, NE // RING * layer
                for b in range(2):
                    q = q0 + b
                    gate_up(0, 2 * b, 2 * q + 1, t0, 2 * q - 1 if q else None)
                    if b:
                        turn_pair(q)
                    gate_up(1, 2 * b + 1, 2 * q + 2, t0, 2 * q if q else None)
                    if b:
                        down_half(0, 0, q, t0, 2 * q - 2 if q > 1 else None)
                        down_half(1, 0, q, t0, 2 * q - 1)
                        scatter_half(0, 0, 2 * q - 1, first=True)
                with pe.Fori(1, NE // RING) as i:
                    for b in range(2):
                        q = i * 2 + (q0 + b)
                        e1 = i * 4 + (2 * (q0 + b) + 1)
                        prev = i + t0 if b else i + (t0 - 1)
                        gate_up(0, 2 * b, e1, i + t0, e1 - 2)
                        turn_pair(q)
                        gate_up(1, 2 * b + 1, e1 + 1, i + t0, e1 - 1)
                        down_half(0, 1 - b, q, prev, e1 - 3)
                        scatter_half(1, b, e1 - 3)
                        down_half(1, 1 - b, q, prev, e1 - 2)
                        scatter_half(0, 1 - b, e1 - 2)
                end = q0 + NE // 2
                turn_pair(end)
                down_half(0, 1, end, t0 + NE // RING - 1, 2 * end - 2)
                scatter_half(1, 0, 2 * end - 2)
                down_half(1, 1, end, t0 + NE // RING - 1, 2 * end - 1)
                scatter_half(0, 1, 2 * end - 1, last=True)
                pe.wait_ge(sem("p_landed"), 16 * (layer + 1))
                for j in range(2):
                    for c in range(TT):
                        ins = pe.transpose(bank[5][:, T * j + P * c:T * j + P * c + P], p_tok[:, c, P * j:P * j + P],
                                           ident[:, :])
                ins.then_inc(sem("p_flip"), 1)
                scatter_half(1, 1, 2 * end, last=True)

                pe.wait_ge(sem("moe_acc"), layer + 1)
                flag = pe.value_load(over_i[0:1, 0:1], min_val=0, max_val=1)
                with pe.If(flag > 0):
                    with pe.Fori(0, NE) as e:
                        pe.wait_ge(sem(f"over_landed{layer}"), e * 48 + 48)
                        for f in range(2):
                            pe.wait_ge(sem(f"over_hid{layer}"), e * 2 + (f + 1))
                            for a in range(2):
                                w = over_w(a).rearrange("p (k f) -> p k f", k=KT)
                                for k in range(KT):
                                    ins = pe.matmul(bank[4 + a][:, 0:T], w[:, k, f:FE:2], xT[:, k, :],
                                                    start=(k == 0), stop=(k == KT - 1))
                            ins.then_inc(sem(f"over_gu{layer}"), 1)
                        pe.wait_ge(sem(f"over_hid{layer}"), e * 2 + 3)
                        w = over_w(2).rearrange("p (j d) -> p j d", j=2)
                        for c in range(TT):
                            for a in range(2):
                                for f in range(2):
                                    ins = pe.matmul(bank[2 * c + a][:, :], over_g[:, f, P * c:P * c + P],
                                                    w[:, f, HALF * a:HALF * a + HALF], start=(f == 0), stop=(f == 1))
                        ins.then_inc(sem(f"over_down{layer}"), 1)

                n = 2 + 3 * layer
                wait_chunk(pe, f"pp{layer}")
                pe.wait_ge(sem("pT_ready"), layer + 1)
                w = wring[:, CHUNKS.index(f"pp{layer}") % WSLOTS, 0:2 * D].rearrange("p (j n) -> p j n", j=2)
                for half in range(2):
                    for c in range(TT):
                        by_token(bank[4 + 2 * half + c][:, :], pT, w[:, :, HALF * half:HALF * half + HALF], c,
                                 sem("ple_emb_done"), kts=2)
                norm_flip(n)
                pe.wait_ge(sem("xT_act"), 2 * (n + 1))
                pe.wait_ge(sem("xT_dve"), 2 * (n + 1))
                for half in range(2):
                    wait_chunk(pe, f"pg{layer}.{half}")
                    for c in range(TT):
                        by_token(bank[2 * half + c][:, :], xT, chunk(f"pg{layer}.{half}"), c, sem("ple_gate_done"))

        @block.vector
        def _(dve):
            link = chain_of(dve, "dve_chain")

            def norm_sum(n, tiles=(0,)):
                for c in tiles:
                    dve.tensor_tensor_reduce(xh[:, c].rearrange("p k q -> p (k q)"), h[:, c, :], h[:, c, :], 1.0, 0.0,
                                             ALU.mult, ALU.add, stat[:, c:c + 1]).then_inc(sem(f"sums{c}"), 1)

            def norm_gain(n, gain):
                for b in (1, 3):
                    dve.wait_ge(sem("norm_flip"), 4 * n + b + 1)
                    if n == 3:
                        dve.wait_ge(sem("xkv_ready"), b + 1)
                    for k in range(2):
                        ins = dve.tensor_scalar(xT[:, 2 * b + k, :], bank[b][:, T * k:T * k + T],
                                                gains[:, gain, 2 * b + k:2 * b + k + 1], None, ALU.mult)
                    ins.then_inc(sem("xT_dve"), 1)

            def norm_apply(n):
                dve.wait_ge(sem("norm_rstd"), n + 1)
                dve.tensor_scalar(xh[:, 0], h[:, 0, :].rearrange("p (q k) -> p k q", k=KT), rstd[:, 0:1], None,
                                  ALU.mult).then_inc(sem("xh_dve"), 1)

            dve.memset(eps_t[:, 0:1], EPS * DH)
            dve.memset(eps_t[:, 1:2], EPS).then_inc(sem("eps_set"), 1)
            dve.wait_ge(sem("x_landed"), 16)
            norm_sum(0)
            norm_apply(0)
            dve.wait_ge(sem("first_landed"), 5 * 16)
            norm_gain(0, 0)
            d = [decay[:, i, :] for i in range(10)]

            def pairs(t):
                return t.rearrange("p (c h) -> p c h", c=TT)
            dve.wait_ge(sem("ab_done"), 1)
            ab = bank[5][:, 0:32].rearrange("p (c n) -> p c n", c=TT)
            link(dve.tensor_tensor(pairs(d[0]), ab[:, :, 0:NH], ab_row[:, 1:2, :].broadcast_to([P, TT, NH]), ALU.add))
            link(dve.tensor_copy(pairs(d[2]), ab[:, :, NH:]))
            link(dve.tensor_scalar(d[1], d[0], -1.0, None, ALU.mult))
            dve.tensor_tensor(d[1], d[1], d[0], ALU.max).then_inc(sem("ab_abs"), 1)
            dve.wait_ge(sem("ab_exp"), 1)
            link(dve.scalar_tensor_tensor(out=d[3], in0=d[0], scalar=0.0, in1=d[1], op0=ALU.max, op1=ALU.add))
            link(dve.tensor_tensor(pairs(d[3]), pairs(d[3]), d[4][:, 0:NH].unsqueeze(1).broadcast_to([P, TT, NH]),
                                   ALU.mult))
            dve.tensor_scalar(d[3], d[3], -1.0, None, ALU.mult).then_inc(sem("g_ready"), 1)
            link(dve.tensor_scalar(d[2], d[2], 1.0, None, ALU.add))
            link(dve.reciprocal(d[8], d[2]))
            G, eG, kdec, beta, neg_eG = d[5], d[6], d[7], d[8], d[9]
            dve.wait_ge(sem("conv_ready"), 1)

            flat = "p u n -> p (u n)"

            def add_h(j, done, src, ready=None):
                half, c = divmod(j, 2)
                dve.wait_ge(*done)
                view = h[:, c, HALF * half:HALF * half + HALF]
                ins = dve.tensor_tensor(view, src[:, :], view, ALU.add)
                if ready:
                    ins.then_inc(sem(ready), 1)
                else:
                    link(ins)

            def gate_out(pair):
                o = o_tok[:, :, 2 * pair:2 * pair + 2, :]
                z = zs[:, :, 256 * pair:256 * pair + 256].rearrange("p c (i n) -> p c i n", i=2)
                dve.tensor_tensor(o, o, z, ALU.mult).then_inc(sem("o_gated"), 1)

            for name, pair, level in plan:
                n = pair * 6 + level
                cols = [NH * c + 2 * pair + i for i in range(2) for c in range(TT)]
                if name == "mm":
                    j, k = pair, level
                    if k < KT - 1 or j >= 3 * NH:
                        continue
                    ct = tile_of(j)[2]
                    dve.wait_ge(sem("proj_done"), j + 1)
                    src, dst = bank[j % 2][:, 0:T], qkvT[:, ct, :]
                    link(dve.tensor_scalar(dst, src, conv_w[:, 3, ct:ct + 1], None, ALU.mult))
                    for tap in (2, 1, 0):
                        lag = 3 - tap
                        ins = dve.scalar_tensor_tensor(out=dst[:, lag:], in0=src[:, 0:T - lag],
                                                       scalar=conv_w[:, tap, ct:ct + 1], in1=dst[:, lag:],
                                                       op0=ALU.mult, op1=ALU.add)
                        if tap:
                            link(ins)
                        else:
                            ins.then_inc(sem("conv_done"), 1)
                elif name == "cum":
                    dve.wait_ge(sem("cum_done"), 1)
                    link(dve.tensor_copy(d[5], bank[6][:, 0:16]))
                    dve.tensor_tensor(d[7], bank[6][:, 16:32], d[5], ALU.subtract).then_inc(sem("cum_ready"), 1)
                    dve.wait_ge(sem("decay_exp"), 1)
                    link(dve.tensor_scalar(d[9], d[6], -1.0, None, ALU.mult))
                    dve.wait_ge(sem("blocks_set"), 1)
                    dve.wait_ge(sem("iota_set"), 1)
                    for n in range(len(LEVELS)):
                        nxt = blk[:, n + 1, :] if n + 1 < len(LEVELS) else ones[:, :]
                        link(dve.tensor_tensor(blk[:, n, :], blk[:, n, :], nxt, ALU.subtract))
                elif name == "norm":
                    dve.wait_ge(sem("row_cum_done"), pair + 1)
                    for u in range(4):
                        ins = dve.tensor_scalar(Dm[:, u, :], bank[4][:, P * u:P * u + P], G[:, cols[u]:cols[u] + 1],
                                                0.0, ALU.subtract, ALU.max)
                    ins.then_inc(sem("decay_diff"), 1)
                    dve.wait_ge(sem("norm_exp"), pair + 1)
                    for a in range(2):
                        view = qkvT[:, 8 * a + 2 * pair:8 * a + 2 * pair + 2, :]
                        ins = dve.tensor_tensor(view, view, sq[:, 512 * a:512 * a + 512].rearrange(
                            "p (u t) -> p u t", u=2), ALU.mult)
                    ins.then_inc(sem("qk_normed"), 1)
                    dve.wait_ge(sem("decay_mat"), pair + 1)
                    link(dve.tensor_tensor(Dm, Dm, lower[:, :].unsqueeze(1).broadcast_to([P, 4, P]), ALU.mult))
                elif name == "gram":
                    dve.wait_ge(sem("gram_done"), pair + 1)
                    for u in range(4):
                        ins = dve.scalar_tensor_tensor(out=Lm[:, u, :], in0=bank[5][:, P * u:P * u + P],
                                                       scalar=beta[:, cols[u]:cols[u] + 1], in1=Dm[:, u, :],
                                                       op0=ALU.mult, op1=ALU.mult)
                    ins.then_inc(sem("L_ready"), 1)
                    dve.tensor_tensor(Am.rearrange(flat), bank[6][:, :], Dm.rearrange(flat), ALU.mult
                                      ).then_inc(sem("A_ready"), 1)
                elif name == "flip":
                    m1 = blk[:, 0:1, :].broadcast_to([P, 4, P])
                    idb = ident[:, :].unsqueeze(1).broadcast_to([P, 4, P])
                    dve.wait_ge(sem("L_ready"), pair + 1)
                    link(dve.tensor_tensor(Tm, Lm, m1, ALU.mult))
                    dve.wait_ge(sem("flip_done"), 2 * pair + 1)
                    dve.tensor_copy(LTm.rearrange(flat), bank[2][:, :]).then_inc(sem("lt_ready"), 1)
                    dve.tensor_tensor(Tm, Tm, idb, ALU.add).then_inc(sem("T_ready"), 1)
                    dve.wait_ge(sem("lt_ready"), pair + 1)
                    dve.tensor_tensor(LMm, LTm, blk[:, 1:2, :].broadcast_to([P, 4, P]), ALU.mult
                                      ).then_inc(sem("LM_ready"), 1)
                    link(dve.tensor_tensor(Zm, LTm, m1, ALU.mult))
                    dve.tensor_tensor(Zm, Zm, idb, ALU.add).then_inc(sem("Z_ready"), 1)
                    dve.wait_ge(sem("kv_flip_done"), pair + 1)
                    link(dve.tensor_copy(v_tok.rearrange(flat), bank[7][:, :]))
                    for i in range(2):
                        ins = dve.tensor_scalar(k_tok[:, i, :], bank[4][:, P * i:P * i + P],
                                                kdec[:, cols[2 * i]:cols[2 * i] + 1], None, ALU.mult)
                    ins.then_inc(sem("kv_tok"), 1)
                    for i in range(2):
                        ins = dve.tensor_scalar(B_in[:, i, :], v_tok[:, 2 * i, :],
                                                beta[:, cols[2 * i]:cols[2 * i] + 1], None, ALU.mult)
                    ins.then_inc(sem("B0_ready"), 1)
                elif name == "half" and level < 6:
                    dve.wait_ge(sem("half_done"), n)
                    dve.tensor_tensor(LMm, LTm, blk[:, level + 1:level + 2, :].broadcast_to([P, 4, P]), ALU.mult
                                      ).then_inc(sem("LM_ready"), 1)
                elif name == "full":
                    if level < 6:
                        dve.wait_ge(sem("fullT_done"), 5 * pair + level)
                        dve.wait_ge(sem("T_ready"), n)
                        dve.tensor_tensor(Tm.rearrange(flat), bank[5][:, :], Tm.rearrange(flat), ALU.add
                                          ).then_inc(sem("T_ready"), 1)
                    dve.wait_ge(sem("fullZ_done"), n)
                    dve.wait_ge(sem("Z_ready"), pair * 7 + level)
                    dve.tensor_tensor(Zm.rearrange(flat), bank[6][:, :], Zm.rearrange(flat), ALU.add
                                      ).then_inc(sem("Z_ready"), 1)
                elif name == "silu_z":
                    dve.wait_ge(sem("z_ready"), 1)
                    for done in range(3):
                        gate_out(done)
                elif name == "read":
                    dve.wait_ge(sem("read_done"), pair + 1)
                    for i in range(2):
                        u = 2 * i + 1
                        link(dve.scalar_tensor_tensor(out=B_in[:, i, :], in0=bank[5][:, 256 + P * i:256 + P * i + P],
                                                      scalar=neg_eG[:, cols[u]:cols[u] + 1], in1=v_tok[:, u, :],
                                                      op0=ALU.mult, op1=ALU.add))
                    for i in range(2):
                        u = 2 * i + 1
                        ins = dve.tensor_scalar(B_in[:, i, :], B_in[:, i, :], beta[:, cols[u]:cols[u] + 1], None,
                                                ALU.mult)
                    ins.then_inc(sem("B1_ready"), 1)
                    dve.wait_ge(sem("q_state_done"), pair + 1)
                    for i in range(2):
                        u = 2 * i + 1
                        ins = dve.tensor_scalar(q_st[:, i, :], bank[6][:, P * i:P * i + P],
                                                eG[:, cols[u]:cols[u] + 1], None, ALU.mult)
                    ins.then_inc(sem("q_state_ready"), 1)
                elif name == "out":
                    dve.wait_ge(sem("o_done"), pair + 1)
                    dve.wait_ge(sem("q_state_ready"), pair + 1)
                    ob = bank[2][:, :].rearrange("p (i c n) -> p i c n", i=2, c=TT)
                    heads = slice(2 * pair, 2 * pair + 2)
                    link(dve.tensor_copy(o_tok[:, 0, heads, :], ob[:, :, 0, :]))
                    dve.tensor_tensor(o_tok[:, 1, heads, :], ob[:, :, 1, :], q_st, ALU.add).then_inc(sem("o_out"), 1)
                    dve.wait_ge(sem("o_out"), pair + 1)
                    for i in range(2):
                        for c in range(TT):
                            o = o_tok[:, c, 2 * pair + i, :]
                            ins = dve.tensor_tensor_reduce(Xm[:, 2 * i + c, :], o, o, 1.0, 0.0, ALU.mult, ALU.add,
                                                           o_sum[:, pair, c, i:i + 1])
                    ins.then_inc(sem("o_sums"), 1)
                    dve.wait_ge(sem("o_rstd"), pair + 1)
                    if pair == 0:
                        dve.wait_ge(sem("small_landed"), 11 * 16)
                    for i in range(2):
                        for c in range(TT):
                            o = o_tok[:, c, 2 * pair + i, :]
                            ins = dve.scalar_tensor_tensor(out=o, in0=o, scalar=o_sum[:, pair, c, i:i + 1],
                                                           in1=o_gain[:, :], op0=ALU.mult, op1=ALU.mult)
                    link(ins)
                    if pair == NH // 2 - 1:
                        gate_out(pair)
            for j in range(4):
                add_h(j, (sem("gdn_out_done"), j + 1), bank[4 + j], "h_ready" if j == 3 else None)
            dve.wait_ge(sem("h_ready"), 1)

            for layer in range(2):
                if layer == 1:
                    norm_sum(3)
                    norm_apply(3)
                    norm_gain(3, 3)

                    def soft_sum(hd):
                        dve.wait_ge(sem("soft_log"), hd + 1)
                        if hd >= 2:
                            dve.wait_ge(sem("rev_done"), hd - 1)
                        s_ = soft[:, hd % 2, :]
                        link(dve.scalar_tensor_tensor(out=s_, in0=bank[hd % 3][:, 0:384], scalar=0.0,
                                                      in1=soft_u[:, hd % 2, :], op0=ALU.min, op1=ALU.subtract,
                                                      reverse1=True))
                        view = s_.rearrange("p (b n) -> p b n", n=P)[:, 0:3:2, :]
                        dve.tensor_tensor(view, view, below[:, :].unsqueeze(1).broadcast_to([P, 2, P]), ALU.mult
                                          ).then_inc(sem("soft_ready"), 1)

                    def out_pair(i):
                        dve.wait_ge(sem("pv_done"), 2 * i + 2)
                        dve.tensor_copy(xT[:, i, :], bank[3 + i % 2][:, 0:T]).then_inc(sem("sbo_ready"), 1)

                    for hd in range(QH + 3):
                        if hd < QH:
                            soft_sum(hd)
                        if hd >= 4 and hd % 2 == 0:
                            out_pair(hd // 2 - 2)
                    for j in range(4):
                        add_h(j, (sem("sb_out_done"), j + 1), bank[(5, 6, 7, 0)[j]], "h_ready" if j == 3 else None)
                    dve.wait_ge(sem("h_ready"), 2)

                n = 1 + 3 * layer
                norm_sum(n)
                norm_apply(n)
                norm_gain(n, n)
                dve.wait_ge(sem("logits_done"), layer + 1)
                lg = bank[4][:, 0:72].rearrange("p (c e) -> p c e", c=TT)
                bias = b_rt[:, layer:layer + 1, :].broadcast_to([P, TT, NG + NE])
                grp, shift, gexp, eq4, hot4 = (rt[:, i, :, 0:NG] for i in (0, 1, 2, 3, 4))
                elog, masked, hot1, masked2, hot2, chosen, cand = (rt[:, i] for i in (5, 6, 7, 8, 10, 9, 11))
                sm = [rt[:, i, :, j:j + 1] for i in (12, 13) for j in range(4)]
                m1, m2, diff, ediff = (rt[:, 14, :, j:j + 1] for j in (0, 3, 1, 2))
                gmax, gsum, gp, c1, w1, w2, pos1, pos2 = sm
                link(dve.tensor_tensor(grp, lg[:, :, 0:NG], bias[:, :, 0:NG], ALU.add))
                link(dve.tensor_tensor(elog, lg[:, :, NG:], bias[:, :, NG:], ALU.add))
                link(dve.tensor_reduce(gmax, grp, AX_X, ALU.max))
                dve.tensor_tensor(shift, grp, gmax.broadcast_to([P, TT, NG]), ALU.subtract
                                  ).then_inc(sem("group_shift"), 1)

                def first_max(hot, vals, m, width):
                    cd = cand[:, :, 0:width]
                    link(dve.tensor_tensor(cd, vals, m.broadcast_to([P, TT, width]), ALU.is_equal))
                    link(dve.tensor_tensor(cd, cd, rev_idx[:, 0:width].unsqueeze(1).broadcast_to([P, TT, width]),
                                           ALU.mult))
                    link(dve.tensor_reduce(c1, cd, AX_X, ALU.max))
                    link(dve.tensor_tensor(hot, cd, c1.broadcast_to([P, TT, width]), ALU.is_equal))

                first_max(hot4, grp, gmax, NG)
                link(dve.tensor_scalar(eq4, hot4, -1.0, BIG, ALU.add, ALU.mult))
                link(dve.tensor_copy(masked.rearrange("p c (g e) -> p c g e", g=NG),
                                     hot4.unsqueeze(3).broadcast_to([P, TT, NG, EPG])))
                link(dve.tensor_tensor(masked, masked, elog, ALU.mult))
                link(dve.tensor_copy(cand.rearrange("p c (g e) -> p c g e", g=NG),
                                     eq4.unsqueeze(3).broadcast_to([P, TT, NG, EPG])))
                link(dve.tensor_tensor(masked, masked, cand, ALU.add))
                link(dve.tensor_reduce(m1, masked, AX_X, ALU.max))
                first_max(hot1, masked, m1, NE)
                link(dve.scalar_tensor_tensor(out=masked2, in0=hot1, scalar=-3 * BIG, in1=masked, op0=ALU.mult,
                                              op1=ALU.add))
                link(dve.tensor_reduce(m2, masked2, AX_X, ALU.max))
                first_max(hot2, masked2, m2, NE)
                dve.tensor_tensor(chosen, hot1, hot2, ALU.add).then_inc(sem("chosen"), 1)
                dve.tensor_tensor(diff, m2, m1, ALU.subtract).then_inc(sem("pair_diff"), 1)
                dve.wait_ge(sem("group_exp"), layer + 1)
                link(dve.tensor_reduce(gsum, gexp, AX_X, ALU.add))
                link(dve.reciprocal(gp, gsum))
                dve.wait_ge(sem("pair_exp"), layer + 1)
                link(dve.tensor_scalar(w2, ediff, 1.0, None, ALU.add))
                link(dve.reciprocal(w1, w2))
                link(dve.tensor_tensor(w1, w1, gp, ALU.mult))
                link(dve.tensor_tensor(w2, w1, ediff, ALU.mult))
                link(dve.tensor_tensor(cw[:, :, :], hot1, w1.broadcast_to([P, TT, NE]), ALU.mult))
                link(dve.tensor_tensor(cand, hot2, w2.broadcast_to([P, TT, NE]), ALU.mult))
                link(dve.tensor_tensor(cw_over[:, :, :], cw[:, :, :], cand, ALU.add))
                dve.wait_ge(sem("counts_done"), layer + 1)
                link(dve.tensor_copy(rank[:, :, :].rearrange("p c e -> p (c e)"), bank[5][:, 0:64]))
                link(dve.tensor_reduce(m1[:, 0, :], bank[5][:, 64:96], AX_X, ALU.max))
                link(dve.tensor_scalar(over_i[:, :], m1[:, 0, :], float(CAP), None, ALU.is_gt))
                link(dve.tensor_scalar(cand, rank[:, :, :], float(CAP), None, ALU.is_lt))
                link(dve.tensor_tensor(cw[:, :, :], cw_over[:, :, :], cand, ALU.mult))
                link(dve.tensor_tensor(cw_over[:, :, :], cw_over[:, :, :], cw[:, :, :], ALU.subtract))
                dve.wait_ge(sem("offsets_done"), layer + 1)
                off = masked[:, 0, :]
                link(dve.tensor_copy(off, bank[7][:, 0:NE]))
                link(dve.tensor_copy(off_i[:, :], off))
                link(dve.tensor_tensor(cand, rank[:, :, :], off.unsqueeze(1).broadcast_to([P, TT, NE]), ALU.add))
                link(dve.tensor_tensor(hot1, hot1, cand, ALU.mult))
                link(dve.tensor_tensor(hot2, hot2, cand, ALU.mult))
                link(dve.tensor_reduce(pos1, hot1, AX_X, ALU.add))
                dve.tensor_reduce(pos2, hot2, AX_X, ALU.add).then_inc(sem("routed"), 1)
                dve.wait_ge(sem("routed"), layer + 1)
                for c in range(TT):
                    link(dve.tensor_scalar(one_hot[:, c, :], iota[:, :], pos1[:, c, :], None, ALU.is_equal))
                    ins = dve.scalar_tensor_tensor(out=one_hot[:, c, :], in0=iota[:, :], scalar=pos2[:, c, :],
                                                   in1=one_hot[:, c, :], op0=ALU.is_equal, op1=ALU.add)
                    if c == 0:
                        link(ins)
                ins.then_inc(sem("one_hot_ready"), 1)
                for k in range(1, KT, 2):
                    dve.wait_ge(sem("gather_done"), KT * layer + k + 1)
                    dve.tensor_scalar(xs[:, k, 0:SLOTS], bank[k % 4][:, :], gains[:, n, k:k + 1], None, ALU.mult
                                      ).then_inc(sem("xs_dve"), 1)
                def scatter_mat(e, used):
                    if used is not None:
                        dve.wait_ge(sem("tr_done"), used)
                    for c in range(TT):
                        for x in range(2):
                            ins = dve.tensor_scalar(rw[:, c, CAP * x:CAP * x + CAP], iota[:, 0:CAP],
                                                    rank[:, c, bass.ds(e + x, 1)], cw[:, c, bass.ds(e + x, 1)],
                                                    ALU.is_equal, ALU.mult)
                    ins.then_inc(sem("rw_ready"), 1)

                def hidden(x, done):
                    dve.wait_ge(sem("sg_ready"), done)
                    dve.tensor_tensor(hh[64:128, x, :], bank[4 + x][64:128, 0:FE], sg[64:128, x, :], ALU.mult
                                      ).then_inc(sem("hh_ready"), 1)

                def rows_out(a, done, used):
                    dve.wait_ge(sem("down_done"), done)
                    if used is not None:
                        dve.wait_ge(sem("scat_done"), used)
                    dve.tensor_copy(ye[:, a, :], bank[7][:, :]).then_inc(sem("ye_ready"), 1)

                q0 = NE // 2 * layer
                for b in range(2):
                    q = q0 + b
                    scatter_mat(2 * b, q if q else None)
                    hidden(0, 2 * q + 1)
                    hidden(1, 2 * q + 2)
                    if b:
                        for a in range(2):
                            rows_out(a, 2 * q - 1 + a, 2 * q - 3 + a if q > 1 else None)
                with dve.Fori(1, NE // RING) as i:
                    for b in range(2):
                        scatter_mat(i * RING + 2 * b, i * 2 + (q0 + b))
                        hidden(0, i * 4 + (2 * (q0 + b) + 1))
                        hidden(1, i * 4 + (2 * (q0 + b) + 2))
                        for a in range(2):
                            rows_out(a, i * 4 + (2 * (q0 + b) - 1 + a), i * 4 + (2 * (q0 + b) - 3 + a))
                end = q0 + NE // 2
                for a in range(2):
                    rows_out(a, 2 * end - 1 + a, 2 * end - 3 + a)
                dve.wait_ge(sem("scat_done"), 2 * end)
                for j in range(4):
                    c, a = divmod(j, 2)
                    view = h[:, c, HALF * a:HALF * a + HALF]
                    ins = dve.tensor_tensor(view, bank[j][:, :], view, ALU.add)
                    if j < 3:
                        link(ins)
                ins.then_inc(sem("moe_acc"), 1)
                dve.wait_ge(sem("moe_acc"), layer + 1)

                flag = dve.value_load(over_i[0:1, 0:1], min_val=0, max_val=1)
                with dve.If(flag > 0):
                    done = sem(f"over_step{layer}")
                    dve.tensor_copy(over_col[:, 0:1], cw_over[:, 0, 0:1]).then_inc(sem(f"over_free{layer}"), 1)
                    dve.tensor_copy(over_col[:, 1:2], cw_over[:, 1, 0:1]).then_inc(sem(f"over_hid{layer}"), 1)
                    with dve.Fori(0, NE) as e:
                        dve.wait_ge(sem(f"over_free{layer}"), e + 1)
                        for f in range(2):
                            dve.wait_ge(sem(f"over_silu{layer}"), e * 2 + (f + 1))
                            dve.tensor_tensor(over_g[:, f, :], bank[5][:, 0:T], over_g[:, f, :], ALU.mult
                                              ).then_inc(sem(f"over_hid{layer}"), 1)
                        for c in range(TT):
                            dve.tensor_copy(over_col[:, c:c + 1], cw_over[:, c, bass.ds(e, 1)]).then_inc(done, 1)
                        dve.wait_ge(sem(f"over_down{layer}"), e + 1)
                        for j in range(4):
                            c, a = divmod(j, 2)
                            view = h[:, c, HALF * a:HALF * a + HALF]
                            dve.wait_ge(done, e * 5 + (j + 2))
                            ins = dve.scalar_tensor_tensor(out=view, in0=bank[j][:, :], scalar=over_col[:, c:c + 1],
                                                           in1=view, op0=ALU.mult, op1=ALU.add)
                            if j < 3:
                                ins.then_inc(done, 1)
                        ins.then_inc(sem(f"over_free{layer}"), 1)
                    dve.wait_ge(sem(f"over_free{layer}"), NE + 1)

                n = 2 + 3 * layer
                norm_sum(n, tiles=range(TT))
                norm_apply(n)
                norm_gain(n, n)
                for j in range(4):
                    half, c = divmod(j, 2)
                    dve.wait_ge(sem("gate_ready"), 4 * layer + j + 1)
                    dve.wait_ge(sem("ple_emb_done"), 4 * layer + j + 1)
                    link(dve.tensor_tensor(gate[:, j, :], bank[4 + j][:, :], gate[:, j, :], ALU.mult))
                    view = h[:, c, HALF * half:HALF * half + HALF]
                    dve.tensor_tensor(view, view, gate[:, j, :], ALU.add).then_inc(sem("ple_h"), 1)
                dve.wait_ge(sem("ple_h"), 4 * layer + 4)
            norm_sum(6, tiles=range(TT))
            dve.wait_ge(sem("norm_rstd"), 7)
            dve.wait_ge(sem("fin_gain_landed"), 16)
            for c in range(TT):
                dve.scalar_tensor_tensor(out=fin_out[:, c, :], in0=h[:, c, :], scalar=rstd[:, c:c + 1], in1=fin_gain,
                                         op0=ALU.mult, op1=ALU.mult).then_inc(sem("fin_ready"), 1)


_INS = ["x", "p", "attn_norm", "moe_norm", "ple_norm", "gdn_w_in", "gdn_conv", "gdn_a_log", "gdn_dt_bias",
        "gdn_o_norm", "gdn_w_out", "kv_norm", "w_kv", "sb_w_q", "sb_w_out", "moe_w_group", "moe_b_group",
        "moe_w_expert", "moe_b_expert", "moe_w_gate", "moe_w_up", "moe_w_down", "ple_w_gate", "ple_w_proj",
        "final_norm"]
_OUTS = [((1, T, D), "float32")]


def kernel(**inputs):
    import numpy as _np
    import concourse.bacc as _bacc
    from concourse import mybir as _mybir
    from concourse.bass_utils import run_bass_kernel_spmd as _run

    nc = _bacc.Bacc("TRN2", target_bir_lowering=False, num_devices=1)
    arrays, args = {}, []
    for name in _INS:
        a = _np.ascontiguousarray(inputs[name])
        arrays[f"in_{name}_dram"] = a
        args.append(nc.dram_tensor(f"in_{name}_dram", a.shape, _mybir.dt.from_np(a.dtype), kind="ExternalInput").ap())
    for i, (shape, dtype) in enumerate(_OUTS):
        dt = _mybir.dt.from_np(_np.dtype(dtype))
        args.append(nc.dram_tensor(f"out_{i}_dram", shape, dt, kind="ExternalOutput").ap())
    yoco_kernel(nc, *args)
    r = _run(nc, [arrays], core_ids=[0])
    got = tuple(r.results[0][f"out_{i}_dram"] for i in range(len(_OUTS)))
    return got[0]
```

```python
from contextlib import ExitStack

import concourse.bass as bass
from concourse import mybir
from concourse.alu_op_type import AluOpType as ALU

ACT = mybir.ActivationFunctionType
F32 = mybir.dt.float32
F32R = mybir.dt.float32r
I32 = mybir.dt.int32
AX_X = mybir.AxisListType.X

P = 128
T = 256
TT = T // P
D = 1024
KT = D // P
HALF = 512
NH, DH = 8, 128
CONV = 4
QH, KVH, SD = 16, 4, 64
NG, NE, FE = 4, 32, 256
EPG = NE // NG
CAP = 64
SLOTS = 2 * T
SPAD = SLOTS + CAP
RING = 4
PAIRS = NE // 2
RING_PAIRS = 3
FILLS = [len(range(g, PAIRS, RING_PAIRS)) for g in range(RING_PAIRS)]
OUT_BANKS = (0, 1, 4, 6)
HEAD_BANKS = (0, 1, 2, 5)
Q_BANKS = (3, 6)
PV_BANKS = (4, 7)
SB_BANKS = (0, 5, 6, 7)
EMB_BANKS = (0, 1, 2, 7)
PLE = 256
EPS = 1e-6
BIG = 1e30
LEVELS = [1 << n for n in range(7)]

CHUNKS = {"qk0": 0, "v0": 1, "qk1": 2, "qk2": 0, "v1": 1, "qk3": 2, "z0": 0, "z1": 1, "pp0": 2, "go0": 0, "go1": 1,
          "pg0.0": 0, "pg0.1": 1, "kv": 0, "sq0": 1, "sq1": 2, "so0": 0, "so1": 1, "pp1": 2, "pg1.0": 0, "pg1.1": 1}
ORDER = list(CHUNKS)
WSLOTS = 3



def gdn_plan():
    tiles = 3 * NH + 4
    stream = [("mm", j, k) for j in range(tiles) for k in range(KT)]
    plan, sent = [], 0

    def fill(n):
        nonlocal sent
        plan.extend(stream[sent:sent + n])
        sent = min(sent + n, len(stream))

    def fill_to(j):
        fill(max(0, j * KT - sent))

    pairs = NH // 2
    fill(12)
    plan.append(("cum", 0, 0))
    fill_to(6)
    plan.append(("silu", 0, 0))
    fill(10)
    plan.append(("norm", 0, 0))
    fill(8)
    plan.append(("gram", 0, 0))
    fill(4)
    plan.append(("flip", 0, 0))
    fill(4)
    for pair in range(pairs - 1):
        for level in range(1, len(LEVELS)):
            plan.append(("half", pair, level))
            if level == 5:
                plan.append(("silu", pair + 1, 0))
                fill(8)
            fill(2)
            if level == 1:
                plan.append(("flip_a", pair, 0))
            plan.append(("full", pair, level))
            fill(2)
            if level == 4:
                fill_to(6 * (pair + 2))
        fill(0)
        plan.append(("new0", pair, 0))
        plan.append(("norm", pair + 1, 0))
        for name in ("state", "read", "new1", "out"):
            fill(2)
            plan.append((name, pair, 0))
        fill(1)
        plan.append(("gram", pair + 1, 0))
        fill(4)
        plan.append(("flip", pair + 1, 0))
        fill(4)
    pair = pairs - 1

    def outputs(*items):
        plan.extend(("w_out", p, q) for p, q in items)

    for level in range(1, len(LEVELS) - 1):
        plan.append(("half", pair, level))
        fill(1)
        if level == 1:
            plan.append(("flip_a", pair, 0))
        plan.append(("full", pair, level))
        fill(1)
        if level == 2:
            fill_to(3 * NH + 2)
            plan.append(("silu_z", 0, 0))
            fill(3)
    fill_to(tiles)
    plan.append(("turn", 0, 0))
    plan.append(("half", pair, len(LEVELS) - 1))
    outputs((0, 0), (0, 1))
    plan.append(("turn", 1, 0))
    plan.append(("full", pair, len(LEVELS) - 1))
    plan.append(("silu_z", 1, 0))
    outputs((1, 0), (1, 1))
    plan.append(("new0", pair, 0))
    plan.append(("turn", 2, 0))
    outputs((0, 2))
    plan.append(("state", pair, 0))
    outputs((1, 2), (2, 0))
    plan.append(("read", pair, 0))
    outputs((2, 1))
    plan.append(("new1", pair, 0))
    outputs((2, 2))
    plan.append(("out", pair, 0))
    outputs((0, 3), (1, 3), (2, 3))
    plan.append(("turn", pair, 0))
    outputs((3, 0), (3, 1), (3, 2), (3, 3))
    return plan


def tile_of(j):
    pair, i = divmod(j, 6)
    kind, head = divmod(i, 2)
    if kind < 2:
        return f"qk{pair}", 256 * kind + 128 * head, 8 * kind + 2 * pair + head
    return f"v{pair // 2}", 256 * (pair % 2) + 128 * head, 16 + 2 * pair + head


def yoco_kernel(nc, x, p, attn_norm, moe_norm, ple_norm, gdn_w_in, gdn_conv, gdn_a_log, gdn_dt_bias,
                gdn_o_norm, gdn_w_out, kv_norm, w_kv, sb_w_q, sb_w_out, moe_w_group, moe_b_group,
                moe_w_expert, moe_b_expert, moe_w_gate, moe_w_up, moe_w_down, ple_w_gate, ple_w_proj,
                final_norm, out):
    ctx = ExitStack()
    with ctx:
        def sb(name, shape, dt=F32):
            return ctx.enter_context(nc.sbuf_tensor(name, shape, dt))

        def rounded(name, shape):
            with nc.sbuf_tensor(name, shape, F32R) as t:
                return t

        sems = {}

        def sem(name):
            if name not in sems:
                sems[name] = ctx.enter_context(nc.semaphore(name))
            return sems[name]

        bank = [ctx.enter_context(nc.psum_tensor(f"bank{i}", [P, HALF], F32)) for i in range(8)]

        moe_w = sb("moe_w", [P, RING, 3, KT * FE])
        wring = sb("wring", [P, WSLOTS, KT * HALF])
        h = sb("h", [P, TT, D])
        xh_part = rounded("xh_part", [P, TT, KT, P])
        xh = sb("xh", [P, TT, KT, P])
        xl_part = rounded("xl_part", [P, TT, KT, P])
        xT = sb("xT", [P, KT, T])
        region = sb("region", [P, KT * SPAD])
        one_hot = rounded("one_hot", [P, TT, SLOTS])
        scr = sb("scr", [P, 3072])
        ident = sb("ident", [P, P])
        upper = sb("upper", [P, P])
        below = sb("below", [P, P])
        lower = sb("lower", [P, P])
        ones = sb("ones", [P, P])
        iota = sb("iota", [P, SLOTS])
        rev_idx = sb("rev_idx", [P, NE])
        gains = sb("gains", [P, 7, KT])
        w_ab = sb("w_ab", [P, KT, 2 * NH])
        w_rt = sb("w_rt", [P, KT, NG + NE])
        b_rt = sb("b_rt", [P, 2, NG + NE])
        ab_row = sb("ab_row", [P, 2, NH])
        o_gain = sb("o_gain", [P, DH])
        half_neg = sb("half_neg", [P, 2 * NH])
        stat = sb("stat", [P, 2])
        rstd = sb("rstd", [P, 2])
        decay = sb("decay", [P, 10, 2 * NH])
        rank = sb("rank", [P, TT, NE])
        cw = sb("cw", [P, TT, NE])
        cw_over = sb("cw_over", [P, TT, NE])
        off_i = sb("off_i", [P, NE], I32)
        over_i = sb("over_i", [P, 1], I32)
        over_col = sb("over_col", [P, TT])
        eps_t = sb("eps_t", [P, 2])

        slot2 = moe_w[:, 2, :, :].rearrange("p a n -> p (a n)")
        slot3 = moe_w[:, 3, :, :].rearrange("p a n -> p (a n)")
        qkvT = slot3.rearrange("p (n t) -> p n t", t=T)
        zs = slot2[:, 0:2048].rearrange("p (c n) -> p c n", c=TT)
        o_tok = slot2[:, 2048:4096].rearrange("p (c h n) -> p c h n", c=TT, h=NH)
        sq = slot2[:, 4096:5120]
        blk = slot2[:, 5120:5120 + 7 * P].rearrange("p (n q) -> p n q", q=P)
        mats = region[:, 0:9 * 512].rearrange("p (m n q) -> p m n q", m=9, n=4)
        Lm, Am, LTm, ATm, Tm, Zm, Xm, Dm, LMm = (mats[:, i] for i in range(9))
        v_tok = scr[:, 0:512].rearrange("p (u n) -> p u n", u=4)
        k_tok = scr[:, 512:768].rearrange("p (u n) -> p u n", u=2)
        S_st = scr[:, 768:1024].rearrange("p (u n) -> p u n", u=2)
        B_in = scr[:, 1024:1280].rearrange("p (u n) -> p u n", u=2)
        v_new = scr[:, 1280:1792].rearrange("p (u n) -> p u n", u=4)
        q_st = scr[:, 1792:2048].rearrange("p (u n) -> p u n", u=2)
        conv_rows = scr[0:CONV * 24, 2560:2688]
        conv_w = scr[:, 2688:2784].rearrange("p (t n) -> p t n", t=CONV)
        o_sum = scr[:, 2784:2800].rearrange("p (n c i) -> p n c i", c=TT, i=2)
        xs = region[:, :].rearrange("p (k s) -> p k s", k=KT)
        xe = scr[:, 0:1024].rearrange("p (b k s) -> p b k s", b=2, k=KT)
        rw = scr[:, 1024:1280].rearrange("p (c s) -> p c s", c=TT)
        sg = scr[:, 1280:1792].rearrange("p (b f) -> p b f", b=2)
        hh = scr[:, 1792:2304].rearrange("p (b f) -> p b f", b=2)
        xh_flat = xh[:, :, :, :].rearrange("p c k q -> p (c k q)")
        ye = xh_flat[:, 0:1024].rearrange("p (a n) -> p a n", a=2)
        hr = xh_flat[:, 1024:2048].rearrange("p (b n) -> p b n", b=2)
        rt = scr[:, 1024:3072].rearrange("p (n c e) -> p n c e", c=TT, e=NE)
        xkvT = region[:, 0:2048].rearrange("p (k t) -> p k t", k=KT)
        qT = region[:, 2048:4096].rearrange("p (k t) -> p k t", k=KT)
        kT = scr[:, 0:1024].rearrange("p (g t) -> p g t", g=KVH)
        v_sb = scr[:, 1024:1536].rearrange("p (c n) -> p c n", c=TT)
        soft = xkvT.rearrange("p k t -> p (k t)")[:, 0:1152].rearrange("p (b n) -> p b n", b=3)
        soft_u = xkvT.rearrange("p k t -> p (k t)")[:, 1152:1920].rearrange("p (b n) -> p b n", b=2)
        attn = scr[:, 1536:3072].rearrange("p (b n) -> p b n", b=4)
        emb = wring[:, CHUNKS["pp0"], 2 * D:4 * D].rearrange("p (n q) -> p n q", n=4)
        p_tok = emb[:, 2, :].rearrange("p (c n) -> p c n", c=TT)
        pT = emb[:, 3, :].rearrange("p (j t) -> p j t", j=2)
        gate = scr[:, 1024:3072].rearrange("p (n q) -> p n q", n=4)
        fin_gain = region[:, 0:D]
        fin_out = region[:, D:3 * D].rearrange("p (c n) -> p c n", c=TT)

        def gu_slot(s):
            if s < RING:
                return moe_w[:, s, 0:2, :]
            return wring[:, s - RING, :].rearrange("p (a n) -> p a n", a=2)

        def d_slot(s):
            if s < RING:
                return moe_w[:, s, 2, :]
            return xT[:, :, :].rearrange("p k t -> p (k t)") if s == RING else wring[:, CHUNKS["pp0"], 0:2 * D]

        def dchunk(name):
            slot = wring[:, CHUNKS[name], :]
            wide = slot.rearrange("p (k n) -> p k n", k=KT)

            def by_row(w):
                return w.rearrange("(p k) n -> p k n", k=KT)

            def by_tile(w):
                return w.rearrange("(k p) n -> p k n", p=P)
            if name[:2] == "qk":
                n = int(name[2])
                w = by_row(gdn_w_in[0])
                return [(wide[:, :, 256 * a:256 * a + 256], w[:, :, D * a + 256 * n:D * a + 256 * n + 256])
                        for a in range(2)]
            half = int(name[-1])
            cols = slice(HALF * half, HALF * half + HALF)
            if name[0] == "v":
                return [(wide, by_row(gdn_w_in[0])[:, :, 2 * D + HALF * half:2 * D + HALF * half + HALF])]
            if name[0] == "z":
                return [(wide, by_row(gdn_w_in[0])[:, :, 3 * D + HALF * half:3 * D + HALF * half + HALF])]
            if name[:2] == "go":
                return [(wide, by_tile(gdn_w_out[0])[:, :, cols])]
            if name[:2] == "pg":
                return [(wide, by_row(ple_w_gate[int(name[2])])[:, :, cols])]
            if name[:2] == "pp":
                return [(slot[:, 0:2 * D].rearrange("p (j n) -> p j n", j=2),
                         ple_w_proj[half].rearrange("(j p) n -> p j n", p=P))]
            if name[:2] == "sq":
                return [(wide, by_row(sb_w_q[0])[:, :, cols])]
            if name[:2] == "so":
                return [(wide, by_tile(sb_w_out[0])[:, :, cols])]
            raise ValueError(name)

        def chunk_parts(name):
            if name == "kv":
                slot = wring[:, CHUNKS[name], :]
                return [(slot.rearrange("p (k n) -> p k n", k=KT), w_kv.rearrange("(p k) n -> p k n", k=KT))]
            return dchunk(name)

        def chunk(name):
            return wring[:, CHUNKS[name], :].rearrange("p (k n) -> p k n", k=KT)

        landed, slot_count = {}, [0] * WSLOTS
        for name, at in CHUNKS.items():
            slot_count[at] += 16 * len(chunk_parts(name))
            landed[name] = slot_count[at]

        def wait_chunk(eng, name):
            eng.wait_ge(sem(f"chunk_landed{CHUNKS[name]}"), landed[name])

        def chunk_used(name):
            if name[:2] == "qk":
                return sem("proj_done"), 6 * int(name[2]) + 4
            if name[0] == "v":
                return sem("proj_done"), 12 * int(name[1]) + 12
            if name[0] == "z":
                return sem("proj_done"), 3 * NH + 2 * int(name[1]) + 2
            if name[:2] == "go":
                return sem("gdn_out_done"), 4
            if name[:2] == "pg":
                return sem("ple_gate_done"), 4 * int(name[2]) + int(name[4]) + 3
            if name[:2] == "pp":
                return sem("h_tile"), 6 + 6 * int(name[2])
            if name == "kv":
                return sem("kv_done"), 4
            if name[:2] == "sq":
                return sem("sbq_done"), 4 * int(name[2]) + 4
            return sem("sb_out_done"), int(name[2]) + 3

        def chain_of(eng, name):
            count = [0]

            def link(ins):
                count[0] += 1
                ins.then_inc(sem(name), 1)
                eng.wait_ge(sem(name), count[0])
            return link

        def over_w(n):
            return (region[:, 0:2048], region[:, 2048:4096], xh_flat)[n]

        over_g = scr[:, 512:1024].rearrange("p (f t) -> p f t", f=2)

        plan = gdn_plan()
        block = ctx.enter_context(nc.Block())

        @block.sync
        def _(sp):
            def load_chunk(name):
                if name[:2] == "pg":
                    sp.wait_ge(sem("gu_done"), NE * int(name[2]) + 2 * PAIRS - 2)
                before = [other for other in ORDER[:ORDER.index(name)] if CHUNKS[other] == CHUNKS[name]]
                if before:
                    sp.wait_ge(*chunk_used(before[-1]))
                for dst, src in chunk_parts(name):
                    sp.dma_start(dst, src).then_inc(sem(f"chunk_landed{CHUNKS[name]}"), 16)
                if name[:2] == "pp":
                    sp.dma_start(p_tok, p[int(name[2]), 0].rearrange("(c p) d -> p c d", p=P)
                                 ).then_inc(sem("p_landed"), 16)

            def load_expert(layer, e, slot, which):
                for n in which:
                    w = (moe_w_gate, moe_w_up, moe_w_down)[n]
                    flat = w[layer].rearrange("g e a b -> (g e) (a b)").rearrange("e (p n) -> e p n", p=P)
                    src = flat[e, :, :] if isinstance(e, int) else flat[bass.ds(e, 1), :, :].rearrange(
                        "e p n -> (e p) n")
                    if n < 2:
                        sp.dma_start(gu_slot(slot)[:, n, :], src).then_inc(sem(f"expert_gu{slot}"), 16)
                    else:
                        sp.dma_start(d_slot(slot), src).then_inc(sem(f"expert_d{slot}"), 16)

            def load_pair(layer, q, third, gu_used, d_used):
                for m in range(2):
                    sp.wait_ge(sem("gu_done"), gu_used + m)
                    load_expert(layer, q * 2 + m, 2 * third + m, (0, 1))
                sp.wait_ge(sem("down_done"), d_used)
                for m in range(2):
                    load_expert(layer, q * 2 + m, 2 * third + m, (2,))

            def load_experts(layer):
                load_pair(layer, 3, 0, NE * layer + 1, NE * layer + 2)
                with sp.Fori(0, 2) as i:
                    for j in range(4, 10):
                        before = i * 12 + (NE * layer + 2 * (j - RING_PAIRS))
                        load_pair(layer, i * 6 + j, j % RING_PAIRS, before + 1, before + 2)

            sp.dma_start(h[:, :, :], x[0].rearrange("(c p) d -> p c d", p=P)).then_inc(sem("x_landed"), 16)
            first, small = sem("first_landed"), sem("small_landed")

            def load_gain(i, g):
                sp.dma_start(gains[:, i, :], g.rearrange("(p k) -> p k", k=KT)).then_inc(small if i else first, 16)

            load_gain(0, attn_norm[0])
            sp.dma_start(conv_rows, gdn_conv[0].rearrange("t (n c) -> (t n) c", c=P)).then_inc(first, 16)
            sp.dma_start(w_ab[:, :, :], gdn_w_in[0].rearrange("(p k) n -> p k n", k=KT)[:, :, 4 * D:4 * D + 16]
                         ).then_inc(first, 16)
            for i, row in enumerate((gdn_a_log, gdn_dt_bias)):
                sp.dma_start(ab_row[:, i, :], row.broadcast_to([P, NH])).then_inc(first, 16)
            for name in ORDER[:WSLOTS]:
                load_chunk(name)
            for i, g in enumerate((moe_norm[0], ple_norm[0], attn_norm[1], moe_norm[1], ple_norm[1], kv_norm)):
                load_gain(i + 1, g)
            sp.dma_start(o_gain[:, :], gdn_o_norm.broadcast_to([P, DH])).then_inc(small, 16)
            for i in range(2):
                sp.dma_start(b_rt[:, i, 0:NG], moe_b_group[i:i + 1, :].broadcast_to([P, NG])).then_inc(small, 16)
                sp.dma_start(b_rt[:, i, NG:], moe_b_expert[i:i + 1, :].broadcast_to([P, NE])).then_inc(small, 16)

            def load_router(layer):
                rtr = sem("router_landed")
                sp.dma_start(w_rt[:, :, 0:NG], moe_w_group[layer].rearrange("(p k) n -> p k n", k=KT)
                             ).then_inc(rtr, 16)
                sp.dma_start(w_rt[:, :, NG:], moe_w_expert[layer].rearrange("(p k) n -> p k n", k=KT)
                             ).then_inc(rtr, 16)

            load_router(0)
            load_expert(0, 0, 0, range(3))
            load_expert(0, 1, 1, range(3))
            for name in ORDER[WSLOTS:ORDER.index("go1") + 1]:
                load_chunk(name)
            sp.wait_ge(sem("oT_flip_done"), 4)
            load_expert(0, 2, 2, range(3))
            load_expert(0, 3, 3, range(3))
            for layer in range(2):
                if layer == 0:
                    sp.wait_ge(*chunk_used("go1"))
                else:
                    sp.wait_ge(*chunk_used("so1"))
                for m in range(2):
                    load_expert(layer, 4 + m, 4 + m, (0, 1))
                sp.wait_ge(sem("ple_emb_done"), 4 * layer + 4)
                sp.wait_ge(sem("gather_done"), KT * (layer + 1))
                for m in range(2):
                    load_expert(layer, 4 + m, 4 + m, (2,))
                load_experts(layer)
                load_chunk(f"pg{layer}.0")
                load_chunk(f"pg{layer}.1")
                sp.wait_ge(sem("routed"), layer + 1)
                flag = sp.value_load(over_i[0:1, 0:1], min_val=0, max_val=1)
                with sp.If(flag > 0):
                    with sp.Fori(0, NE) as e:
                        sp.wait_ge(sem(f"over_free{layer}"), e + 1)
                        for n, w in enumerate((moe_w_gate, moe_w_up, moe_w_down)):
                            flat = w[layer].rearrange("g e a b -> (g e) (a b)").rearrange("e (p n) -> e p n", p=P)
                            sp.dma_start(over_w(n), flat[bass.ds(e, 1), :, :].rearrange("e p n -> (e p) n")
                                         ).then_inc(sem(f"over_landed{layer}"), 16)
                if layer == 0:
                    load_router(1)
                    for g in range(2):
                        load_pair(1, g, g, NE - 1, NE)
                    for name in ORDER[ORDER.index("kv"):ORDER.index("pg1.0")]:
                        load_chunk(name)
            sp.wait_ge(sem("norm_flip"), 24)
            sp.dma_start(fin_gain, final_norm.rearrange("(a n) -> a n", a=1).broadcast_to([P, D])
                         ).then_inc(sem("fin_gain_landed"), 16)
            for j in range(4):
                c, half = divmod(j, 2)
                cols = slice(HALF * half, HALF * half + HALF)
                sp.wait_ge(sem("fin_ready"), j + 1)
                sp.dma_start(out[0].rearrange("(c p) d -> p c d", p=P)[:, c, cols], fin_out[:, c, cols]
                             ).then_inc(sem("out_stored"), 16)
            sp.wait_ge(sem("out_stored"), 4 * 16)

        @block.gpsimd
        def _(pool):
            link = chain_of(pool, "pool_chain")
            for t in (ident, upper, below, lower):
                pool.memset(t[:, :], 0.0 if t is ident else 1.0).then_inc(sem("mask_set"), 1)
            pool.memset(half_neg[:, :], -0.5).then_inc(sem("mask_set"), 1)
            pool.memset(ones[:, :], 1.0).then_inc(sem("mask_set"), 1)
            pool.wait_ge(sem("mask_set"), 6)
            pool.affine_select(out=ident[:, :], in_=ident[:, :], compare_op=ALU.not_equal, fill=1.0, base=0,
                               pattern=[[-1, P]], channel_multiplier=1).then_inc(sem("mask_set"), 1)
            pool.affine_select(out=upper[:, :], in_=upper[:, :], compare_op=ALU.is_ge, fill=0.0, base=0,
                               pattern=[[1, P]], channel_multiplier=-1).then_inc(sem("mask_set"), 1)
            pool.affine_select(out=below[:, :], in_=below[:, :], compare_op=ALU.is_gt, fill=0.0, base=0,
                               pattern=[[1, P]], channel_multiplier=-1).then_inc(sem("mask_set"), 1)
            pool.affine_select(out=lower[:, :], in_=lower[:, :], compare_op=ALU.is_ge, fill=0.0, base=0,
                               pattern=[[-1, P]], channel_multiplier=1).then_inc(sem("mask_set"), 1)

            def rsqrt(dst, src, scale, n, ready):
                link(pool.tensor_scalar(dst, src, scale, EPS, ALU.mult, ALU.add))
                pool.tensor_tensor(dst, dst, half_neg[:, 0:n], ALU.pow).then_inc(ready, 1)

            def norm_scale(n):
                for c in range(TT):
                    pool.wait_ge(sem(f"sums{c}"), n + 1)
                    rsqrt(rstd[:, c:c + 1], stat[:, c:c + 1], 1.0 / D, 1, sem("norm_rstd"))

            pool.wait_ge(sem("mask_set"), 10)
            norm_scale(0)
            for n in range(len(LEVELS)):
                b = LEVELS[n]
                view = blk[:, n, :].rearrange("p (m b) -> p m b", b=b)
                link(pool.memset(blk[:, n, :], 1.0))
                link(pool.affine_select(out=view, in_=view, compare_op=ALU.is_ge, fill=0.0, base=0,
                                        pattern=[[-b, P // b], [0, b]], channel_multiplier=1))
                ins = pool.affine_select(out=view, in_=view, compare_op=ALU.is_ge, fill=0.0, base=b - 1,
                                         pattern=[[b, P // b], [0, b]], channel_multiplier=-1)
                if n < len(LEVELS) - 1:
                    link(ins)
                else:
                    ins.then_inc(sem("blocks_set"), 1)
            iota_i = region[:, 0:SLOTS].bitcast(I32)
            link(pool.iota(iota_i, [[1, SLOTS]], base=0, channel_multiplier=0))
            link(pool.tensor_copy(iota[:, :], iota_i))
            pool.tensor_scalar(rev_idx[:, :], iota[:, 0:NE], -1.0, float(NE), ALU.mult, ALU.add
                               ).then_inc(sem("blocks_set"), 1)
            for pair in range(NH // 2):
                pool.wait_ge(sem("o_sums"), pair + 1)
                cols = o_sum[:, pair, :, :].rearrange("p c i -> p (c i)")
                rsqrt(cols, cols, 1.0 / DH, 4, sem("o_rstd"))

            for layer in range(2):
                if layer == 1:
                    norm_scale(3)
                    for hd in range(QH):
                        pool.wait_ge(sem("attn_exp"), hd + 1)
                        view = attn[:, hd % 4, :].rearrange("p (b n) -> p b n", n=P)[:, 0:3:2, :]
                        pool.tensor_tensor(view, view, below[:, :].unsqueeze(1).broadcast_to([P, 2, P]), ALU.mult
                                           ).then_inc(sem("attn_ready"), 1)
                norm_scale(1 + 3 * layer)
                n = 1 + 3 * layer
                pool.wait_ge(sem("norm_rstd"), 2 * n + 2)
                pool.wait_ge(sem("logits_done"), layer + 1)
                for c in range(TT):
                    pool.wait_ge(sem("xh_gather"), TT * layer + c + 1)
                    whole = region[:, D * c:D * c + D].rearrange("p (k q) -> p k q", k=KT)
                    link(pool.tensor_scalar(whole, h[:, c, :].rearrange("p (q k) -> p k q", k=KT),
                                            rstd[:, c:c + 1], None, ALU.mult))
                    pool.tensor_tensor(xl_part[:, c], whole, xh_part[:, c].bitcast(F32), ALU.subtract
                                       ).then_inc(sem("xl_gather"), 1)
                pool.wait_ge(sem("xl_gather"), TT * layer + 2)
                pool.memset(xs[:, :, SLOTS:], 0.0).then_inc(sem("pad_set"), 1)
                pool.wait_ge(sem("pad_set"), layer + 1)
                pool.wait_ge(sem("xs_act"), 4 * layer + 4)
                pool.wait_ge(sem("xs_dve"), 4 * layer + 4)
                pool.wait_ge(sem("routed"), layer + 1)

                def window(e, buf, base):
                    at = pool.value_load(off_i[0:1, bass.ds(e, 1)], min_val=0, max_val=SLOTS)
                    if base is not None:
                        pool.wait_ge(sem("gu_done"), base)
                    pool.tensor_copy(xe[:, buf, :, :], xs[:, :, bass.ds(at, CAP)]).then_inc(sem("xe_ready"), 1)

                for e in range(RING):
                    window(e, e % 2, NE * layer + e - 1 if e >= 2 else None)
                with pool.Fori(1, NE // RING) as i:
                    for s in range(RING):
                        window(i * RING + s, s % 2, i * RING + (NE * layer + s - 1))
                norm_scale(2 + 3 * layer)
            norm_scale(6)

        @block.scalar
        def _(act):
            link = chain_of(act, "act_chain")

            exp_ln = "natural_log_exp_and_others"

            def norm_sum(n):
                if n:
                    act.wait_ge(sem("h_tile"), 2 * n)
                else:
                    act.wait_ge(sem("x_landed"), 16)
                act.activation(xh[:, 1].rearrange("p k q -> p (k q)"), h[:, 1, :], ACT.Square,
                               accum_out=stat[:, 1:2]).then_inc(sem("sums1"), 1)

            def norm_apply(n):
                act.wait_ge(sem("norm_rstd"), 2 * n + 2)
                act.activation(xh[:, 1], h[:, 1, :].rearrange("p (q k) -> p k q", k=KT), ACT.Copy,
                               scale=rstd[:, 1:2]).then_inc(sem("xh_act"), 1)

            def norm_gain(n, gain, dst):
                for b in (0, 2):
                    act.wait_ge(sem("norm_flip"), 4 * n + b + 1)
                    act.activation(dst[:, 2 * b, :], bank[b][:, 0:T], ACT.Copy, scale=gains[:, gain, 2 * b:2 * b + 1])
                    act.activation(dst[:, 2 * b + 1, :], bank[b][:, T:2 * T], ACT.Copy,
                                   scale=gains[:, gain, 2 * b + 1:2 * b + 2]).then_inc(sem("xT_act"), 1)

            act.preload_act_table_set(exp_ln)
            norm_sum(0)
            norm_apply(0)
            act.wait_ge(sem("first_landed"), 5 * 16)
            norm_gain(0, 0, xT)
            act.wait_ge(sem("start_done"), 1)
            act.activation(conv_w.rearrange("p t n -> p (t n)"), bank[4][:, 0:96], ACT.Copy
                           ).then_inc(sem("conv_ready"), 1)
            act.wait_ge(sem("conv_ready"), 1)
            d = [decay[:, i, :] for i in range(10)]
            act.wait_ge(sem("ab_abs"), 1)
            link(act.activation(d[1], d[1], ACT.Exp, scale=-1.0))
            link(act.activation(d[1], d[1], ACT.Ln, bias=1.0))
            link(act.activation(d[4][:, 0:NH], ab_row[:, 0, :], ACT.Exp))
            act.activation(d[2], d[2], ACT.Exp, scale=-1.0).then_inc(sem("ab_exp"), 1)
            for name, pair, level in plan:
                n = pair * 6 + level - 1
                if name == "mm":
                    j, k = pair, level
                    if k == KT - 1 and j < 3 * NH:
                        ct = tile_of(j)[2]
                        act.wait_ge(sem("proj_done"), j + 1)
                        act.activation(qkvT[:, ct, :], bank[j % 2][:, 0:T], ACT.Copy, scale=conv_w[:, 3, ct:ct + 1]
                                       ).then_inc(sem("conv_first"), 1)
                    elif k == KT - 1:
                        cn, c = divmod(j - 3 * NH, 2)
                        act.wait_ge(sem("proj_done"), j + 1)
                        act.activation(zs[:, c, HALF * cn:HALF * cn + HALF], bank[j % 2][:, :], ACT.Copy
                                       ).then_inc(sem("z_out"), 1)
                elif name == "cum":
                    act.wait_ge(sem("cum_ready"), 1)
                    link(act.activation(d[6], d[5], ACT.Exp))
                    act.activation(d[7], d[7], ACT.Exp).then_inc(sem("decay_exp"), 1)
                elif name == "silu":
                    act.wait_ge(sem("conv_done"), 6 * pair + 6)
                    for first in (0, 8, 16):
                        view = qkvT[:, first + 2 * pair:first + 2 * pair + 2, :]
                        act.activation(view, view, ACT.Silu).then_inc(sem("silu_done"), 1)
                    act.preload_act_table_set(exp_ln)
                    act.wait_ge(sem("silu_done"), 3 * pair + 3)
                    if pair:
                        act.wait_ge(sem("qk_normed"), pair)
                    for a in range(2):
                        act.activation(sq[:, 512 * a:512 * a + 512].rearrange("p (u t) -> p u t", u=2),
                                       qkvT[:, 8 * a + 2 * pair:8 * a + 2 * pair + 2, :], ACT.Square
                                       ).then_inc(sem("squares"), 1)
                elif name == "silu_z":
                    act.wait_ge(sem("z_out"), 2 * pair + 2)
                    view = zs[:, :, HALF * pair:HALF * pair + HALF]
                    act.activation(view, view, ACT.Silu).then_inc(sem("z_ready"), 1)
                elif name == "norm":
                    act.wait_ge(sem("sumsq_done"), pair + 1)
                    act.activation(sq[:, 0:512], bank[2][:, :], ACT.Ln, scale=float(DH), bias=eps_t[:, 0:1]
                                   ).then_inc(sem("norm_ln"), 1)
                    act.activation(sq[:, 512:1024], bank[3][:, :], ACT.Ln, bias=eps_t[:, 1:2]
                                   ).then_inc(sem("norm_ln"), 1)
                    act.wait_ge(sem("norm_ln"), 2 * pair + 2)
                    act.activation(sq, sq, ACT.Exp, scale=-0.5).then_inc(sem("norm_exp"), 1)
                    act.wait_ge(sem("decay_diff"), pair + 1)
                    act.activation(Dm, Dm, ACT.Exp, scale=-1.0).then_inc(sem("decay_mat"), 1)
                elif name == "gram":
                    act.wait_ge(sem("kv_flip_done"), pair + 1)
                    for i in range(2):
                        act.activation(k_tok[:, i, :], bank[4][:, P * i:P * i + P], ACT.Copy,
                                       scale=d[7][:, 2 * pair + i:2 * pair + i + 1]).then_inc(sem("kv_tok"), 1)
                    act.activation(v_tok.rearrange("p u n -> p (u n)"), bank[7][:, :], ACT.Copy
                                   ).then_inc(sem("kv_tok"), 1)
                elif name == "flip":
                    act.wait_ge(sem("Z_ready"), 7 * pair + 1)
                    act.activation(LTm.rearrange("p u n -> p (u n)"), bank[2][:, :], ACT.Copy
                                   ).then_inc(sem("lt_ready"), 1)
                elif name == "flip_a":
                    act.wait_ge(sem("A_flip_done"), pair + 1)
                    act.activation(ATm.rearrange("p u n -> p (u n)"), bank[3][:, :], ACT.Copy
                                   ).then_inc(sem("AT_ready"), 1)
                elif name == "half":
                    act.wait_ge(sem("half_done"), n + 1)
                    act.activation(Xm.rearrange("p u n -> p (u n)"), bank[4][:, :], ACT.Copy
                                   ).then_inc(sem("X_ready"), 1)
                elif name in ("new0", "new1"):
                    first = int(name[3])
                    act.wait_ge(sem(f"{name}_done"), pair + 1)
                    act.activation(v_new[:, first:4:2, :], bank[7][:, 0:256].rearrange("p (u n) -> p u n", u=2),
                                   ACT.Copy).then_inc(sem(f"{name}_ready"), 1)
                elif name == "state":
                    act.wait_ge(sem("state_done"), pair + 1)
                    act.activation(S_st, bank[5][:, 0:256].rearrange("p (u n) -> p u n", u=2), ACT.Copy
                                   ).then_inc(sem("state_ready"), 1)
                elif name == "turn":
                    act.wait_ge(sem("oT_flip_done"), pair + 1)
                    act.activation(xT[:, 2 * pair:2 * pair + 2, :].rearrange("p k t -> p (k t)"),
                                   bank[3][:, :], ACT.Copy).then_inc(sem("oT_ready"), 1)

            act.wait_ge(sem("small_landed"), 11 * 16)
            for layer in range(2):
                if layer == 1:
                    norm_sum(3)
                    norm_apply(3)
                    norm_gain(3, 6, xkvT)
                    norm_gain(3, 3, xT)
                    for c in range(TT):
                        act.wait_ge(sem("kv_done"), c + 1)
                        act.activation(v_sb[:, c, :], bank[4 + c][:, 0:256], ACT.Copy).then_inc(sem("kv_ready"), 1)
                    for g in range(2):
                        act.wait_ge(sem("kv_done"), 3 + g)
                        for a in range(2):
                            for b in range(2):
                                ins = act.activation(kT[64 * b:64 * b + 64, 2 * g + a, :],
                                                     bank[6 + g][64 * a:64 * a + 64, 0:T], ACT.Copy)
                        ins.then_inc(sem("kv_ready"), 1)
                    def softplus(hd):
                        act.wait_ge(sem("z_score"), hd + 1)
                        u = soft_u[:, hd % 2, :]
                        if hd >= 2:
                            act.wait_ge(sem("soft_ready"), hd - 1)
                        link(act.activation(u, bank[HEAD_BANKS[hd % 4]][:, 0:384], ACT.Abs))
                        link(act.activation(u, u, ACT.Exp, scale=-1.0))
                        act.activation(u, u, ACT.Ln, bias=1.0).then_inc(sem("soft_log"), 1)

                    def attn_exp(hd):
                        act.wait_ge(sem("rev_done"), hd + 1)
                        if hd >= 4:
                            act.wait_ge(sem("pv_done"), hd // 2 - 1)
                        act.activation(attn[:, hd % 4, :], bank[HEAD_BANKS[hd % 4]][:, 0:384], ACT.Exp, scale=-1.0
                                       ).then_inc(sem("attn_exp"), 1)

                    def head_step(hd):
                        if hd < QH:
                            softplus(hd)
                        if hd >= 2:
                            attn_exp(hd - 2)

                    act.preload_act_table_set(exp_ln)
                    for i in range(KT):
                        act.wait_ge(sem("sbq_done"), i + 1)
                        act.activation(qT[:, i, :], bank[Q_BANKS[i % 2]][:, 0:T], ACT.Copy, scale=-(SD ** -0.5)
                                       ).then_inc(sem("qT_ready"), 1)
                        if i >= 2:
                            head_step(i - 2)
                    for hd in range(KT - 2, QH + 2):
                        head_step(hd)

                n = 1 + 3 * layer
                norm_sum(n)
                norm_gain(n, n, xT)
                act.wait_ge(sem("p_flip"), layer + 1)
                act.activation(pT.rearrange("p j t -> p (j t)"), bank[5][:, :], ACT.Copy).then_inc(sem("pT_ready"), 1)
                act.wait_ge(sem("norm_rstd"), 2 * n + 2)
                for c in range(TT):
                    act.activation(xh_part[:, c], h[:, c, :].rearrange("p (q k) -> p k q", k=KT), ACT.Copy,
                                   scale=rstd[:, c:c + 1]).then_inc(sem("xh_gather"), 1)
                act.wait_ge(sem("group_shift"), layer + 1)
                act.activation(rt[:, 2, :, 0:NG], rt[:, 1, :, 0:NG], ACT.Exp).then_inc(sem("group_exp"), 1)

                def emb_out(q):
                    act.wait_ge(sem("ple_emb_done"), 4 * layer + q + 1)
                    act.activation(emb[:, q, :], bank[EMB_BANKS[q]][:, :], ACT.Copy).then_inc(sem("emb_out"), 1)

                for q in range(3):
                    emb_out(q)
                act.wait_ge(sem("pair_diff"), layer + 1)
                act.activation(rt[:, 14, :, 2:3], rt[:, 14, :, 1:2], ACT.Exp).then_inc(sem("pair_exp"), 1)
                emb_out(3)
                for k in range(0, KT, 2):
                    act.wait_ge(sem("gather_done"), KT * layer + k + 1)
                    act.activation(xs[:, k, 0:SLOTS], bank[k % 4][:, :], ACT.Copy,
                                   scale=gains[:, 1 + 3 * layer, k:k + 1]).then_inc(sem("xs_act"), 1)

                def gate_silu(x, done, used):
                    act.wait_ge(sem("gu_done"), done)
                    if used is not None:
                        act.wait_ge(sem("hh_ready"), used)
                    act.activation(sg[64:128, x, :], bank[4 + x][0:64, 0:FE], ACT.Silu).then_inc(sem("sg_ready"), 1)

                def turned_out(x, done, used):
                    act.wait_ge(sem("tr_done"), done)
                    if used is not None:
                        act.wait_ge(sem("scat_done"), used)
                    act.activation(hr[:, x, :], bank[6][:, :], ACT.Copy).then_inc(sem("hr_ready"), 1)

                q0 = NE // 2 * layer
                for x in range(2):
                    q = q0 + x
                    gate_silu(0, 2 * q + 1, 2 * q - 1 if q else None)
                    if x:
                        turned_out(0, q, 2 * q - 4 if q > 2 else None)
                    gate_silu(1, 2 * q + 2, 2 * q if q else None)
                with act.Fori(1, NE // RING) as i:
                    for x in range(2):
                        gate_silu(0, i * 4 + (2 * (q0 + x) + 1), i * 4 + (2 * (q0 + x) - 1))
                        turned_out(1 - x, i * 2 + (q0 + x), i * 4 + (2 * (q0 + x) - 4) if x or q0 else
                                   i * 4 + (2 * q0 - 3))
                        gate_silu(1, i * 4 + (2 * (q0 + x) + 2), i * 4 + 2 * (q0 + x))
                turned_out(1, q0 + NE // 2, 2 * (q0 + NE // 2) - 4)

                flag = act.value_load(over_i[0:1, 0:1], min_val=0, max_val=1)
                with act.If(flag > 0):
                    with act.Fori(0, NE) as e:
                        for f in range(2):
                            act.wait_ge(sem(f"over_gu{layer}"), e * 2 + (f + 2))
                            act.activation(over_g[:, f, :], bank[4][:, 0:T], ACT.Silu
                                           ).then_inc(sem(f"over_silu{layer}"), 1)
                    act.wait_ge(sem(f"over_free{layer}"), NE + 1)

                n = 2 + 3 * layer
                norm_sum(n)
                norm_gain(n, n, xT)
                act.wait_ge(sem("norm_rstd"), 2 * n + 2)
                for j in range(4):
                    act.wait_ge(sem("ple_gate_done"), 4 * layer + j + 1)
                    act.activation(gate[:, j, :], bank[j][:, :], ACT.Sigmoid, scale=rstd[:, j // 2:j // 2 + 1]
                                   ).then_inc(sem("gate_ready"), 1)
            norm_sum(6)

        @block.tensor
        def _(pe):
            def turn_tiles(n, src, tile_ready):
                for c in range(TT):
                    pe.wait_ge(*tile_ready[c])
                    for k in range(KT):
                        col = T * (k % 2) + P * c
                        ins = pe.transpose(bank[k // 2][:, col:col + P], src(c, k), ident[:, :])
                        if c == 1 and k % 2:
                            ins.then_inc(sem("norm_flip"), 1)

            def norm_flip(n):
                m = (0, 3).index(n) + 1
                turn_tiles(n, lambda c, k: xh[:, c, k, :], ((sem("xh_dve"), m), (sem("xh_act"), m)))

            def raw_flip(n):
                early = 2 * n if n in (2, 5) else 2 * n - 1
                turn_tiles(n, lambda c, k: h[:, c, k:D:KT], ((sem("h_tile"), early), (sem("h_tile"), 2 * n)))

            def wait_turned(n, k, kv=False):
                before = 2 * (n + (n > 3 or (n == 3 and not kv)))
                if k % 2 == 0:
                    pe.wait_ge(sem(("xT_act", "xT_dve")[k // 2 % 2]), before + k // 4 + 1)

            def by_token(dst, src, w, c, ready, kts=KT, wait=None):
                for k in range(kts):
                    if wait:
                        wait(k)
                    ins = pe.matmul(dst, src[:, k, P * c:P * c + P], w[:, k, :], start=(k == 0),
                                    stop=(k == kts - 1))
                ins.then_inc(ready, 1)

            pe.wait_ge(sem("mask_set"), 10)
            norm_flip(0)
            pe.wait_ge(sem("first_landed"), 5 * 16)
            pe.transpose(bank[4][:, 0:96], conv_rows, ident[0:96, 0:96]).then_inc(sem("start_done"), 1)
            for c in range(TT):
                for k in range(KT):
                    if c == 0:
                        wait_turned(0, k)
                    ins = pe.matmul(bank[5][:, 16 * c:16 * c + 16], xT[:, k, P * c:P * c + P], w_ab[:, k, :],
                                    start=(k == 0), stop=(k == KT - 1))
            ins.then_inc(sem("start_done"), 1)
            g_all = decay[:, 3, :]

            def head(pair, kind, i, c):
                return qkvT[:, 8 * kind + 2 * pair + i, P * c:P * c + P]

            for name, pair, level in plan:
                n = pair * 6 + level
                if name == "mm" and pair < 3 * NH:
                    j, k = pair, level
                    source, col, _ = tile_of(j)
                    if k == 0:
                        wait_chunk(pe, source)
                        if j >= 2:
                            pe.wait_ge(sem("conv_done"), j - 1)
                    ins = pe.matmul(bank[j % 2][:, 0:T], chunk(source)[:, k, col:col + P], xT[:, k, :],
                                    start=(k == 0), stop=(k == KT - 1))
                    if k == KT - 1:
                        ins.then_inc(sem("proj_done"), 1)
                elif name == "mm":
                    j, k = pair, level
                    cn, c = divmod(j - 3 * NH, 2)
                    if k == 0:
                        wait_chunk(pe, f"z{cn}")
                        if j < 3 * NH + 2:
                            pe.wait_ge(sem("conv_done"), j - 1)
                        else:
                            pe.wait_ge(sem("z_out"), j - 3 * NH - 1)
                    ins = pe.matmul(bank[j % 2][:, :], xT[:, k, P * c:P * c + P], chunk(f"z{cn}")[:, k, :],
                                    start=(k == 0), stop=(k == KT - 1))
                    if k == KT - 1:
                        ins.then_inc(sem("proj_done"), 1)
                elif name == "cum":
                    pe.wait_ge(sem("g_ready"), 1)
                    pe.matmul(bank[6][:, 0:16], upper[:, :], g_all, start=True, stop=True)
                    pe.matmul(bank[6][:, 16:32], ones[:, :], g_all, start=True, stop=True
                              ).then_inc(sem("start_done"), 1)
                elif name == "norm":
                    for a in range(2):
                        pe.wait_ge(sem("squares"), 2 * pair + a + 1)
                        if pair and not a:
                            pe.wait_ge(sem("lt_ready"), pair)
                            pe.wait_ge(sem("AT_ready"), pair)
                        ins = pe.matmul(bank[2 + a][:, :], ones[:, :], sq[:, 512 * a:512 * a + 512],
                                        start=True, stop=True)
                    ins.then_inc(sem("sumsq_done"), 1)
                    for u in range(4):
                        i, c = divmod(u, 2)
                        col = NH * c + 2 * pair + i
                        ins = pe.matmul(bank[4][:, P * u:P * u + P], g_all[:, col:col + 1].broadcast_to([P, P]),
                                        upper[:, :], start=True, stop=True)
                    ins.then_inc(sem("row_cum_done"), 1)
                elif name == "gram":
                    pe.wait_ge(sem("qk_normed"), pair + 1)
                    if pair:
                        pe.wait_ge(sem("q_state_ready"), pair)
                    for kind in (1, 0):
                        for u in range(4):
                            i, c = divmod(u, 2)
                            ins = pe.matmul(bank[6 - kind][:, P * u:P * u + P], head(pair, kind, i, c),
                                            head(pair, 1, i, c), start=True, stop=True)
                        ins.then_inc(sem("gram_done"), 1)
                    pe.wait_ge(sem("decay_diff"), pair + 1)
                    for i in range(2):
                        for c in range(TT):
                            u = 2 * i + c
                            pe.transpose(bank[7][:, P * u:P * u + P], qkvT[:, 16 + 2 * pair + i, P * c:P * c + P],
                                         ident[:, :])
                        ins = pe.transpose(bank[4][:, P * i:P * i + P], head(pair, 1, i, 0), ident[:, :])
                    ins.then_inc(sem("kv_flip_done"), 1)
                elif name == "flip":
                    pe.wait_ge(sem("L_ready"), pair + 1)
                    pe.wait_ge(sem("norm_ln"), 2 * pair + 2)
                    if pair:
                        pe.wait_ge(sem("o_out"), pair)
                    for u in range(4):
                        ins = pe.transpose(bank[2][:, P * u:P * u + P], Lm[:, u, :], ident[:, :])
                    ins.then_inc(sem("L_flip_done"), 1)
                elif name == "flip_a":
                    pe.wait_ge(sem("A_ready"), pair + 1)
                    for u in range(4):
                        ins = pe.transpose(bank[3][:, P * u:P * u + P], Am[:, u, :], ident[:, :])
                    ins.then_inc(sem("A_flip_done"), 1)
                elif name == "half":
                    pe.wait_ge(sem("LM_ready"), n)
                    pe.wait_ge(sem("T_ready"), n)
                    if level == 1:
                        pe.wait_ge(sem("kv_tok"), 3 * pair + 2)
                    for u in range(4):
                        ins = pe.matmul(bank[4][:, P * u:P * u + P], LMm[:, u, :], Tm[:, u, :], start=True, stop=True)
                    ins.then_inc(sem("half_done"), 1)
                elif name == "full":
                    pe.wait_ge(sem("X_ready"), n)
                    pe.wait_ge(sem("Z_ready"), pair * 7 + level)
                    if level == 1:
                        pe.wait_ge(sem("A_ready"), pair + 1)
                    if level < 6:
                        for u in range(4):
                            ins = pe.matmul(bank[5][:, P * u:P * u + P], Zm[:, u, :], Xm[:, u, :],
                                            start=True, stop=True)
                        ins.then_inc(sem("fullT_done"), 1)
                    for u in range(4):
                        ins = pe.matmul(bank[6][:, P * u:P * u + P], Xm[:, u, :], Zm[:, u, :], start=True, stop=True)
                    ins.then_inc(sem("fullZ_done"), 1)
                elif name == "new0":
                    pe.wait_ge(sem("Z_ready"), pair * 7 + 7)
                    pe.wait_ge(sem("B0_ready"), pair + 1)
                    for i in range(2):
                        ins = pe.matmul(bank[7][:, P * i:P * i + P], Zm[:, 2 * i, :], B_in[:, i, :],
                                        start=True, stop=True)
                    ins.then_inc(sem("new0_done"), 1)
                elif name == "state":
                    pe.wait_ge(sem("new0_ready"), pair + 1)
                    for i in range(2):
                        ins = pe.matmul(bank[5][:, P * i:P * i + P], k_tok[:, i, :], v_new[:, 2 * i, :],
                                        start=True, stop=True)
                    ins.then_inc(sem("state_done"), 1)
                elif name == "read":
                    pe.wait_ge(sem("state_ready"), pair + 1)
                    for i in range(2):
                        ins = pe.matmul(bank[5][:, 256 + P * i:256 + P * i + P], head(pair, 1, i, 1), S_st[:, i, :],
                                        start=True, stop=True)
                    ins.then_inc(sem("read_done"), 1)
                    for i in range(2):
                        ins = pe.matmul(bank[6][:, P * i:P * i + P], head(pair, 0, i, 1), S_st[:, i, :],
                                        start=True, stop=True)
                    ins.then_inc(sem("q_state_done"), 1)
                elif name == "new1":
                    pe.wait_ge(sem("B1_ready"), pair + 1)
                    for i in range(2):
                        ins = pe.matmul(bank[7][:, P * i:P * i + P], Zm[:, 2 * i + 1, :], B_in[:, i, :],
                                        start=True, stop=True)
                    ins.then_inc(sem("new1_done"), 1)
                elif name == "out":
                    pe.wait_ge(sem("new1_ready"), pair + 1)
                    if pair + 2 <= NH // 2:
                        pe.wait_ge(sem("norm_ln"), 2 * pair + 4)
                    for u in range(4):
                        ins = pe.matmul(bank[2][:, P * u:P * u + P], ATm[:, u, :], v_new[:, u, :],
                                        start=True, stop=True)
                    ins.then_inc(sem("o_done"), 1)
                elif name == "w_out":
                    c, half = divmod(level, 2)
                    pe.wait_ge(sem("oT_ready"), pair + 1)
                    if pair == 0:
                        wait_chunk(pe, f"go{half}")
                        if c == 0:
                            pe.wait_ge(sem("z_out"), 4)
                        elif half == 0:
                            pe.wait_ge(sem("X_ready"), 6 * (NH // 2))
                        else:
                            pe.wait_ge(sem("q_state_ready"), NH // 2)
                    for k in (2 * pair, 2 * pair + 1):
                        ins = pe.matmul(bank[OUT_BANKS[level]][:, :], xT[:, k, P * c:P * c + P],
                                        chunk(f"go{half}")[:, k, :], start=(k == 0), stop=(k == KT - 1))
                    if pair == NH // 2 - 1:
                        ins.then_inc(sem("gdn_out_done"), 1)
                elif name == "turn":
                    pe.wait_ge(sem("o_gated"), pair + 1)
                    if pair:
                        pe.wait_ge(sem("oT_ready"), pair)
                    for i in range(2):
                        for c in range(TT):
                            ins = pe.transpose(bank[3][:, T * i + P * c:T * i + P * c + P],
                                               o_tok[:, c, 2 * pair + i, :], ident[:, :])
                    ins.then_inc(sem("oT_flip_done"), 1)
            for layer in range(2):
                if layer == 1:
                    norm_flip(3)
                    wait_chunk(pe, "kv")
                    for c in range(TT):
                        by_token(bank[4 + c][:, 0:256], xkvT, chunk("kv")[:, :, 256:512], c, sem("kv_done"),
                                 wait=None if c else lambda k: wait_turned(3, k, kv=True))
                    for g in range(2):
                        for k in range(KT):
                            ins = pe.matmul(bank[6 + g][:, 0:T], chunk("kv")[:, k, P * g:P * g + P], xkvT[:, k, :],
                                            start=(k == 0), stop=(k == KT - 1))
                        ins.then_inc(sem("kv_done"), 1)
                    def score(hd):
                        lo = 64 * (hd % 2)
                        if hd >= 4:
                            pe.wait_ge(sem("attn_exp"), hd - 3)
                        if hd % 2 == 0:
                            pe.wait_ge(sem("qT_ready"), hd // 2 + 1)
                        k_, q_ = kT[lo:lo + 64, hd // 4, :], qT[lo:lo + 64, hd // 2, :]
                        b = bank[HEAD_BANKS[hd % 4]]
                        pe.matmul(b[:, 0:256], k_[:, 0:P], q_, start=True, stop=True)
                        pe.matmul(b[:, 256:384], k_[:, P:T], q_[:, P:T], start=False, stop=True,
                                  skip_group_check=True).then_inc(sem("z_score"), 1)

                    def reverse(hd):
                        pe.wait_ge(sem("soft_ready"), hd + 1)
                        b, s_ = bank[HEAD_BANKS[hd % 4]], soft[:, hd % 3, :]
                        pe.matmul(b[:, 0:256], lower[:, :], s_[:, 0:256], start=False, stop=False,
                                  skip_group_check=True)
                        pe.matmul(b[:, 128:256], ones[:, :], s_[:, 256:384], start=False, stop=False,
                                  skip_group_check=True)
                        pe.matmul(b[:, 256:384], lower[:, :], s_[:, 256:384], start=False, stop=True,
                                  skip_group_check=True).then_inc(sem("rev_done"), 1)

                    def values(i):
                        pe.wait_ge(sem("attn_ready"), 2 * i + 2)
                        if i >= 2:
                            pe.wait_ge(sem("sbo_ready"), i - 1)
                        for c in range(TT):
                            for m in range(2):
                                hd = 2 * i + m
                                v_ = v_sb[:, c, SD * (hd // 4):SD * (hd // 4) + SD]
                                o = bank[PV_BANKS[i % 2]][64 * m:64 * m + 64, P * c:T]
                                ins = pe.matmul(o, v_, attn[:, hd % 4, T * c:T + P * c], start=(c == 0), stop=(c == 1),
                                                skip_group_check=True)
                        ins.then_inc(sem("pv_done"), 1)

                    def head_step(hd):
                        if hd < QH:
                            score(hd)
                        if 2 <= hd < QH + 2:
                            reverse(hd - 2)
                        if hd >= 5 and hd % 2:
                            values((hd - 5) // 2)

                    for k in range(KT):
                        wait_turned(3, k)
                    for i in range(KT):
                        cn = i // 4
                        if i == 1:
                            pe.wait_ge(sem("kv_ready"), 4)
                        if i % 4 == 0:
                            wait_chunk(pe, f"sq{cn}")
                        if i >= 2:
                            pe.wait_ge(sem("qT_ready"), i - 1)
                        for k in range(KT):
                            ins = pe.matmul(bank[Q_BANKS[i % 2]][:, 0:T],
                                            chunk(f"sq{cn}")[:, k, P * (i % 4):P * (i % 4) + P],
                                            xT[:, k, :], start=(k == 0), stop=(k == KT - 1))
                        ins.then_inc(sem("sbq_done"), 1)
                        if i >= 2:
                            head_step(i - 2)
                    for hd in range(KT - 2, QH + 4):
                        head_step(hd)
                    for j in range(4):
                        c, half = divmod(j, 2)
                        wait_chunk(pe, f"so{half}")
                        by_token(bank[SB_BANKS[j]][:, :], xT, chunk(f"so{half}"), c, sem("sb_out_done"),
                                 wait=None if j else lambda k: pe.wait_ge(sem("sbo_ready"), k + 1))

                n = 1 + 3 * layer
                raw_flip(n)
                pe.wait_ge(sem("p_landed"), 16 * (layer + 1))
                for j in range(2):
                    for c in range(TT):
                        ins = pe.transpose(bank[5][:, T * j + P * c:T * j + P * c + P], p_tok[:, c, P * j:P * j + P],
                                           ident[:, :])
                ins.then_inc(sem("p_flip"), 1)
                pe.wait_ge(sem("router_landed"), 32 * (layer + 1))
                for c in range(TT):
                    for k in range(KT):
                        if c == 0:
                            wait_turned(n, k)
                        ins = pe.matmul(bank[4][:, 36 * c:36 * c + 36], xT[:, k, P * c:P * c + P], w_rt[:, k, :],
                                        start=(k == 0), stop=(k == KT - 1))
                ins.then_inc(sem("logits_done"), 1)

                def embed(q):
                    c, half = divmod(q, 2)
                    w = wring[:, CHUNKS[f"pp{layer}"], 0:2 * D].rearrange("p (j n) -> p j n", j=2)
                    by_token(bank[EMB_BANKS[q]][:, :], pT, w[:, :, HALF * half:HALF * half + HALF], c,
                             sem("ple_emb_done"), kts=2)

                wait_chunk(pe, f"pp{layer}")
                pe.wait_ge(sem("pT_ready"), layer + 1)
                for q in range(3):
                    embed(q)
                pe.wait_ge(sem("picked"), 2 * layer + 1)
                ch = rt[:, 9, :, :]
                pe.matmul(bank[5][:, 0:32], below[:, :], ch[:, 0, :], start=True, stop=True)
                pe.matmul(bank[5][:, 32:64], ones[:, :], ch[:, 0, :], start=True, stop=False)
                pe.matmul(bank[5][:, 32:64], below[:, :], ch[:, 1, :], start=False, stop=True)
                pe.wait_ge(sem("picked"), 2 * layer + 2)
                for c in range(TT):
                    ins = pe.matmul(bank[5][:, 64:96], ones[:, :], rt[:, 10, c, :], start=(c == 0), stop=(c == 1))
                ins.then_inc(sem("offsets_done"), 1)
                for c in range(TT):
                    ins = pe.matmul(bank[6][:, 0:NE], ones[:, :], ch[:, c, :], start=(c == 0), stop=(c == 1))
                ins.then_inc(sem("counts_done"), 1)
                embed(3)
                pe.wait_ge(sem("xh_gather"), TT * layer + 2)
                pe.wait_ge(sem("emb_out"), 4 * layer + 3)

                def gather(k, c):
                    for part in (xh_part, xl_part):
                        ins = pe.matmul(bank[k % 4][:, :], part[:, c, k, :], one_hot[:, c, :],
                                        start=(c == 0 and part is xh_part), stop=(c == 1 and part is xl_part))
                    return ins

                for c in range(TT):
                    pe.wait_ge(sem("xl_gather"), TT * layer + c + 1)
                    pe.wait_ge(sem("one_hot_ready"), TT * layer + c + 1)
                    for k in range(4):
                        ins = gather(k, c)
                        if c == 1:
                            ins.then_inc(sem("gather_done"), 1)
                pe.wait_ge(sem("emb_out"), 4 * layer + 4)
                for k in range(4, KT):
                    pe.wait_ge(sem("xs_act" if k % 2 == 0 else "xs_dve"), 4 * layer + (k - 4) // 2 + 1)
                    gather(k, 0)
                    gather(k, 1).then_inc(sem("gather_done"), 1)
                pe.wait_ge(sem("xs_act"), 4 * layer + 4)
                pe.wait_ge(sem("xs_dve"), 4 * layer + 4)

                def gate_up(x, g, e1, fills, used):
                    s = 2 * g + x
                    pe.wait_ge(sem(f"expert_gu{s}"), fills * 32)
                    pe.wait_ge(sem("xe_ready"), e1)
                    if used is not None:
                        pe.wait_ge(sem("hh_ready"), used)
                    w = gu_slot(s).rearrange("p a (k f) -> p a k f", k=KT)
                    for k in range(KT):
                        for a in range(2):
                            ins = pe.matmul(bank[4 + x][64 * a:64 * a + 64, 0:FE], xe[:, x, k, :], w[:, a, k, :],
                                            start=(k == 0), stop=(k == KT - 1), skip_group_check=True)
                    ins.then_inc(sem("gu_done"), 1)

                def turn_pair(q1):
                    pe.wait_ge(sem("hh_ready"), q1 * 2)
                    pe.wait_ge(sem("rw_ready"), q1)
                    for c in range(TT):
                        pe.transpose(bank[6][:, 256 + P * c:256 + P * c + P], rw[:, c, :], ident[:, :])
                    for x in range(2):
                        for j in range(2):
                            ins = pe.transpose(bank[6][:, P * x + 64 * j:P * x + 64 * j + 64],
                                               hh[64:128, x, j:FE:2], ident[64:128, 64:128])
                    ins.then_inc(sem("tr_done"), 1)

                def down_half(a, b, g, q1, fills, ready):
                    if a == 0:
                        for x in range(2):
                            pe.wait_ge(sem(f"expert_d{2 * g + x}"), fills * 16)
                        pe.wait_ge(sem("hr_ready"), q1)
                    if ready is not None:
                        pe.wait_ge(sem("ye_ready"), ready)
                    for j in range(2):
                        for x in range(2):
                            w = d_slot(2 * g + x).rearrange("p (j d) -> p j d", j=2)
                            ins = pe.matmul(bank[7][64 * x:64 * x + 64, :], hr[:, b, P * x + 64 * j:P * x + 64 * j + 64],
                                            w[:, j, HALF * a:HALF * a + HALF], start=(j == 0), stop=(j == 1),
                                            skip_group_check=True)
                    ins.then_inc(sem("down_done"), 1)

                def scatter_half(a, b, ready, first=False, last=False):
                    pe.wait_ge(sem("ye_ready"), ready)
                    for c in range(TT):
                        ins = pe.matmul(bank[2 * c + a][:, :], hr[:, b, 256 + P * c:256 + P * c + P], ye[:, a, :],
                                        start=first, stop=last, skip_group_check=True)
                    ins.then_inc(sem("scat_done"), 1)

                pe.wait_ge(sem("pad_set"), layer + 1)
                for j in (1, 3):
                    pe.matmul(bank[j][:, :], ones[:, :], xs[:, :, SLOTS:], start=True, stop=False,
                              skip_group_check=True)

                q0 = PAIRS * layer

                def expert_pair(q, g, b, fills, fills_before):
                    e1, before = q * 2 + (2 * q0 + 1), (g - 1) % RING_PAIRS
                    gate_up(0, g, e1, fills, e1 - 2)
                    turn_pair(q + q0)
                    gate_up(1, g, e1 + 1, fills, e1 - 1)
                    down_half(0, 1 - b, before, q + q0, fills_before, e1 - 3)
                    scatter_half(1, b, e1 - 3)
                    down_half(1, 1 - b, before, q + q0, fills_before, e1 - 2)
                    scatter_half(0, 1 - b, e1 - 2)

                def fill(q):
                    return q // RING_PAIRS + FILLS[q % RING_PAIRS] * layer + 1

                for b in range(2):
                    q = q0 + b
                    gate_up(0, b, 2 * q + 1, fill(b), 2 * q - 1 if q else None)
                    if b:
                        turn_pair(q)
                    gate_up(1, b, 2 * q + 2, fill(b), 2 * q if q else None)
                    if b:
                        down_half(0, 0, 0, q, fill(0), 2 * q - 2 if q > 1 else None)
                        down_half(1, 0, 0, q, fill(0), 2 * q - 1)
                        scatter_half(0, 0, 2 * q - 1, first=True)
                with pe.Fori(0, 2) as i:
                    for j in range(2, 8):
                        expert_pair(i * 6 + j, j % RING_PAIRS, j % 2, i * 2 + fill(j), i * 2 + fill(j - 1))
                for q in range(PAIRS - 2, PAIRS):
                    expert_pair(q, q % RING_PAIRS, q % 2, fill(q), fill(q - 1))
                end, g = q0 + PAIRS, (PAIRS - 1) % RING_PAIRS
                turn_pair(end)
                down_half(0, 1, g, end, fill(PAIRS - 1), 2 * end - 2)
                scatter_half(1, 0, 2 * end - 2)
                down_half(1, 1, g, end, fill(PAIRS - 1), 2 * end - 1)
                scatter_half(0, 1, 2 * end - 1, last=True)
                scatter_half(1, 1, 2 * end, last=True)

                flag = pe.value_load(over_i[0:1, 0:1], min_val=0, max_val=1)
                with pe.If(flag > 0):
                    pe.wait_ge(sem(f"over_x{layer}"), 1)
                    for k in range(KT):
                        for c in range(TT):
                            col = T * (k % 2) + P * c
                            ins = pe.transpose(bank[4 + k // 2][:, col:col + P], xh[:, c, k, :], ident[:, :])
                    ins.then_inc(sem(f"over_gu{layer}"), 1)
                    pe.wait_ge(sem(f"over_x{layer}"), 2)
                    pe.wait_ge(sem("h_tile"), 2 * (2 + 3 * layer))
                    with pe.Fori(0, NE) as e:
                        pe.wait_ge(sem(f"over_landed{layer}"), e * 48 + 48)
                        for f in range(2):
                            pe.wait_ge(sem(f"over_hid{layer}"), e * 2 + (f + 1))
                            for a in range(2):
                                w = over_w(a).rearrange("p (k f) -> p k f", k=KT)
                                for k in range(KT):
                                    ins = pe.matmul(bank[4 + a][:, 0:T], w[:, k, f:FE:2], xT[:, k, :],
                                                    start=(k == 0), stop=(k == KT - 1))
                            ins.then_inc(sem(f"over_gu{layer}"), 1)
                        pe.wait_ge(sem(f"over_hid{layer}"), e * 2 + 3)
                        w = over_w(2).rearrange("p (j d) -> p j d", j=2)
                        for c in range(TT):
                            for a in range(2):
                                for f in range(2):
                                    ins = pe.matmul(bank[2 * c + a][:, :], over_g[:, f, P * c:P * c + P],
                                                    w[:, f, HALF * a:HALF * a + HALF], start=(f == 0), stop=(f == 1))
                        ins.then_inc(sem(f"over_down{layer}"), 1)
                    pe.wait_ge(sem(f"over_free{layer}"), NE + 1)

                n = 2 + 3 * layer
                raw_flip(n)
                for j in range(4):
                    c, half = divmod(j, 2)
                    wait_chunk(pe, f"pg{layer}.{half}")
                    by_token(bank[j][:, :], xT, chunk(f"pg{layer}.{half}"), c, sem("ple_gate_done"),
                             wait=None if j else lambda k: wait_turned(n, k))

        @block.vector
        def _(dve):
            link = chain_of(dve, "dve_chain")

            def norm_sum(n):
                if n:
                    dve.wait_ge(sem("h_tile"), 2 * n - 1)
                dve.tensor_tensor_reduce(xh[:, 0].rearrange("p k q -> p (k q)"), h[:, 0, :], h[:, 0, :], 1.0, 0.0,
                                         ALU.mult, ALU.add, stat[:, 0:1]).then_inc(sem("sums0"), 1)

            def norm_gain(n, gain, dst=xT):
                for b in (1, 3):
                    dve.wait_ge(sem("norm_flip"), 4 * n + b + 1)
                    for k in range(2):
                        ins = dve.tensor_scalar(dst[:, 2 * b + k, :], bank[b][:, T * k:T * k + T],
                                                gains[:, gain, 2 * b + k:2 * b + k + 1], None, ALU.mult)
                    ins.then_inc(sem("xT_dve"), 1)

            def norm_apply(n):
                dve.wait_ge(sem("norm_rstd"), 2 * n + 1)
                dve.tensor_scalar(xh[:, 0], h[:, 0, :].rearrange("p (q k) -> p k q", k=KT), rstd[:, 0:1], None,
                                  ALU.mult).then_inc(sem("xh_dve"), 1)

            dve.memset(eps_t[:, 0:1], EPS * DH)
            dve.memset(eps_t[:, 1:2], EPS)
            dve.wait_ge(sem("x_landed"), 16)
            norm_sum(0)
            norm_apply(0)
            dve.wait_ge(sem("first_landed"), 5 * 16)
            norm_gain(0, 0)
            d = [decay[:, i, :] for i in range(10)]

            def pairs(t):
                return t.rearrange("p (c h) -> p c h", c=TT)
            dve.wait_ge(sem("start_done"), 2)
            ab = bank[5][:, 0:32].rearrange("p (c n) -> p c n", c=TT)
            link(dve.tensor_tensor(pairs(d[0]), ab[:, :, 0:NH], ab_row[:, 1:2, :].broadcast_to([P, TT, NH]), ALU.add))
            link(dve.tensor_copy(pairs(d[2]), ab[:, :, NH:]))
            link(dve.tensor_scalar(d[1], d[0], -1.0, None, ALU.mult))
            dve.tensor_tensor(d[1], d[1], d[0], ALU.max).then_inc(sem("ab_abs"), 1)
            dve.wait_ge(sem("ab_exp"), 1)
            link(dve.scalar_tensor_tensor(out=d[3], in0=d[0], scalar=0.0, in1=d[1], op0=ALU.max, op1=ALU.add))
            link(dve.tensor_tensor(pairs(d[3]), pairs(d[3]), d[4][:, 0:NH].unsqueeze(1).broadcast_to([P, TT, NH]),
                                   ALU.mult))
            dve.tensor_scalar(d[3], d[3], -1.0, None, ALU.mult).then_inc(sem("g_ready"), 1)
            link(dve.tensor_scalar(d[2], d[2], 1.0, None, ALU.add))
            link(dve.reciprocal(d[8], d[2]))
            G, eG, kdec, beta, neg_eG = d[5], d[6], d[7], d[8], d[9]
            dve.wait_ge(sem("conv_ready"), 1)

            flat = "p u n -> p (u n)"

            def add_h(j, done, src, ready):
                c, half = divmod(j, 2)
                dve.wait_ge(*done)
                view = h[:, c, HALF * half:HALF * half + HALF]
                ins = dve.tensor_tensor(view, src[:, :], view, ALU.add)
                if ready:
                    ins.then_inc(sem("h_tile"), 1)
                else:
                    link(ins)

            def gate_out(pair):
                o = o_tok[:, :, 2 * pair:2 * pair + 2, :]
                z = zs[:, :, 256 * pair:256 * pair + 256].rearrange("p c (i n) -> p c i n", i=2)
                dve.tensor_tensor(o, o, z, ALU.mult).then_inc(sem("o_gated"), 1)

            for name, pair, level in plan:
                n = pair * 6 + level
                cols = [NH * c + 2 * pair + i for i in range(2) for c in range(TT)]
                if name == "mm":
                    j, k = pair, level
                    if k < KT - 1 or j >= 3 * NH:
                        continue
                    ct = tile_of(j)[2]
                    dve.wait_ge(sem("conv_first"), j + 1)
                    src, dst = bank[j % 2][:, 0:T], qkvT[:, ct, :]
                    for tap in (2, 1, 0):
                        lag = 3 - tap
                        ins = dve.scalar_tensor_tensor(out=dst[:, lag:], in0=src[:, 0:T - lag],
                                                       scalar=conv_w[:, tap, ct:ct + 1], in1=dst[:, lag:],
                                                       op0=ALU.mult, op1=ALU.add)
                        if tap:
                            link(ins)
                        else:
                            ins.then_inc(sem("conv_done"), 1)
                elif name == "cum":
                    dve.wait_ge(sem("start_done"), 3)
                    link(dve.tensor_copy(d[5], bank[6][:, 0:16]))
                    dve.tensor_tensor(d[7], bank[6][:, 16:32], d[5], ALU.subtract).then_inc(sem("cum_ready"), 1)
                    dve.wait_ge(sem("decay_exp"), 1)
                    link(dve.tensor_scalar(d[9], d[6], -1.0, None, ALU.mult))
                    dve.wait_ge(sem("blocks_set"), 2)
                    for n in range(len(LEVELS)):
                        nxt = blk[:, n + 1, :] if n + 1 < len(LEVELS) else ones[:, :]
                        link(dve.tensor_tensor(blk[:, n, :], blk[:, n, :], nxt, ALU.subtract))
                elif name == "norm":
                    dve.wait_ge(sem("row_cum_done"), pair + 1)
                    for u in range(4):
                        ins = dve.tensor_scalar(Dm[:, u, :], bank[4][:, P * u:P * u + P], G[:, cols[u]:cols[u] + 1],
                                                0.0, ALU.subtract, ALU.max)
                    ins.then_inc(sem("decay_diff"), 1)
                    dve.wait_ge(sem("norm_exp"), pair + 1)
                    for a in range(2):
                        view = qkvT[:, 8 * a + 2 * pair:8 * a + 2 * pair + 2, :]
                        ins = dve.tensor_tensor(view, view, sq[:, 512 * a:512 * a + 512].rearrange(
                            "p (u t) -> p u t", u=2), ALU.mult)
                    ins.then_inc(sem("qk_normed"), 1)
                    dve.wait_ge(sem("decay_mat"), pair + 1)
                    link(dve.tensor_tensor(Dm, Dm, lower[:, :].unsqueeze(1).broadcast_to([P, 4, P]), ALU.mult))
                elif name == "gram":
                    DBm = Xm
                    for u in range(4):
                        ins = dve.tensor_scalar(DBm[:, u, :], Dm[:, u, :], beta[:, cols[u]:cols[u] + 1], None,
                                                ALU.mult)
                    link(ins)
                    dve.wait_ge(sem("gram_done"), 2 * pair + 1)
                    dve.tensor_tensor(Lm.rearrange(flat), bank[5][:, :], DBm.rearrange(flat), ALU.mult
                                      ).then_inc(sem("L_ready"), 1)
                elif name == "flip":
                    m1 = blk[:, 0:1, :].broadcast_to([P, 4, P])
                    idb = ident[:, :].unsqueeze(1).broadcast_to([P, 4, P])
                    LTb = bank[2][:, :].rearrange("p (u n) -> p u n", u=4)
                    dve.wait_ge(sem("L_ready"), pair + 1)
                    link(dve.tensor_tensor(Tm, Lm, m1, ALU.mult))
                    dve.tensor_tensor(Tm, Tm, idb, ALU.add).then_inc(sem("T_ready"), 1)
                    dve.wait_ge(sem("L_flip_done"), pair + 1)
                    dve.tensor_tensor(LMm, LTb, blk[:, 1:2, :].broadcast_to([P, 4, P]), ALU.mult
                                      ).then_inc(sem("LM_ready"), 1)
                    link(dve.tensor_tensor(Zm, LTb, m1, ALU.mult))
                    dve.tensor_tensor(Zm, Zm, idb, ALU.add).then_inc(sem("Z_ready"), 1)
                    dve.wait_ge(sem("gram_done"), 2 * pair + 2)
                    dve.tensor_tensor(Am.rearrange(flat), bank[6][:, :], Dm.rearrange(flat), ALU.mult
                                      ).then_inc(sem("A_ready"), 1)
                elif name == "flip_a":
                    dve.wait_ge(sem("kv_tok"), 3 * pair + 3)
                    for i in range(2):
                        ins = dve.tensor_scalar(B_in[:, i, :], v_tok[:, 2 * i, :],
                                                beta[:, cols[2 * i]:cols[2 * i] + 1], None, ALU.mult)
                    ins.then_inc(sem("B0_ready"), 1)
                elif name == "half" and level < 6:
                    dve.wait_ge(sem("half_done"), n)
                    if level == 1:
                        dve.wait_ge(sem("lt_ready"), pair + 1)
                    dve.tensor_tensor(LMm, LTm, blk[:, level + 1:level + 2, :].broadcast_to([P, 4, P]), ALU.mult
                                      ).then_inc(sem("LM_ready"), 1)
                elif name == "full":
                    if level < 6:
                        dve.wait_ge(sem("fullT_done"), 5 * pair + level)
                        dve.wait_ge(sem("T_ready"), n)
                        dve.tensor_tensor(Tm.rearrange(flat), bank[5][:, :], Tm.rearrange(flat), ALU.add
                                          ).then_inc(sem("T_ready"), 1)
                    dve.wait_ge(sem("fullZ_done"), n)
                    dve.wait_ge(sem("Z_ready"), pair * 7 + level)
                    dve.tensor_tensor(Zm.rearrange(flat), bank[6][:, :], Zm.rearrange(flat), ALU.add
                                      ).then_inc(sem("Z_ready"), 1)
                elif name == "silu_z":
                    dve.wait_ge(sem("z_ready"), pair + 1)
                    for done in range(3)[2 * pair:2 * pair + 2]:
                        gate_out(done)
                elif name == "read":
                    dve.wait_ge(sem("read_done"), pair + 1)
                    for i in range(2):
                        u = 2 * i + 1
                        link(dve.scalar_tensor_tensor(out=B_in[:, i, :], in0=bank[5][:, 256 + P * i:256 + P * i + P],
                                                      scalar=neg_eG[:, cols[u]:cols[u] + 1], in1=v_tok[:, u, :],
                                                      op0=ALU.mult, op1=ALU.add))
                    for i in range(2):
                        u = 2 * i + 1
                        ins = dve.tensor_scalar(B_in[:, i, :], B_in[:, i, :], beta[:, cols[u]:cols[u] + 1], None,
                                                ALU.mult)
                    ins.then_inc(sem("B1_ready"), 1)
                    dve.wait_ge(sem("q_state_done"), pair + 1)
                    for i in range(2):
                        u = 2 * i + 1
                        ins = dve.tensor_scalar(q_st[:, i, :], bank[6][:, P * i:P * i + P],
                                                eG[:, cols[u]:cols[u] + 1], None, ALU.mult)
                    ins.then_inc(sem("q_state_ready"), 1)
                elif name == "out":
                    dve.wait_ge(sem("o_done"), pair + 1)
                    dve.wait_ge(sem("q_state_ready"), pair + 1)
                    ob = bank[2][:, :].rearrange("p (i c n) -> p i c n", i=2, c=TT)
                    heads = slice(2 * pair, 2 * pair + 2)
                    link(dve.tensor_copy(o_tok[:, 0, heads, :], ob[:, :, 0, :]))
                    dve.tensor_tensor(o_tok[:, 1, heads, :], ob[:, :, 1, :], q_st, ALU.add).then_inc(sem("o_out"), 1)
                    dve.wait_ge(sem("o_out"), pair + 1)
                    for i in range(2):
                        for c in range(TT):
                            o = o_tok[:, c, 2 * pair + i, :]
                            ins = dve.tensor_tensor_reduce(Xm[:, 2 * i + c, :], o, o, 1.0, 0.0, ALU.mult, ALU.add,
                                                           o_sum[:, pair, c, i:i + 1])
                    ins.then_inc(sem("o_sums"), 1)
                    dve.wait_ge(sem("o_rstd"), pair + 1)
                    if pair == 0:
                        dve.wait_ge(sem("small_landed"), 11 * 16)
                    for i in range(2):
                        for c in range(TT):
                            o = o_tok[:, c, 2 * pair + i, :]
                            ins = dve.scalar_tensor_tensor(out=o, in0=o, scalar=o_sum[:, pair, c, i:i + 1],
                                                           in1=o_gain[:, :], op0=ALU.mult, op1=ALU.mult)
                    link(ins)
                    if pair == NH // 2 - 1:
                        gate_out(pair)
            for j in range(4):
                add_h(j, (sem("gdn_out_done"), j + 1), bank[OUT_BANKS[j]], j % 2)
                if j == 1:
                    norm_sum(1)

            for layer in range(2):
                if layer == 1:
                    norm_apply(3)
                    norm_gain(3, 6, xkvT)
                    norm_gain(3, 3)

                    def soft_sum(hd):
                        dve.wait_ge(sem("soft_log"), hd + 1)
                        if hd >= 3:
                            dve.wait_ge(sem("rev_done"), hd - 2)
                        s_ = soft[:, hd % 3, :]
                        link(dve.scalar_tensor_tensor(out=s_, in0=bank[HEAD_BANKS[hd % 4]][:, 0:384], scalar=0.0,
                                                      in1=soft_u[:, hd % 2, :], op0=ALU.min, op1=ALU.subtract,
                                                      reverse1=True))
                        view = s_.rearrange("p (b n) -> p b n", n=P)[:, 0:3:2, :]
                        dve.tensor_tensor(view, view, below[:, :].unsqueeze(1).broadcast_to([P, 2, P]), ALU.mult
                                          ).then_inc(sem("soft_ready"), 1)

                    def out_pair(i):
                        if i == 0:
                            dve.wait_ge(sem("sbq_done"), KT)
                        dve.wait_ge(sem("pv_done"), i + 1)
                        dve.tensor_copy(xT[:, i, :], bank[PV_BANKS[i % 2]][:, 0:T]).then_inc(sem("sbo_ready"), 1)

                    for hd in range(QH + 5):
                        if hd < QH:
                            soft_sum(hd)
                        if hd >= 6 and hd % 2 == 0:
                            out_pair(hd // 2 - 3)
                    for j in range(4):
                        add_h(j, (sem("sb_out_done"), j + 1), bank[SB_BANKS[j]], j % 2)
                        if j == 1:
                            norm_sum(4)

                n = 1 + 3 * layer
                norm_gain(n, n)
                dve.wait_ge(sem("norm_rstd"), 2 * n + 2)
                dve.wait_ge(sem("logits_done"), layer + 1)
                lg = bank[4][:, 0:72].rearrange("p (c e) -> p c e", c=TT)
                grp, shift, gexp = (rt[:, i, :, 0:NG] for i in (0, 1, 2))
                drop = rt[:, 4].rearrange("p c e -> p (c e)")[:, 0:TT * NG]
                elog, masked, hot1, masked2, hot2, chosen, passed, cand = (rt[:, i] for i in (5, 6, 7, 8, 3, 9, 10, 11))
                sm = [rt[:, i, :, j:j + 1] for i in (12, 13) for j in range(4)]
                m1, m2, diff, ediff = (rt[:, 14, :, j:j + 1] for j in (0, 3, 1, 2))
                off = rt[:, 15, 0, :]
                gmax, gsum, gp, c1, w1, w2, pos1, pos2 = sm
                c2 = rt[:, 14, :, 4:5]
                by_group = "p c (g e) -> p (c g) e"

                def each(op):
                    for c in range(TT):
                        ins = op(c)
                    link(ins)

                for c in range(TT):
                    dve.scalar_tensor_tensor(out=grp[:, c, :], in0=lg[:, c, 0:NG], scalar=rstd[:, c:c + 1],
                                             in1=b_rt[:, layer, 0:NG], op0=ALU.mult, op1=ALU.add)
                each(lambda c: dve.scalar_tensor_tensor(out=elog[:, c, :], in0=lg[:, c, NG:], scalar=rstd[:, c:c + 1],
                                                        in1=b_rt[:, layer, NG:], op0=ALU.mult, op1=ALU.add))
                link(dve.tensor_reduce(gmax, grp, AX_X, ALU.max))
                dve.tensor_tensor(shift, grp, gmax.broadcast_to([P, TT, NG]), ALU.subtract
                                  ).then_inc(sem("group_shift"), 1)

                def first_max(first, vals, m, width):
                    each(lambda c: dve.scalar_tensor_tensor(out=cand[:, c, 0:width], in0=vals[:, c, :],
                                                            scalar=m[:, c, :], in1=rev_idx[:, 0:width],
                                                            op0=ALU.is_equal, op1=ALU.mult))
                    link(dve.tensor_reduce(first, cand[:, :, 0:width], AX_X, ALU.max))

                first_max(c1, grp, gmax, NG)
                each(lambda c: dve.tensor_scalar(drop[:, NG * c:NG * c + NG], cand[:, c, 0:NG], c1[:, c, :], -BIG,
                                                 ALU.not_equal, ALU.mult))
                link(dve.tensor_tensor(masked.rearrange(by_group, g=NG), elog.rearrange(by_group, g=NG),
                                       drop.unsqueeze(2).broadcast_to([P, TT * NG, EPG]), ALU.add))
                link(dve.tensor_reduce(m1, masked, AX_X, ALU.max))
                first_max(c1, masked, m1, NE)
                link(dve.tensor_tensor(hot1, cand, c1.broadcast_to([P, TT, NE]), ALU.is_equal))
                link(dve.scalar_tensor_tensor(out=masked2, in0=hot1, scalar=-3 * BIG, in1=masked, op0=ALU.mult,
                                              op1=ALU.add))
                link(dve.tensor_reduce(m2, masked2, AX_X, ALU.max))
                first_max(c2, masked2, m2, NE)
                link(dve.tensor_tensor(hot2, cand, c2.broadcast_to([P, TT, NE]), ALU.is_equal))
                dve.tensor_tensor(chosen, hot1, hot2, ALU.add).then_inc(sem("picked"), 1)
                each(lambda c: dve.tensor_scalar(passed[:, c, :], rev_idx[:, 0:NE], c1[:, c, :], None, ALU.is_lt))
                for c in range(TT):
                    ins = dve.scalar_tensor_tensor(out=passed[:, c, :], in0=rev_idx[:, 0:NE], scalar=c2[:, c, :],
                                                   in1=passed[:, c, :], op0=ALU.is_lt, op1=ALU.add)
                ins.then_inc(sem("picked"), 1)
                dve.tensor_tensor(diff, m2, m1, ALU.subtract).then_inc(sem("pair_diff"), 1)
                dve.wait_ge(sem("offsets_done"), layer + 1)
                link(dve.tensor_copy(off, bank[5][:, 64:96]))
                link(dve.tensor_tensor(cand, bank[5][:, 0:64].rearrange("p (c e) -> p c e", c=TT),
                                       off.unsqueeze(1).broadcast_to([P, TT, NE]), ALU.add))
                for c in range(TT):
                    for i, (hot, pos) in enumerate(((hot1, pos1), (hot2, pos2))):
                        ins = dve.tensor_tensor_reduce((masked, masked2)[i][:, c, :], hot[:, c, :], cand[:, c, :],
                                                       1.0, 0.0, ALU.mult, ALU.add, pos[:, c, :])
                link(ins)
                for c in range(TT):
                    link(dve.tensor_scalar(one_hot[:, c, :], iota[:, :], pos1[:, c, :], None, ALU.is_equal))
                    dve.scalar_tensor_tensor(out=one_hot[:, c, :], in0=iota[:, :], scalar=pos2[:, c, :],
                                             in1=one_hot[:, c, :].bitcast(F32), op0=ALU.is_equal, op1=ALU.add
                                             ).then_inc(sem("one_hot_ready"), 1)
                dve.tensor_copy(off_i[:, :], off)
                link(dve.tensor_copy(rank[:, :, :].rearrange("p c e -> p (c e)"), bank[5][:, 0:64]))
                dve.wait_ge(sem("group_exp"), layer + 1)
                link(dve.tensor_reduce(gsum, gexp, AX_X, ALU.add))
                link(dve.reciprocal(gp, gsum))
                dve.wait_ge(sem("pair_exp"), layer + 1)
                link(dve.tensor_scalar(w2, ediff, 1.0, None, ALU.add))
                link(dve.reciprocal(w1, w2))
                link(dve.tensor_tensor(w1, w1, gp, ALU.mult))
                link(dve.tensor_tensor(w2, w1, ediff, ALU.mult))
                link(dve.tensor_tensor(cw[:, :, :], hot1, w1.broadcast_to([P, TT, NE]), ALU.mult))
                each(lambda c: dve.scalar_tensor_tensor(out=cw_over[:, c, :], in0=hot2[:, c, :], scalar=w2[:, c, :],
                                                        in1=cw[:, c, :], op0=ALU.mult, op1=ALU.add))
                link(dve.tensor_scalar(cand, rank[:, :, :], float(CAP), None, ALU.is_lt))
                link(dve.tensor_tensor(cw[:, :, :], cw_over[:, :, :], cand, ALU.mult))
                link(dve.tensor_tensor(cw_over[:, :, :], cw_over[:, :, :], cw[:, :, :], ALU.subtract))
                dve.wait_ge(sem("counts_done"), layer + 1)
                link(dve.tensor_reduce(m1[:, 0, :], bank[6][:, 0:NE], AX_X, ALU.max))
                dve.tensor_scalar(over_i[:, :], m1[:, 0, :], float(CAP), None, ALU.is_gt).then_inc(sem("routed"), 1)
                for k in range(1, KT, 2):
                    dve.wait_ge(sem("gather_done"), KT * layer + k + 1)
                    dve.tensor_scalar(xs[:, k, 0:SLOTS], bank[k % 4][:, :], gains[:, n, k:k + 1], None, ALU.mult
                                      ).then_inc(sem("xs_dve"), 1)
                def scatter_mat(e, used):
                    if used is not None:
                        dve.wait_ge(sem("tr_done"), used)
                    for c in range(TT):
                        for x in range(2):
                            ins = dve.tensor_scalar(rw[:, c, CAP * x:CAP * x + CAP], iota[:, 0:CAP],
                                                    rank[:, c, bass.ds(e + x, 1)], cw[:, c, bass.ds(e + x, 1)],
                                                    ALU.is_equal, ALU.mult)
                    ins.then_inc(sem("rw_ready"), 1)

                def hidden(x, done):
                    dve.wait_ge(sem("sg_ready"), done)
                    dve.tensor_tensor(hh[64:128, x, :], bank[4 + x][64:128, 0:FE], sg[64:128, x, :], ALU.mult
                                      ).then_inc(sem("hh_ready"), 1)

                def rows_out(a, done, used):
                    dve.wait_ge(sem("down_done"), done)
                    if used is not None:
                        dve.wait_ge(sem("scat_done"), used)
                    dve.tensor_copy(ye[:, a, :], bank[7][:, :]).then_inc(sem("ye_ready"), 1)

                q0 = NE // 2 * layer
                for b in range(2):
                    q = q0 + b
                    scatter_mat(2 * b, q if q else None)
                    hidden(0, 2 * q + 1)
                    hidden(1, 2 * q + 2)
                    if b:
                        for a in range(2):
                            rows_out(a, 2 * q - 1 + a, 2 * q - 3 + a if q > 1 else None)
                with dve.Fori(1, NE // RING) as i:
                    for b in range(2):
                        scatter_mat(i * RING + 2 * b, i * 2 + (q0 + b))
                        hidden(0, i * 4 + (2 * (q0 + b) + 1))
                        hidden(1, i * 4 + (2 * (q0 + b) + 2))
                        for a in range(2):
                            rows_out(a, i * 4 + (2 * (q0 + b) - 1 + a), i * 4 + (2 * (q0 + b) - 3 + a))
                end = q0 + NE // 2
                for a in range(2):
                    rows_out(a, 2 * end - 1 + a, 2 * end - 3 + a)
                flag = dve.value_load(over_i[0:1, 0:1], min_val=0, max_val=1)
                with dve.If(flag > 0):
                    dve.wait_ge(sem("scat_done"), 2 * end)
                    for c in range(TT):
                        ins = dve.tensor_scalar(xh[:, c], h[:, c, :].rearrange("p (q k) -> p k q", k=KT),
                                                rstd[:, c:c + 1], None, ALU.mult)
                    ins.then_inc(sem(f"over_x{layer}"), 1)
                    dve.wait_ge(sem(f"over_gu{layer}"), 1)
                    for k in range(KT):
                        ins = dve.tensor_scalar(xT[:, k, :], bank[4 + k // 2][:, T * (k % 2):T * (k % 2) + T],
                                                gains[:, n, k:k + 1], None, ALU.mult)
                    ins.then_inc(sem(f"over_x{layer}"), 1)
                for a in range(2):
                    for c in range(TT):
                        add_h(2 * c + a, (sem("scat_done"), 2 * end - 1 + a), bank[2 * c + a], a)

                with dve.If(flag > 0):
                    done = sem(f"over_step{layer}")
                    dve.wait_ge(sem("h_tile"), 2 * (2 + 3 * layer))
                    dve.tensor_copy(over_col[:, 0:1], cw_over[:, 0, 0:1]).then_inc(sem(f"over_free{layer}"), 1)
                    dve.tensor_copy(over_col[:, 1:2], cw_over[:, 1, 0:1]).then_inc(sem(f"over_hid{layer}"), 1)
                    with dve.Fori(0, NE) as e:
                        dve.wait_ge(sem(f"over_free{layer}"), e + 1)
                        for f in range(2):
                            dve.wait_ge(sem(f"over_silu{layer}"), e * 2 + (f + 1))
                            dve.tensor_tensor(over_g[:, f, :], bank[5][:, 0:T], over_g[:, f, :], ALU.mult
                                              ).then_inc(sem(f"over_hid{layer}"), 1)
                        for c in range(TT):
                            dve.tensor_copy(over_col[:, c:c + 1], cw_over[:, c, bass.ds(e, 1)]).then_inc(done, 1)
                        dve.wait_ge(sem(f"over_down{layer}"), e + 1)
                        for j in range(4):
                            c, a = divmod(j, 2)
                            view = h[:, c, HALF * a:HALF * a + HALF]
                            dve.wait_ge(done, e * 5 + (j + 2))
                            ins = dve.scalar_tensor_tensor(out=view, in0=bank[j][:, :], scalar=over_col[:, c:c + 1],
                                                           in1=view, op0=ALU.mult, op1=ALU.add)
                            if j < 3:
                                ins.then_inc(done, 1)
                        ins.then_inc(sem(f"over_free{layer}"), 1)
                    dve.wait_ge(sem(f"over_free{layer}"), NE + 1)

                n = 2 + 3 * layer
                norm_sum(n)
                norm_gain(n, n)
                for j in range(4):
                    c, half = divmod(j, 2)
                    dve.wait_ge(sem("gate_ready"), 4 * layer + j + 1)
                    dve.wait_ge(sem("emb_out"), 4 * layer + 4)
                    link(dve.tensor_tensor(gate[:, j, :], emb[:, j, :], gate[:, j, :], ALU.mult))
                    view = h[:, c, HALF * half:HALF * half + HALF]
                    ins = dve.tensor_tensor(view, view, gate[:, j, :], ALU.add)
                    if half:
                        ins.then_inc(sem("h_tile"), 1)
                    else:
                        link(ins)
                    if j == 1:
                        norm_sum(n + 1)
            dve.wait_ge(sem("fin_gain_landed"), 16)
            for c in range(TT):
                dve.wait_ge(sem("norm_rstd"), 13 + c)
                for half in range(2):
                    cols = slice(HALF * half, HALF * half + HALF)
                    dve.scalar_tensor_tensor(out=fin_out[:, c, cols], in0=h[:, c, cols], scalar=rstd[:, c:c + 1],
                                             in1=fin_gain[:, cols], op0=ALU.mult, op1=ALU.mult
                                             ).then_inc(sem("fin_ready"), 1)


_INS = ["x", "p", "attn_norm", "moe_norm", "ple_norm", "gdn_w_in", "gdn_conv", "gdn_a_log", "gdn_dt_bias",
        "gdn_o_norm", "gdn_w_out", "kv_norm", "w_kv", "sb_w_q", "sb_w_out", "moe_w_group", "moe_b_group",
        "moe_w_expert", "moe_b_expert", "moe_w_gate", "moe_w_up", "moe_w_down", "ple_w_gate", "ple_w_proj",
        "final_norm"]
_OUTS = [((1, T, D), "float32")]


def kernel(**inputs):
    import numpy as _np
    import concourse.bacc as _bacc
    from concourse import mybir as _mybir
    from concourse.bass_utils import run_bass_kernel_spmd as _run

    nc = _bacc.Bacc("TRN2", target_bir_lowering=False, num_devices=1)
    arrays, args = {}, []
    for name in _INS:
        a = _np.ascontiguousarray(inputs[name])
        arrays[f"in_{name}_dram"] = a
        args.append(nc.dram_tensor(f"in_{name}_dram", a.shape, _mybir.dt.from_np(a.dtype), kind="ExternalInput").ap())
    for i, (shape, dtype) in enumerate(_OUTS):
        dt = _mybir.dt.from_np(_np.dtype(dtype))
        args.append(nc.dram_tensor(f"out_{i}_dram", shape, dt, kind="ExternalOutput").ap())
    yoco_kernel(nc, *args)
    r = _run(nc, [arrays], core_ids=[0])
    got = tuple(r.results[0][f"out_{i}_dram"] for i in range(len(_OUTS)))
    return got[0]
```
